# Optimizing a Trainium2 kernel written in Bass

```python
import math
import jax, jax.numpy as jnp
from jax import lax
import numpy as np

D_MODEL = 1024
BATCH = 1
SEQ = 512
DEPTH = 2
DEC_BATCH = 8
DEC_SEQ = 8
PAST_LEN = 1024
PAGE_SIZE = 128

N_A_LAYERS = DEPTH // 2
N_B_LAYERS = DEPTH - N_A_LAYERS
D_RNN = D_MODEL
N_LRU_BLOCKS = 8
LRU_BLOCK = D_RNN // N_LRU_BLOCKS
CONV_WIDTH = 4
LRU_C = 8.0
N_HEADS = 8
HEAD_DIM = D_MODEL // (2 * N_HEADS)
V_DIM = 2 * HEAD_DIM
D_FF = 2816
ROPE_THETA = 10000.0
Q_BLOCK = 128
NORM_EPS = 1e-6
N_ADA = 9

kernel_name = "yoco_hawk_diff_attn_macaron_adaln"

def rms_norm(x, g):
    xf = x.astype(jnp.float32)
    y = xf * lax.rsqrt(jnp.mean(xf * xf, axis=-1, keepdims=True) + NORM_EPS)
    return (y * g.astype(jnp.float32)).astype(x.dtype)

def modulate(x, g, shift, scale):
    return rms_norm(x, g) * (1 + scale[:, None, :]) + shift[:, None, :]

def rope(x, pos):
    half = HEAD_DIM // 2
    inv = 1.0 / (ROPE_THETA ** (jnp.arange(half, dtype=jnp.float32) * (2.0 / HEAD_DIM)))
    ang = pos.astype(jnp.float32)[:, None] * inv[None, :]
    cos = jnp.cos(ang)[None, :, None, None, :]
    sin = jnp.sin(ang)[None, :, None, None, :]
    xf = x.astype(jnp.float32)
    x1, x2 = xf[..., :half], xf[..., half:]
    return jnp.concatenate([x1 * cos - x2 * sin, x2 * cos + x1 * sin], axis=-1).astype(x.dtype)

def swiglu(h, w_gu, w_d):
    gu = h @ w_gu
    g, u = gu[..., :D_FF], gu[..., D_FF:]
    return (jax.nn.silu(g) * u) @ w_d

def rglru_mixer(h, conv0, h0, w_in, conv_w, conv_b, w_rg, b_rg, w_ig, b_ig, lru_lambda, w_out):
    B, S, _ = h.shape
    xy = h @ w_in
    xb, yb = xy[..., :D_RNN], jax.nn.gelu(xy[..., D_RNN:])
    xp = jnp.concatenate([conv0.astype(xb.dtype), xb], axis=1)
    xc = conv_b + conv_w[0] * xp[:, 0:S]
    for j in range(1, CONV_WIDTH):
        xc = xc + conv_w[j] * xp[:, j:j + S]
    new_conv = xp[:, -(CONV_WIDTH - 1):]
    xblk = xc.reshape(B, S, N_LRU_BLOCKS, LRU_BLOCK)
    r = jax.nn.sigmoid(jnp.einsum('bsnc,ncd->bsnd', xblk, w_rg).reshape(B, S, D_RNN) + b_rg)
    i = jax.nn.sigmoid(jnp.einsum('bsnc,ncd->bsnd', xblk, w_ig).reshape(B, S, D_RNN) + b_ig)
    log_a = (-LRU_C * r.astype(jnp.float32)) * jax.nn.softplus(-lru_lambda.astype(jnp.float32))
    a = jnp.exp(log_a)
    u = jnp.sqrt(-jnp.expm1(2.0 * log_a)) * (i * xc).astype(jnp.float32)

    def combine(left, right):
        a_l, b_l = left
        a_r, b_r = right
        return a_r * a_l, a_r * b_l + b_r

    a_cum, b_cum = lax.associative_scan(combine, (a, u), axis=1)
    hs = a_cum * h0.astype(jnp.float32)[:, None, :] + b_cum
    out = (hs.astype(h.dtype) * yb) @ w_out
    return out, new_conv, hs[:, -1]

def diff_attn_mixer(h, pos, k_all, v_all, k_pos, w_q, lam_p, subln_g, w_o, lam_init):
    B, S, _ = h.shape
    q = (h @ w_q).reshape(B, S, N_HEADS, 2, HEAD_DIM)
    q = rope(q, pos) * (HEAD_DIM ** -0.5)
    lp = lam_p.astype(jnp.float32)
    lam = jnp.exp(jnp.sum(lp[0] * lp[1])) - jnp.exp(jnp.sum(lp[2] * lp[3])) + lam_init

    def block(args):
        qb, qpb = args
        s = jnp.einsum('bqhmd,bkhmd->bhmqk', qb, k_all).astype(jnp.float32)
        s = jnp.where(k_pos[None, :] <= qpb[:, None], s, -jnp.inf)
        p = jax.nn.softmax(s, axis=-1)
        att = p[:, :, 0] - lam * p[:, :, 1]
        return jnp.einsum('bhqk,bkhe->bqhe', att.astype(v_all.dtype), v_all)

    if S > Q_BLOCK and S % Q_BLOCK == 0:
        nb = S // Q_BLOCK
        qb = jnp.moveaxis(q.reshape(B, nb, Q_BLOCK, N_HEADS, 2, HEAD_DIM), 1, 0)
        o = lax.map(block, (qb, pos.reshape(nb, Q_BLOCK)))
        o = jnp.moveaxis(o, 0, 1).reshape(B, S, N_HEADS, V_DIM)
    else:
        o = block((q, pos))
    o = rms_norm(o, subln_g) * (1.0 - lam_init)
    return o.reshape(B, S, N_HEADS * V_DIM) @ w_o

def run_trunk(x, c, past_k, past_v, conv0, h0, params):
    (ada_w, ada_b, norm_g, ffn_w_gu, ffn_w_d,
     a_w_in, a_conv_w, a_conv_b, a_w_rg, a_b_rg, a_w_ig, a_b_ig, a_lambda, a_w_out,
     kv_ada_w, kv_ada_b, kv_norm_g, w_kv,
     b_w_q, b_lambda, b_subln_g, b_w_o, final_g) = params
    B, S, _ = x.shape
    past_len = past_k.shape[1]
    pos = past_len + jnp.arange(S, dtype=jnp.int32)
    k_pos = jnp.arange(past_len + S, dtype=jnp.int32)
    c_act = jax.nn.silu(c)
    new_conv, new_h = [], []
    k_new = v_new = k_all = v_all = None
    for l in range(DEPTH):
        if l == N_A_LAYERS:
            kvm = c_act @ kv_ada_w + kv_ada_b
            hkv = modulate(x, kv_norm_g, kvm[:, :D_MODEL], kvm[:, D_MODEL:])
            kv = hkv @ w_kv
            k_new = rope(kv[..., :N_HEADS * 2 * HEAD_DIM].reshape(B, S, N_HEADS, 2, HEAD_DIM), pos)
            v_new = kv[..., N_HEADS * 2 * HEAD_DIM:].reshape(B, S, N_HEADS, V_DIM)
            k_all = jnp.concatenate([past_k.astype(k_new.dtype), k_new], axis=1)
            v_all = jnp.concatenate([past_v.astype(v_new.dtype), v_new], axis=1)
        mod = (c_act @ ada_w[l] + ada_b[l]).reshape(B, N_ADA, D_MODEL)
        hh = modulate(x, norm_g[l, 0], mod[:, 0], mod[:, 1])
        x = x + 0.5 * mod[:, 2, None] * swiglu(hh, ffn_w_gu[l, 0], ffn_w_d[l, 0])
        hh = modulate(x, norm_g[l, 1], mod[:, 3], mod[:, 4])
        if l < N_A_LAYERS:
            m, cs, hs = rglru_mixer(hh, conv0[l], h0[l], a_w_in[l], a_conv_w[l], a_conv_b[l],
                                    a_w_rg[l], a_b_rg[l], a_w_ig[l], a_b_ig[l], a_lambda[l], a_w_out[l])
            new_conv.append(cs)
            new_h.append(hs)
        else:
            j = l - N_A_LAYERS
            lam_init = 0.8 - 0.6 * math.exp(-0.3 * l)
            m = diff_attn_mixer(hh, pos, k_all, v_all, k_pos, b_w_q[j], b_lambda[j], b_subln_g[j],
                                b_w_o[j], lam_init)
        x = x + mod[:, 5, None] * m
        hh = modulate(x, norm_g[l, 2], mod[:, 6], mod[:, 7])
        x = x + 0.5 * mod[:, 8, None] * swiglu(hh, ffn_w_gu[l, 1], ffn_w_d[l, 1])
    y = rms_norm(x, final_g)
    return y, jnp.stack(new_conv, 0), jnp.stack(new_h, 0), k_new, v_new

def setup_inputs(seed: int = 0) -> dict:
    key = jax.random.key(seed)
    ks = iter(jax.random.split(key, 48))
    f32 = jnp.float32

    def nrm(shape, scale):
        return jax.random.normal(next(ks), shape, f32) * scale

    n_pages = PAST_LEN // PAGE_SIZE
    n_used = DEC_BATCH * n_pages
    n_phys = n_used + n_used // 4
    page_table = jax.random.permutation(next(ks), n_phys)[:n_used].reshape(DEC_BATCH, n_pages).astype(jnp.int32)

    u = jax.random.uniform(next(ks), (N_A_LAYERS, D_RNN), f32, minval=0.9, maxval=0.999)
    s = u ** (1.0 / LRU_C)
    a_lambda = jnp.log(s) - jnp.log1p(-s)

    return {
        "x_prompt": nrm((BATCH, SEQ, D_MODEL), 1.0),
        "x_sample": nrm((DEC_BATCH, DEC_SEQ, D_MODEL), 1.0),
        "c_prompt": nrm((BATCH, D_MODEL), 1.0),
        "c_sample": nrm((DEC_BATCH, D_MODEL), 1.0),
        "state_conv": nrm((N_A_LAYERS, DEC_BATCH, CONV_WIDTH - 1, D_RNN), 1.0),
        "state_h": nrm((N_A_LAYERS, DEC_BATCH, D_RNN), 0.5),
        "cache_k": nrm((n_phys, PAGE_SIZE, N_HEADS, 2, HEAD_DIM), 1.0),
        "cache_v": nrm((n_phys, PAGE_SIZE, N_HEADS, V_DIM), 1.0),
        "page_table": page_table,
        "ada_w": nrm((DEPTH, D_MODEL, N_ADA * D_MODEL), D_MODEL ** -0.5),
        "ada_b": nrm((DEPTH, N_ADA * D_MODEL), 0.01),
        "norm_g": 1.0 + nrm((DEPTH, 3, D_MODEL), 0.05),
        "ffn_w_gu": nrm((DEPTH, 2, D_MODEL, 2 * D_FF), D_MODEL ** -0.5),
        "ffn_w_d": nrm((DEPTH, 2, D_FF, D_MODEL), D_FF ** -0.5),
        "a_w_in": nrm((N_A_LAYERS, D_MODEL, 2 * D_RNN), D_MODEL ** -0.5),
        "a_conv_w": nrm((N_A_LAYERS, CONV_WIDTH, D_RNN), CONV_WIDTH ** -0.5),
        "a_conv_b": nrm((N_A_LAYERS, D_RNN), 0.01),
        "a_w_rg": nrm((N_A_LAYERS, N_LRU_BLOCKS, LRU_BLOCK, LRU_BLOCK), LRU_BLOCK ** -0.5),
        "a_b_rg": nrm((N_A_LAYERS, D_RNN), 0.01),
        "a_w_ig": nrm((N_A_LAYERS, N_LRU_BLOCKS, LRU_BLOCK, LRU_BLOCK), LRU_BLOCK ** -0.5),
        "a_b_ig": nrm((N_A_LAYERS, D_RNN), 0.01),
        "a_lambda": a_lambda,
        "a_w_out": nrm((N_A_LAYERS, D_RNN, D_MODEL), D_RNN ** -0.5),
        "kv_ada_w": nrm((D_MODEL, 2 * D_MODEL), D_MODEL ** -0.5),
        "kv_ada_b": nrm((2 * D_MODEL,), 0.01),
        "kv_norm_g": 1.0 + nrm((D_MODEL,), 0.05),
        "w_kv": nrm((D_MODEL, N_HEADS * 2 * HEAD_DIM + N_HEADS * V_DIM), D_MODEL ** -0.5),
        "b_w_q": nrm((N_B_LAYERS, D_MODEL, N_HEADS * 2 * HEAD_DIM), D_MODEL ** -0.5),
        "b_lambda": nrm((N_B_LAYERS, 4, HEAD_DIM), 0.1),
        "b_subln_g": 1.0 + nrm((N_B_LAYERS, V_DIM), 0.05),
        "b_w_o": nrm((N_B_LAYERS, N_HEADS * V_DIM, D_MODEL), (N_HEADS * V_DIM) ** -0.5),
        "final_g": 1.0 + nrm((D_MODEL,), 0.05),
    }

def reference(x_prompt, x_sample, c_prompt, c_sample, state_conv, state_h, cache_k, cache_v, page_table,
              ada_w, ada_b, norm_g, ffn_w_gu, ffn_w_d,
              a_w_in, a_conv_w, a_conv_b, a_w_rg, a_b_rg, a_w_ig, a_b_ig, a_lambda, a_w_out,
              kv_ada_w, kv_ada_b, kv_norm_g, w_kv,
              b_w_q, b_lambda, b_subln_g, b_w_o, final_g):
    params = (ada_w, ada_b, norm_g, ffn_w_gu, ffn_w_d,
              a_w_in, a_conv_w, a_conv_b, a_w_rg, a_b_rg, a_w_ig, a_b_ig, a_lambda, a_w_out,
              kv_ada_w, kv_ada_b, kv_norm_g, w_kv,
              b_w_q, b_lambda, b_subln_g, b_w_o, final_g)
    bp = x_prompt.shape[0]
    zk = jnp.zeros((bp, 0, N_HEADS, 2, HEAD_DIM), x_prompt.dtype)
    zv = jnp.zeros((bp, 0, N_HEADS, V_DIM), x_prompt.dtype)
    zc = jnp.zeros((N_A_LAYERS, bp, CONV_WIDTH - 1, D_RNN), x_prompt.dtype)
    zh = jnp.zeros((N_A_LAYERS, bp, D_RNN), jnp.float32)
    y_prompt, conv_prompt, h_prompt, k_prompt, v_prompt = run_trunk(x_prompt, c_prompt, zk, zv, zc, zh, params)
    bs = x_sample.shape[0]
    n_pages = page_table.shape[1]
    past_k = cache_k[page_table].reshape(bs, n_pages * PAGE_SIZE, N_HEADS, 2, HEAD_DIM)
    past_v = cache_v[page_table].reshape(bs, n_pages * PAGE_SIZE, N_HEADS, V_DIM)
    y_sample, conv_sample, h_sample, k_sample, v_sample = run_trunk(
        x_sample, c_sample, past_k, past_v, state_conv, state_h, params)
    return (y_prompt, y_sample, conv_prompt, h_prompt, k_prompt, v_prompt,
            conv_sample, h_sample, k_sample, v_sample)


_drawn_inputs = setup_inputs


def setup_inputs(seed=0):
    import zlib

    import numpy as np

    out = dict(_drawn_inputs(seed))
    spreads = {}
    factors = {'a_conv_b': 3.393,
     'a_b_rg': 37.628,
     'a_b_ig': 8.0,
     'kv_ada_b': 5.209,
     'b_lambda': 22.469,
     'b_subln_g': 3.617}
    for name, (base, spread) in spreads.items():
        noise = np.random.default_rng([zlib.crc32(name.encode()), seed]).standard_normal(out[name].shape)
        drawn = base * np.exp(spread * noise) if base else spread * noise
        out[name] = __import__('jax').numpy.asarray(drawn.astype(out[name].dtype))
    for name, factor in factors.items():
        out[name] = (out[name] * factor).astype(out[name].dtype)
    return out
```

```python
from contextlib import ExitStack
import math

import numpy as np
import concourse.bass as bass
from concourse import mybir

F32 = mybir.dt.float32
F32R = mybir.dt.float32r
I32 = mybir.dt.int32
ALU = mybir.AluOpType
ACT = mybir.ActivationFunctionType
AXX = mybir.AxisListType.X

P = 128
D_MODEL = 1024
SEQ = 512
DEC_BATCH = 8
DEC_SEQ = 8
PAST_LEN = 1024
PAGE = 128
N_HEADS = 8
HEAD_DIM = 64
D_FF = 2816
CONV_W = 4
N_ADA = 9
EPS = 1e-6
ROPE_THETA = 10000.0
LAM_INIT = 0.8 - 0.6 * math.exp(-0.3 * 1)
NEG = -1e30

KT = D_MODEL // P
FT = D_FF // P
S_TOK = DEC_BATCH * DEC_SEQ
T = SEQ + S_TOK
TH = T // 2
PB = SEQ - TH
NC_ = 1 + DEC_BATCH
N_PAGES = PAST_LEN // PAGE
PADS = CONV_W - 1
SEG = PADS + DEC_SEQ
TPAD = PADS + SEQ + DEC_BATCH * SEG
TC = TPAD - PADS
TCH = TC // 2
S0 = SEQ + PADS
UNIT = 8 * 256
CHUNKS = (8, 8, 6)
ADA_FIRST = 14
ADA_TILES = N_ADA * KT
KV_TILE0 = ADA_TILES
L1_TILE0 = ADA_TILES + 2 * KT
N_MOD_TILES = 2 * ADA_TILES + 2 * KT

CONST = {}
_at = 0
for _name, _n in (("ident", P), ("ones", P), ("cond", KT * NC_), ("ada_b", N_MOD_TILES), ("norm_g", 6 * KT),
                  ("kv_g", KT), ("final_g", KT), ("conv_w", KT * CONV_W), ("conv_b", KT), ("b_rg", KT), ("b_ig", KT),
                  ("lru_lambda", KT), ("subln_g", 1), ("lam_p", 4 * HEAD_DIM), ("st_conv", KT * DEC_BATCH * PADS),
                  ("st_h", KT * DEC_BATCH), ("cos", T), ("sin", T), ("causal", P), ("smask", DEC_BATCH * S_TOK),
                  ("comb", S_TOK), ("map0", 1), ("map1", 1)):
    CONST[_name] = (_at, _n)
    _at += _n
N_CONST = _at

RG = {n: i + 1 for i, n in enumerate(
    ("state_in", "conv_prompt_out", "conv_sample_out", "tap0", "tap1", "tap2", "tap3", "gelu_poly", "gelu_arg",
     "gated_x", "one_minus_a2", "u", "reset_a", "reset_u", "scan", "h_prompt", "h_sample",
     "z_prompt", "z_sample"))}
NRG = len(RG)
RA = {n: i + 1 for i, n in enumerate(("y2", "gelu_tanh", "tanh_r", "tanh_i", "tau", "a", "a2", "root"))}
NRA = len(RA)

CREDITS = {"k_out0": 16, "k_out1": 16, "v_out0": 16, "v_out1": 16, "w_done": 2, "w_lo": 2, "s0_free": 2,
           "s1_free": 2, "ada_done": 2, "ada_evac": 2, "sq_used": 2,
           "rstd_ready": 1, "norm_p": 2, "norm_s": 2, "norm_lo": 2, "res_tmp": 1, "h_lo": 2, "mod_ready": 1,
           "rg_dve": NRG, "rg_act": NRA, "gates_done": 2, "rope_done": 2, "v_turned": 1,
           "v_ready": 2, "p_ready": 2, "att_ready": 2, "tp_done": 2, "attT_ready": 2, "pv_done": 8, "o_evac": 2,
           "nmx_ready": 1, "kg_done": 2, "v_used": 4, "ss_full": 1, "sp_ready": 1, "c_ready": 1, "at_done": 1,
           "at_ready": 1, "pvs_done": 1, "os_evac": 1, "so_sum": 2, "so_rs": 2, "so_n": 2, "out_y0": 16, "out_y1": 16}


def trunk(nc, consts, xT, page_table, ada_w, w_gu, w_d8, w_d6, w_in, w_gate, w_out, w_kv, w_q, w_o, k_cache, v_cache,
          yT, conv_out, h_out, kT_out, v_prompt, v_sample):
    qT = nc.dram_tensor("qT", [N_HEADS, P, T], F32, kind="Internal").ap()

    plan = []
    count = {"u": 0, "ada": ADA_FIRST, "norm": 0, "h": 0, "res": 0, "rope": 0}

    def stage(kind, units=0, **more):
        plan.append({"kind": kind, "units": units, **count, **more})
        count["u"] += units

    def ffn(layer, which):
        tile0 = L1_TILE0 * layer
        chunk0 = 6 * which
        stage("norm", sh=tile0 + 8 * chunk0, sc=tile0 + 8 * chunk0 + 8, ga=tile0 + 8 * chunk0 + 16,
              g=CONST["norm_g"][0] + 8 * (3 * layer + 2 * which), half=0.5)
        count["norm"] += 1
        first = 0
        for c, tiles in enumerate(CHUNKS):
            has_ada = not (layer == 1 and which == 1)
            stage("up", tiles, src=w_gu[2 * layer + which], row=first, has_ada=has_ada)
            count["h"] += tiles
            count["ada"] += tiles if has_ada else 0
            first += tiles
            src = w_d8[2 * layer + which, c] if tiles == 8 else w_d6[2 * layer + which]
            stage("down", 4, src=src, row=0, k=tiles, last=(layer == 1 and which == 1 and c == 2))
            count["res"] += 8

    def mixer_norm(tile0, g, gate):
        stage("norm", sh=tile0, sc=tile0 + 8, ga=tile0 + 16 if gate else None, g=g, half=1.0)
        count["norm"] += 1

    ffn(0, 0)
    mixer_norm(24, CONST["norm_g"][0] + 8, True)
    stage("rglru", 8, src=w_in, row=0)
    count["h"] += 8
    stage("down", 4, src=w_out, row=0, k=8, last=False)
    count["res"] += 8
    ffn(0, 1)
    mixer_norm(KV_TILE0, CONST["kv_g"][0], False)
    stage("kv", 8, src=w_kv, row=0)
    count["rope"] += 8
    ffn(1, 0)
    mixer_norm(L1_TILE0 + 24, CONST["norm_g"][0] + 8 * 4, True)
    stage("q", 4, src=w_q, row=0)
    count["rope"] += 8
    stage("attention")
    count["h"] += 8
    stage("down", 4, src=w_o, row=0, k=8, last=False, loaded=2)
    count["res"] += 8
    ffn(1, 1)
    stage("final")
    n_units = count["u"]
    assert count["ada"] * 2 == N_MOD_TILES

    with ExitStack() as ctx:
        def sb(name, shape, dt=F32, where=None):
            return (where or ctx).enter_context(nc.sbuf_tensor(name, shape, dt))

        cst = sb("cst", [P, N_CONST])
        x = sb("x", [P, KT, T])
        raw = [sb(f"raw{j}", [P, UNIT]) for j in range(2)]
        w_hi = [sb(f"w_hi{j}", [P, 8, 256], F32R) for j in range(2)]
        w_lo = [sb(f"w_lo{j}", [P, 8, 256], F32R) for j in range(2)]
        mods = sb("mods", [P, N_MOD_TILES, NC_])
        act_c = sb("act_c", [P, KT, NC_])
        mod_a = sb("mod_a", [P, KT, NC_])
        mod_g = sb("mod_g", [P, KT, NC_])
        sg = [sb(f"sg{j}", [P, T]) for j in range(2)]
        hf = [sb(f"hf{j}", [P, T]) for j in range(2)]
        nt = [sb(f"nt{j}", [P, T]) for j in range(2)]
        rstd = sb("rstd", [P, T])
        small = sb("small", [P, 256])
        s_tmp = small[:, 0:S_TOK]
        r_tmp = small[:, S_TOK:2 * S_TOK]
        rg_c4 = small[:, 128:136]
        rg_nc4 = small[:, 136:144]
        rg_brh = small[:, 144:152]
        rg_bih = small[:, 152:160]
        neg_lam = small[:, 160:161]
        map_gain = small[:, 241:243]
        eps_x = small[:, 240:241]
        eps_o = small[:, 243:244]
        row_sign = small[:, 161:162]
        gain_o = small[:, 162:163]
        mx = small[:, 164:166]
        nmx = small[:, 166:168]
        sums = [small[:, 168:170], small[:, 170:172]]
        rsum = small[:, 172:174]
        mxs = small[:, 174:175]
        nmxs = small[:, 175:176]
        sumss = small[:, 176:177]
        rss = small[:, 177:178]
        coef = small[:, 178:179]
        setup = [small[:, 180 + 8 * i:188 + 8 * i] for i in range(6)]
        lam4 = small[:, 228:232]
        pt_sb = sb("pt_sb", [1, DEC_BATCH * N_PAGES], I32)
        conv_sb = sb("conv_sb", [P, KT, NC_, PADS])
        h_sb = sb("h_sb", [P, KT, NC_])

        region = {}

        def laid(key, below, *tensors):
            with ExitStack() as part:
                if below:
                    sb("below_" + key, [P, below], F32, part)
                for name, shape, dt in tensors:
                    region[name] = sb(name, shape, dt, part)

        hh = KT * T
        laid("linear", 0, ("hh_hi", [P, KT, T], F32R), ("hh_lo", [P, KT, T], F32R),
             ("h_hi", [P, KT, T], F32R), ("h_lo", [P, KT, T], F32R),
             ("ada0", [P, UNIT], F32), ("ada1", [P, UNIT], F32))
        laid("rglru", 4 * hh, *[(n, [P, TPAD if n == "xp" else TC], F32) for n in
                                ("xp", "xc", "th_r", "th_i", "tau", "a", "a2", "hs", "gv", "gt", "gy")],
             ("gw0", [P, 256], F32), ("gw1", [P, 256], F32))
        laid("rope", 4 * hh + 2 * UNIT, ("swapped", [P, T], F32), ("rope_a", [P, T], F32),
             ("rope_b", [P, T], F32))
        laid("rope_out", 2 * hh, ("rk0", [P, T], F32), ("rk1", [P, T], F32), ("vraw", [P, T], F32),
             ("vt0", [P, SEQ], F32), ("vt1", [P, SEQ], F32), ("vts0", [S_TOK, P], F32), ("vts1", [S_TOK, P], F32))
        laid("attention", 0, ("kr0", [P, 4, N_HEADS, PAGE], F32), ("kr1", [P, 4, N_HEADS, PAGE], F32),
             *[(f"vr{i}", [P, N_HEADS * P], F32) for i in range(4)],
             ("qs", [P, N_HEADS, S_TOK], F32), ("ks", [P, N_HEADS, S_TOK], F32),
             ("vs", [S_TOK, N_HEADS, P], F32))
        att0 = 8192 + 4096 + 2 * N_HEADS * S_TOK + N_HEADS * P
        laid("att_prompt", att0, ("qh0", [P, SEQ], F32), ("qh1", [P, SEQ], F32), ("kh0", [P, SEQ], F32),
             ("kh1", [P, SEQ], F32), ("vh0", [P, 4, P], F32), ("vh1", [P, 4, P], F32), ("pp0", [P, 2, SEQ], F32),
             ("pp1", [P, 2, SEQ], F32), ("att", [P, SEQ], F32), ("attT", [P, SEQ], F32),
             ("oT", [P, N_HEADS, T], F32))
        laid("att_sample", att0, ("qbd", [P, N_HEADS * 144], F32), ("sp", [P, PAST_LEN + S_TOK], F32),
             ("cmat", [P, S_TOK], F32), ("aT", [P, (N_PAGES + 1) * S_TOK], F32))
        R = region
        hh_hi, hh_lo, h_hi, h_lo = R["hh_hi"], R["hh_lo"], R["h_hi"], R["h_lo"]
        ada = [R["ada0"], R["ada1"]]
        xp, xc, th_r, th_i = R["xp"], R["xc"], R["th_r"], R["th_i"]
        tau, dec, dec2, hs, gv, gt, gy = R["tau"], R["a"], R["a2"], R["hs"], R["gv"], R["gt"], R["gy"]
        gw = [R["gw0"], R["gw1"]]
        swapped, rope_a, rope_b = R["swapped"], R["rope_a"], R["rope_b"]
        rk, vraw, vt, vts = [R["rk0"], R["rk1"]], R["vraw"], [R["vt0"], R["vt1"]], [R["vts0"], R["vts1"]]
        kr, vr = [R["kr0"], R["kr1"]], [R[f"vr{i}"] for i in range(4)]
        oT, qs, ks, vs = R["oT"], R["qs"], R["ks"], R["vs"]
        qh, kh, vh = [R["qh0"], R["qh1"]], [R["kh0"], R["kh1"]], [R["vh0"], R["vh1"]]
        pp, att, attT = [R["pp0"], R["pp1"]], R["att"], R["attT"]
        qbd, sp, cmat, aT = R["qbd"], R["sp"], R["cmat"], R["aT"]

        ps = ctx.enter_context(nc.psum_tensor("ps", [P, 8, 512], F32))

        def slot(s):
            return ps[:, 2 * s:2 * s + 2, 0:TH]

        def halves(tile):
            return tile.rearrange("p (a b) -> p a b", a=2)

        def c(name, a=0, b=None):
            at, n = CONST[name]
            return cst[:, at + a:at + (n if b is None else b)]

        def by_seq(ap):
            return ap.rearrange("p (b s) -> p b s", b=DEC_BATCH)

        def seq_cols(tile, first, n, seg=SEG):
            base = tile[:, first:first + (DEC_BATCH - 1) * seg + n]
            return bass.AP(base.tensor, base.offset, [list(base.ap[0]), [seg, DEC_BATCH], [1, n]])

        ident, ones = c("ident"), c("ones")

        sems = {}

        def sem(name):
            if name not in sems:
                sems[name] = ctx.enter_context(nc.semaphore("s_" + name))
            return sems[name]

        for name in ("cst_in", "x_in", "pt_in", "cond_ready", "setup_done", "setup_exp", "setup_step", "raw_full0",
                     "raw_full1", "w_hi", "out0_full", "ada_full0", "ada_full1", "sq_full", "ln_ready", "norm_t",
                     "norm_tmp", "norm_hi", "h_hi", "gw_full0", "gw_full1", "rope_swap", "rope_t2",
                     "ph_full0", "ph_full1", "sc_full", "masked", "max_ready",
                     "coef_ready", "att_part", "s_small", "k_full0", "k_full1", *[f"v_full{i}" for i in range(4)],
                     "qbd_zero", "qbd_ready", "smasked", "smax", "snmx", "srs", "so_sq", "so_ln", "state_out",
                     "rg_pad", *CREDITS):
            sem(name)

        def count(name, n):
            return n + CREDITS.get(name, 0)

        def credit(eng, *names):
            for name in names:
                eng.sem_inc(sems[name], CREDITS[name])

        block = ctx.enter_context(nc.Block())

        @block.sync
        def _(sp):
            credit(sp, "k_out0", "k_out1", "v_out0", "v_out1", "out_y0", "out_y1")
            sp.dma_start(cst[:, :], consts).then_inc(sems["cst_in"], 16)

            def ada_load(a, j):
                sp.wait_ge(sems["ada_done"], a - 1 + CREDITS["ada_done"])
                sp.dma_start(ada[j][:, :], ada_w[a]).then_inc(sems[f"ada_full{j}"], 16)

            def unit_load(src, row, u, j):
                sp.wait_ge(sems["w_lo"], u - 1 + CREDITS["w_lo"])
                sp.dma_start(raw[j][:, 0:src.shape[-1]], src[row]).then_inc(sems[f"raw_full{j}"], 16)

            for j in range(2):
                ada_load(j, j)
            sp.dma_start(x[:, :, :], xT).then_inc(sems["x_in"], 16)
            sp.dma_start(pt_sb[:, :], page_table).then_inc(sems["pt_in"], 16)
            with sp.Fori(1, ADA_FIRST // 2) as i:
                for j in range(2):
                    ada_load(2 * i + j, j)

            for s in plan:
                u0, a0 = s["u"], s["ada"]
                if s["kind"] == "up" and s["has_ada"] and s["row"] == 0 and u0 > 0:
                    sp.wait_ge(sems["rg_dve"], NRG * KT + CREDITS["rg_dve"])
                if s["units"]:
                    with sp.Fori(s.get("loaded", 0) // 2, s["units"] // 2) as i:
                        for j in range(2):
                            unit_load(s["src"], s["row"] + 2 * i + j, u0 + 2 * i + j, j)
                            if s["kind"] == "up" and s["has_ada"]:
                                ada_load(a0 + 2 * i + j, j)
                            if s["kind"] == "rglru":
                                sp.wait_ge(sems["gates_done"], 2 * i + j - 1 + CREDITS["gates_done"])
                                sp.dma_start(gw[j][:, :], w_gate[2 * i + j]).then_inc(sems[f"gw_full{j}"], 16)
                if s["kind"] == "attention":
                    for j in range(2):
                        unit_load(w_o, j, u0 + j, j)
                    for j in range(2):
                        sp.wait_ge(sems[f"k_out{j}"], 16 * 8 + CREDITS[f"k_out{j}"])
                        sp.wait_ge(sems[f"v_out{j}"], 16 * 8 + CREDITS[f"v_out{j}"])
                    sp.wait_ge(sems["w_done"], u0 + CREDITS["w_done"])
                    sp.dma_start(qs[:, :, :], qT[:, :, SEQ:T].rearrange("h p s -> p h s")).then_inc(sems["s_small"], 16)
                    sp.dma_start(ks[:, :, :], kT_out[:, :, SEQ:T].rearrange("h p s -> p h s"))\
                        .then_inc(sems["s_small"], 16)
                    sp.dma_start(vs[:, :, :], v_sample.rearrange("h s e -> s h e")).then_inc(sems["s_small"], 16)

                    def head_load(h, j):
                        sp.wait_ge(sems["pv_done"], 4 * (h - 1) + CREDITS["pv_done"])
                        f = sems[f"ph_full{j}"]
                        sp.dma_start(qh[j][:, :], qT[h, :, 0:SEQ]).then_inc(f, 16)
                        sp.dma_start(kh[j][:, :], kT_out[h, :, 0:SEQ]).then_inc(f, 16)
                        sp.dma_start(vh[j][:, :, :], v_prompt[h]).then_inc(f, 16)

                    def k_load(b):
                        for g in range(2):
                            sp.wait_ge(sems["kg_done"], 2 * (b - 1) + g + 1 + CREDITS["kg_done"])
                            for p in range(4):
                                page = sp.value_load(pt_sb[0:1, bass.ds(b * N_PAGES + 4 * g + p, 1)], min_val=0,
                                                     max_val=k_cache.shape[0] - 1)
                                sp.dma_start(kr[g][:, p, :, :], k_cache[bass.ds(page, 1)].rearrange(
                                    "o p (h n) -> p (o h) n", h=N_HEADS)).then_inc(sems[f"k_full{g}"], 16)

                    def v_load(b):
                        for p in range(N_PAGES):
                            sp.wait_ge(sems["v_used"], N_PAGES * b + p - 3 + CREDITS["v_used"])
                            page = sp.value_load(pt_sb[0:1, bass.ds(b * N_PAGES + p, 1)], min_val=0,
                                                 max_val=v_cache.shape[0] - 1)
                            sp.dma_start(vr[p % 4][:, :], v_cache[bass.ds(page, 1)].rearrange(
                                "o p n -> p (o n)")).then_inc(sems[f"v_full{p % 4}"], 16)

                    sp.wait_ge(sems["pt_in"], 16)
                    for j in range(2):
                        head_load(j, j)
                    k_load(0)
                    with sp.Fori(1, 4) as i:
                        for j in range(2):
                            head_load(2 * i + j, j)
                    with sp.Fori(1, DEC_BATCH) as b:
                        k_load(b)
                        v_load(b - 1)
                    v_load(DEC_BATCH - 1)
                if s["kind"] == "final":
                    n0 = 8 * s["norm"]
                    with sp.Fori(0, 4) as i:
                        for j in range(2):
                            sp.wait_ge(sems["norm_p"], n0 + 2 * i + j + 1 + CREDITS["norm_p"])
                            sp.dma_start(yT[2 * i + j], hf[j][:, :]).then_inc(sems[f"out_y{j}"], 16)
                    sp.wait_ge(sems["rg_dve"], NRG * 8 + CREDITS["rg_dve"])
                    sp.dma_start(conv_out, conv_sb[:, :, :, :]).then_inc(sems["state_out"], 16)
                    sp.dma_start(h_out, h_sb[:, :, :]).then_inc(sems["state_out"], 16)
                    sp.wait_ge(sems["state_out"], 32)
                    for j in range(2):
                        sp.wait_ge(sems[f"out_y{j}"], 16 * 4 + CREDITS[f"out_y{j}"])

        @block.tensor
        def _(pe):
            credit(pe, "w_done", "ada_done", "sq_used", "gates_done", "v_turned", "tp_done", "pv_done", "kg_done",
                   "v_used", "ss_full", "at_done", "pvs_done", "so_sum")

            def ada_unit(a, j, turn):
                pe.wait_ge(sems[f"ada_full{j}"], 16 * (turn + 1))
                pe.wait_ge(sems["ada_evac"], a - 1 + CREDITS["ada_evac"])
                for t in range(2):
                    for k in range(KT):
                        mm = pe.matmul(ps[:, 4 + j, NC_ * t:NC_ * t + NC_],
                                       ada[j][:, 256 * k + P * t:256 * k + P * t + P], act_c[:, k, :],
                                       start=(k == 0), stop=(k == KT - 1))
                mm.then_inc(sems["ada_done"], 1)

            def tile_products(j, half_tile, rhs_hi, rhs_lo, s, k_tiles, ready, first, done):
                for k in range(k_tiles):
                    if ready:
                        pe.wait_ge(sems[ready], first + k + 1 + CREDITS[ready])
                    whi = w_hi[j][:, k, P * half_tile:P * half_tile + P]
                    wlo = w_lo[j][:, k, P * half_tile:P * half_tile + P]
                    for n in range(2):
                        for r in (rhs_hi, rhs_lo):
                            pe.matmul(ps[:, 2 * s + n, 0:TH], whi, r[:, k, TH * n:TH * n + TH],
                                      start=(k == 0 and r is rhs_hi), stop=False)
                    for n in range(2):
                        mm = pe.matmul(ps[:, 2 * s + n, 0:TH], wlo, rhs_hi[:, k, TH * n:TH * n + TH],
                                       start=False, stop=(k == k_tiles - 1))
                mm.then_inc(sems[done], 1)

            def unit(u, j, rhs_hi, rhs_lo, k_tiles, ready, first):
                pe.wait_ge(sems["w_lo"], u + 1 + CREDITS["w_lo"])
                pe.wait_ge(sems["s0_free"], u + CREDITS["s0_free"])
                tile_products(j, 0, rhs_hi, rhs_lo, 0, k_tiles, ready if j == 0 else None, first, "out0_full")
                pe.wait_ge(sems["s1_free"], u + CREDITS["s1_free"])
                tile_products(j, 1, rhs_hi, rhs_lo, 1, k_tiles, None, 0, "w_done")

            pe.wait_ge(sems["cst_in"], 16)
            pe.wait_ge(sems["cond_ready"], 1)
            with pe.Fori(0, ADA_FIRST // 2) as i:
                for j in range(2):
                    ada_unit(2 * i + j, j, i)

            for s in plan:
                u0, a0, n0 = s["u"], s["ada"], 8 * s["norm"]
                if s["kind"] in ("norm", "final"):
                    pe.wait_ge(sems["rstd_ready"], s["norm"] + CREDITS["rstd_ready"])
                    for k in range(KT):
                        pe.wait_ge(sems["sq_full"], n0 + k + 1)
                        for n in range(2):
                            mm = pe.matmul(ps[:, 6 + n, 0:TH], ones, sg[k % 2][:, TH * n:TH * n + TH],
                                           start=(k == 0), stop=(k == KT - 1))
                        mm.then_inc(sems["sq_used"], 1)
                if s["kind"] in ("up", "rglru", "kv", "q"):
                    with pe.Fori(0, s["units"] // 2) as i:
                        for j in range(2):
                            u = u0 + 2 * i + j
                            unit(u, j, hh_hi, hh_lo, KT, "norm_lo", n0 - 8)
                            if s["kind"] == "up" and s["has_ada"]:
                                ada_unit(a0 + 2 * i + j, j, a0 // 2 + i)
                            if s["kind"] == "rglru":
                                n = 2 * i + j
                                pe.wait_ge(sems[f"gw_full{j}"], 16 * i + 16)
                                pe.wait_ge(sems["rg_dve"], NRG * n + RG["tap3"] + CREDITS["rg_dve"])
                                pe.wait_ge(sems["rg_act"], NRA * (n - 1) + RA["tanh_i"] + CREDITS["rg_act"])
                                for g in range(2):
                                    for q in range(2):
                                        mm = pe.matmul(ps[:, 4 + 2 * g + q, 0:TCH], gw[j][:, P * g:P * g + P],
                                                       xc[:, TCH * q:TCH * q + TCH], start=True, stop=True)
                                mm.then_inc(sems["gates_done"], 1)
                            if s["kind"] == "kv":
                                pe.wait_ge(sems["s1_free"], u + 1 + CREDITS["s1_free"])
                                pe.wait_ge(sems["v_ready"], 2 * i + j + CREDITS["v_ready"])
                                for b in range(4):
                                    pe.transpose(ps[:, 4, P * b:P * b + P], vraw[:, P * b:P * b + P], ident)
                                pe.transpose(ps[0:S_TOK, 5, 0:P], vraw[:, SEQ:T], ident)\
                                    .then_inc(sems["v_turned"], 1)
                if s["kind"] == "down":
                    h_all = s["h"]
                    with pe.Fori(0, s["units"] // 2) as i:
                        for j in range(2):
                            kt = s["k"]
                            unit(u0 + 2 * i + j, j, h_hi, h_lo, kt, "h_lo", h_all - kt)
                if s["kind"] == "attention":
                    def scores(h, i, j, t):
                        n = P * (i + 1)
                        pe.wait_ge(sems["p_ready"], t - 1 + CREDITS["p_ready"])
                        for m in range(2):
                            rows = slice(64 * m, 64 * m + 64)
                            mm = pe.matmul(ps[:, 2 * (i % 2) + m, 0:n], qh[j][rows, P * i:P * i + P],
                                           kh[j][rows, 0:n], start=True, stop=True)
                        mm.then_inc(sems["sc_full"], 1)

                    def weigh(h, i, j, t):
                        pe.wait_ge(sems["att_ready"], t + 1 + CREDITS["att_ready"])
                        pe.wait_ge(sems["attT_ready"], t - 1 + CREDITS["attT_ready"])
                        for b in range(i + 1):
                            mm = pe.transpose(ps[:, 4 + i % 2, P * b:P * b + P], att[:, P * b:P * b + P], ident)
                        mm.then_inc(sems["tp_done"], 1)
                        pe.wait_ge(sems["attT_ready"], t + 1 + CREDITS["attT_ready"])
                        if i == 0:
                            pe.wait_ge(sems["o_evac"], h - 1 + CREDITS["o_evac"])
                        for b in range(i + 1):
                            mm = pe.matmul(ps[:, 6 + j, P * i:P * i + P], vh[j][:, b, :], attT[:, P * b:P * b + P],
                                           start=(b == 0), stop=(b == i))
                        mm.then_inc(sems["pv_done"], 1)

                    pe.wait_ge(sems["w_done"], u0 + CREDITS["w_done"])
                    with pe.Fori(0, 4) as hp:
                        steps = [(2 * hp + j, i, j, 8 * hp + 4 * j + i) for j in range(2) for i in range(4)]
                        for n, st in enumerate(steps):
                            if st[1] == 0:
                                pe.wait_ge(sems[f"ph_full{st[2]}"], 48 * hp + 48)
                            scores(*st)
                            if n:
                                weigh(*steps[n - 1])
                        weigh(*steps[-1])

                    def sample_scores(b):
                        pe.wait_ge(sems["qbd_ready"], 2 * b + 2)
                        pe.wait_ge(sems["sp_ready"], b + CREDITS["sp_ready"])
                        for g in range(2):
                            pe.wait_ge(sems[f"k_full{g}"], 64 * b + 64)
                            for h in range(N_HEADS):
                                mm = pe.matmul(ps[:, g, :].rearrange("p (n k) -> p n k", k=PAGE),
                                               qbd[:, P * h:P * h + P], kr[g][:, :, h, :],
                                               start=(h == 0), stop=(h == N_HEADS - 1))
                            mm.then_inc(sems["kg_done"], 1)
                        for h in range(N_HEADS):
                            mm = pe.matmul(ps[:, 2, 0:S_TOK], qbd[:, P * h:P * h + P], ks[:, h, :],
                                           start=(h == 0), stop=(h == N_HEADS - 1))
                        mm.then_inc(sems["ss_full"], 1)

                    def sample_weigh(b):
                        pe.wait_ge(sems["c_ready"], b + 1 + CREDITS["c_ready"])
                        pe.wait_ge(sems["at_ready"], b + CREDITS["at_ready"])
                        for p in range(N_PAGES):
                            pe.matmul(ps[:, 3, S_TOK * p:S_TOK * p + S_TOK], R["sp"][:, PAGE * p:PAGE * p + PAGE],
                                      cmat[:, :], start=True, stop=True)
                        pe.matmul(ps[0:S_TOK, 4, 0:S_TOK], R["sp"][:, PAST_LEN:PAST_LEN + S_TOK], cmat[:, :],
                                  start=True, stop=True).then_inc(sems["at_done"], 1)
                        pe.wait_ge(sems["at_ready"], b + 1 + CREDITS["at_ready"])
                        pe.wait_ge(sems["os_evac"], b + CREDITS["os_evac"])
                        for p in range(N_PAGES):
                            pe.wait_ge(sems[f"v_full{p % 4}"], 32 * b + 16 * (p // 4) + 16)
                            for h in range(N_HEADS):
                                mm = pe.matmul(ps[:, 5, 8 * h:8 * h + 8], vr[p % 4][:, P * h:P * h + P],
                                               aT[:, S_TOK * p + 8 * h:S_TOK * p + 8 * h + 8],
                                               start=(p == 0 and h == 0), stop=False, skip_group_check=True)
                            mm.then_inc(sems["v_used"], 1)
                        for h in range(N_HEADS):
                            mm = pe.matmul(ps[:, 5, 8 * h:8 * h + 8], vs[:, h, :],
                                           aT[0:S_TOK, PAST_LEN // 2 + 8 * h:PAST_LEN // 2 + 8 * h + 8],
                                           start=False, stop=(h == N_HEADS - 1), skip_group_check=True)
                        mm.then_inc(sems["pvs_done"], 1)

                    pe.wait_ge(sems["s_small"], 48)
                    sample_scores(0)
                    with pe.Fori(0, DEC_BATCH - 1) as b:
                        sample_scores(b + 1)
                        sample_weigh(b)
                    sample_weigh(DEC_BATCH - 1)
                    with pe.Fori(0, 4) as i:
                        for j in range(2):
                            h = 2 * i + j
                            pe.wait_ge(sems["so_sq"], h + 1)
                            pe.wait_ge(sems["so_rs"], h - 1 + CREDITS["so_rs"])
                            for n in range(2):
                                mm = pe.matmul(ps[:, 2 * j + n, 0:TH], ones, sg[j][:, TH * n:TH * n + TH],
                                               start=True, stop=True)
                            mm.then_inc(sems["so_sum"], 1)

        @block.scalar
        def _(act):
            credit(act, "rstd_ready", "norm_p", "rg_act", "p_ready", "attT_ready", "sp_ready", "at_ready", "so_rs")

            def split_unit(u, j):
                act.wait_ge(sems[f"raw_full{j}"], 16 * (u[0] + 1))
                act.wait_ge(sems["w_done"], u[1] - 1 + CREDITS["w_done"])
                act.activation(w_hi[j][:, :, :].rearrange("p k n -> p (k n)"), raw[j][:, :], ACT.Copy)\
                   .then_inc(sems["w_hi"], 1)

            def look_ahead(u0, i, j):
                split_unit((u0 // 2 + i + j, u0 + 2 * i + j + 1), 1 - j)

            act.wait_ge(sems["cst_in"], 16)
            act.activation(act_c[:, :, :].rearrange("p k n -> p (k n)"), c("cond"), ACT.Silu)\
               .then_inc(sems["cond_ready"], 1)
            act.wait_ge(sems["setup_step"], 5)
            act.activation(setup[0], setup[1], ACT.Exp).then_inc(sems["setup_exp"], 1)
            act.activation(lam4[:, 2:4], lam4[:, 0:2], ACT.Exp).then_inc(sems["setup_exp"], 1)
            split_unit((0, 0), 0)

            def statistics(s):
                n0 = 8 * s["norm"]
                act.wait_ge(sems["x_in"], 16)
                act.wait_ge(sems["s0_free"], s["u"] + CREDITS["s0_free"])
                act.wait_ge(sems["s1_free"], s["u"] + CREDITS["s1_free"])
                act.wait_ge(sems["h_lo"], s["h"] + CREDITS["h_lo"])
                with act.Fori(0, 4) as i:
                    for j in range(2):
                        k = 2 * i + j
                        act.wait_ge(sems["sq_used"], n0 + k - 1 + CREDITS["sq_used"])
                        act.activation(sg[j][:, :], x[:, k, :], ACT.Square).then_inc(sems["sq_full"], 1)
                act.wait_ge(sems["sq_used"], n0 + 8 + CREDITS["sq_used"])
                act.activation(halves(rstd[:, :]), ps[:, 6:8, 0:TH], ACT.Ln, scale=1.0 / D_MODEL,
                               bias=eps_x).then_inc(sems["ln_ready"], 1)
                act.wait_ge(sems["ln_ready"], s["norm"] + 1)
                act.activation(rstd[:, :], rstd[:, :], ACT.Exp, scale=-0.5).then_inc(sems["rstd_ready"], 1)

            act.wait_ge(sems["setup_done"], 1)
            for s in plan:
                u0, h0 = s["u"], s["h"]
                n0 = 8 * s["norm"]
                if s["kind"] == "norm":
                    statistics(s)
                    act.wait_ge(sems["mod_ready"], s["norm"] + 1 + CREDITS["mod_ready"])
                    with act.Fori(0, 4) as i:
                        for j in range(2):
                            k = 2 * i + j
                            act.wait_ge(sems["norm_t"], n0 + k + 1)
                            act.wait_ge(sems["norm_lo"], n0 + k - 1 + CREDITS["norm_lo"])
                            act.activation(hf[j][:, 0:SEQ], nt[j][:, 0:SEQ], ACT.Identity, scale=mod_a[:, k, 0:1],
                                           bias=mods[:, s["sh"] + k, 0:1]).then_inc(sems["norm_p"], 1)
                            act.wait_ge(sems["norm_p"], n0 + k + 1 + CREDITS["norm_p"])
                            act.wait_ge(sems["norm_s"], n0 + k + 1 + CREDITS["norm_s"])
                            act.activation(hh_hi[:, k, :], hf[j][:, :], ACT.Copy).then_inc(sems["norm_hi"], 1)
                if s["kind"] == "up":
                    if s["rope"] == 8 and s["row"] == 0:
                        for j in range(2):
                            act.wait_ge(sems[f"k_out{j}"], 16 * 4 + CREDITS[f"k_out{j}"])
                            act.wait_ge(sems[f"v_out{j}"], 32 * 4 + CREDITS[f"v_out{j}"])
                    with act.Fori(0, s["units"] // 2) as i:
                        for j in range(2):
                            u, h = u0 + 2 * i + j, h0 + 2 * i + j
                            look_ahead(u0, i, j)
                            act.wait_ge(sems["out0_full"], u + 1)
                            act.wait_ge(sems["s1_free"], u - 1 + CREDITS["s1_free"])
                            act.activation(halves(sg[j][:, :]), slot(0), ACT.Silu).then_inc(sems["s0_free"], 1)
                            act.wait_ge(sems["s1_free"], u + 1 + CREDITS["s1_free"])
                            act.activation(h_hi[:, 2 * i + j, :], hf[j][:, :], ACT.Copy).then_inc(sems["h_hi"], 1)
                if s["kind"] == "down":
                    n_pairs = s["units"] // 2
                    if s["last"]:
                        for n in range(s["units"] - 1):
                            look_ahead(u0, n // 2, n % 2)
                    else:
                        with act.Fori(0, n_pairs) as i:
                            for j in range(2):
                                look_ahead(u0, i, j)
                if s["kind"] == "rglru":
                    with act.Fori(0, 4) as i:
                        for j in range(2):
                            u, n = u0 + 2 * i + j, 2 * i + j
                            ra, rg = NRA * n, NRG * n

                            look_ahead(u0, i, j)
                            act.wait_ge(sems["out0_full"], u + 1)
                            act.wait_ge(sems["rg_dve"], NRG * (n - 1) + RG["tap3"] + CREDITS["rg_dve"])
                            act.activation(xp[:, PADS:PADS + TH], ps[:, 0, 0:TH], ACT.Copy)
                            act.activation(xp[:, PADS + TH:S0], ps[:, 1, 0:PB], ACT.Copy)
                            act.activation(seq_cols(xp, S0 + PADS, DEC_SEQ), by_seq(ps[:, 1, PB:TH]), ACT.Copy)\
                               .then_inc(sems["s0_free"], 1)
                            act.wait_ge(sems["w_done"], u + 1 + CREDITS["w_done"])
                            act.wait_ge(sems["s1_free"], u + CREDITS["s1_free"])
                            act.activation(halves(gv[:, 0:T]), slot(1), ACT.Square).then_inc(sems["rg_act"], 1)
                            act.wait_ge(sems["rg_dve"], rg + RG["gelu_arg"] + CREDITS["rg_dve"])
                            act.activation(gt[:, 0:T], gv[:, 0:T], ACT.Tanh, scale=math.sqrt(2.0 / math.pi))\
                               .then_inc(sems["rg_act"], 1)
                            act.wait_ge(sems["gates_done"], n + 1 + CREDITS["gates_done"])
                            act.wait_ge(sems["rg_dve"], NRG * (n - 1) + RG["z_sample"] + CREDITS["rg_dve"])
                            act.activation(halves(th_r[:, :]), ps[:, 4:6, 0:TCH], ACT.Tanh, scale=0.5,
                                           bias=rg_brh[:, bass.ds(n, 1)]).then_inc(sems["rg_act"], 1)
                            act.activation(halves(th_i[:, :]), ps[:, 6:8, 0:TCH], ACT.Tanh, scale=0.5,
                                           bias=rg_bih[:, bass.ds(n, 1)]).then_inc(sems["rg_act"], 1)
                            act.wait_ge(sems["rg_act"], ra + RA["tanh_r"] + CREDITS["rg_act"])
                            act.activation(tau[:, :], th_r[:, :], ACT.Tanh, scale=rg_c4[:, bass.ds(n, 1)],
                                           bias=rg_c4[:, bass.ds(n, 1)]).then_inc(sems["rg_act"], 1)
                            act.activation(dec[:, :], th_r[:, :], ACT.Exp, scale=rg_nc4[:, bass.ds(n, 1)],
                                           bias=rg_nc4[:, bass.ds(n, 1)]).then_inc(sems["rg_act"], 1)
                            act.wait_ge(sems["rg_act"], ra + RA["a"] + CREDITS["rg_act"])
                            act.activation(dec2[:, :], dec[:, :], ACT.Square).then_inc(sems["rg_act"], 1)
                            act.wait_ge(sems["rg_dve"], rg + RG["one_minus_a2"] + CREDITS["rg_dve"])
                            act.activation(dec2[:, :], tau[:, :], ACT.Sqrt).then_inc(sems["rg_act"], 1)
                            act.wait_ge(sems["rg_dve"], rg + RG["z_sample"] + CREDITS["rg_dve"])
                            act.activation(h_hi[:, n, :], hf[j][:, :], ACT.Copy).then_inc(sems["h_hi"], 1)
                if s["kind"] in ("kv", "q"):
                    kv = s["kind"] == "kv"
                    with act.Fori(0, s["units"] // 2) as i:
                        for j in range(2):
                            u = u0 + 2 * i + j
                            look_ahead(u0, i, j)
                            for t in range(1 if kv else 2):
                                r = s["rope"] + (2 * i + j if kv else 4 * i + 2 * j + t)
                                full = "w_done" if t else "out0_full"
                                act.wait_ge(sems[full], count(full, u + 1))
                                act.wait_ge(sems["rope_done"], r + CREDITS["rope_done"])
                                for q in range(4):
                                    cp = act.activation(halves(swapped[32 * q:32 * q + 32, :]),
                                                        ps[32 * (q ^ 1):32 * (q ^ 1) + 32, 2 * t:2 * t + 2, 0:TH],
                                                        ACT.Copy)
                                cp.then_inc(sems["rope_swap"], 1)
                            if kv:
                                act.wait_ge(sems["w_done"], u + 1 + CREDITS["w_done"])
                                act.wait_ge(sems["v_turned"], 2 * i + j + CREDITS["v_turned"])
                                act.activation(halves(vraw[:, :]), slot(1), ACT.Copy).then_inc(sems["s1_free"], 1)
                            for t in range(1 if kv else 2):
                                n, rj = (2 * i + j, j) if kv else (4 * i + 2 * j + t, t)
                                act.wait_ge(sems["rope_done"], s["rope"] + n + 1 + CREDITS["rope_done"])
                                act.dma_start((kT_out if kv else qT)[n], rk[rj][:, :])\
                                   .then_inc(sems[f"k_out{rj}"], 16)
                            if kv:
                                act.wait_ge(sems["v_ready"], 2 * i + j + 1 + CREDITS["v_ready"])
                                act.dma_start(v_prompt[2 * i + j], vt[j][:, :].rearrange("p (b e) -> p b e", e=P))\
                                   .then_inc(sems[f"v_out{j}"], 16)
                                act.dma_start(v_sample[2 * i + j], vts[j][:, :]).then_inc(sems[f"v_out{j}"], 16)
                if s["kind"] == "attention":
                    def exps(i, j, t):
                        n = P * (i + 1)
                        act.wait_ge(sems["nmx_ready"], t + 1 + CREDITS["nmx_ready"])
                        act.wait_ge(sems["att_ready"], t - 1 + CREDITS["att_ready"])
                        for m in range(2):
                            e = act.activation(pp[i % 2][:, m, 0:n], ps[:, 2 * (i % 2) + m, 0:n], ACT.Exp,
                                               bias=nmx[:, m:m + 1], accum_out=sums[i % 2][:, m:m + 1])
                        e.then_inc(sems["p_ready"], 1)

                    def turned(i, j, t):
                        n = P * (i + 1)
                        act.wait_ge(sems["tp_done"], t + 1 + CREDITS["tp_done"])
                        act.wait_ge(sems["pv_done"], t + CREDITS["pv_done"])
                        act.activation(attT[:, 0:n], ps[:, 4 + i % 2, 0:n], ACT.Copy).then_inc(sems["attT_ready"], 1)

                    with act.Fori(0, 4) as hp:
                        steps = [(i, j, 8 * hp + 4 * j + i) for j in range(2) for i in range(4)]
                        for n, st in enumerate(steps):
                            exps(*st)
                            if n:
                                turned(*steps[n - 1])
                        turned(*steps[-1])

                    def sample_exp(b):
                        act.wait_ge(sems["snmx"], b + 1)
                        act.wait_ge(sems["at_done"], b + CREDITS["at_done"])
                        act.activation(R["sp"][:, :], ps[:, 0:3, :].rearrange("p b n -> p (b n)")[:, 0:PAST_LEN + S_TOK],
                                       ACT.Exp, bias=nmxs, accum_out=sumss).then_inc(sems["sp_ready"], 1)

                    def sample_turned(b):
                        act.wait_ge(sems["at_done"], b + 1 + CREDITS["at_done"])
                        act.wait_ge(sems["pvs_done"], b + CREDITS["pvs_done"])
                        act.activation(aT[:, 0:512], ps[:, 3, :], ACT.Copy)
                        act.activation(aT[0:S_TOK, 512:512 + S_TOK], ps[0:S_TOK, 4, 0:S_TOK], ACT.Copy)\
                           .then_inc(sems["at_ready"], 1)

                    sample_exp(0)
                    with act.Fori(0, DEC_BATCH - 1) as b:
                        sample_turned(b)
                        sample_exp(b + 1)
                    sample_turned(DEC_BATCH - 1)
                    act.wait_ge(sems["os_evac"], DEC_BATCH + CREDITS["os_evac"])
                    with act.Fori(0, 4) as i:
                        for j in range(2):
                            h = 2 * i + j
                            act.wait_ge(sems["so_sum"], h - 1 + CREDITS["so_sum"])
                            act.activation(sg[j][:, :], oT[:, h, :], ACT.Square).then_inc(sems["so_sq"], 1)
                            act.wait_ge(sems["so_sum"], h + 1 + CREDITS["so_sum"])
                            act.wait_ge(sems["so_n"], h - 1 + CREDITS["so_n"])
                            act.activation(halves(nt[j][:, :]), ps[:, 2 * j:2 * j + 2, 0:TH], ACT.Ln, scale=1.0 / P,
                                           bias=eps_o).then_inc(sems["so_ln"], 1)
                            act.wait_ge(sems["so_ln"], h + 1)
                            act.activation(nt[j][:, :], nt[j][:, :], ACT.Exp, scale=-0.5).then_inc(sems["so_rs"], 1)
                            act.wait_ge(sems["so_n"], h + 1 + CREDITS["so_n"])
                            act.activation(h_hi[:, h, :], hf[j][:, :], ACT.Copy).then_inc(sems["h_hi"], 1)
                if s["kind"] == "final":
                    statistics(s)
                    with act.Fori(0, 4) as i:
                        for j in range(2):
                            k = 2 * i + j
                            act.wait_ge(sems["norm_t"], n0 + k + 1)
                            act.wait_ge(sems[f"out_y{j}"], 16 * i + CREDITS[f"out_y{j}"])
                            act.activation(hf[j][:, :], nt[j][:, :], ACT.Copy, scale=c("final_g")[:, bass.ds(k, 1)])\
                               .then_inc(sems["norm_p"], 1)

        @block.vector
        def _(dve):
            credit(dve, "w_lo", "s0_free", "s1_free", "ada_evac", "norm_s", "res_tmp", "mod_ready", "rg_dve", "rope_done",
                   "v_ready", "att_ready", "o_evac", "nmx_ready", "c_ready", "os_evac", "so_n")
            dve.memset(eps_x, EPS).then_inc(sems["setup_step"], 1)
            dve.wait_ge(sems["setup_step"], 1)
            dve.wait_ge(sems["cst_in"], 16)
            lam_in = c("lru_lambda")
            dve.tensor_scalar(setup[2], lam_in, -1.0, None, ALU.mult).then_inc(sems["setup_step"], 1)
            dve.wait_ge(sems["setup_step"], 2)
            dve.tensor_tensor(setup[1], setup[2], lam_in, ALU.min).then_inc(sems["setup_step"], 1)
            dve.wait_ge(sems["setup_step"], 3)
            lp = c("lam_p").rearrange("p (a b d) -> p a b d", a=2, b=2)
            dots = sg[0][:, 0:2 * HEAD_DIM].rearrange("p (a d) -> p a d", a=2)
            dve.tensor_tensor(dots, lp[:, :, 0, :], lp[:, :, 1, :], ALU.mult).then_inc(sems["setup_step"], 1)
            dve.wait_ge(sems["setup_step"], 4)
            dve.tensor_reduce(lam4[:, 0:2], dots, AXX, ALU.add).then_inc(sems["setup_step"], 1)
            dve.wait_ge(sems["setup_step"], 5)
            dve.wait_ge(sems["setup_exp"], 2)
            dve.tensor_tensor(lam4[:, 0:1], lam4[:, 3:4], lam4[:, 2:3], ALU.subtract).then_inc(sems["setup_step"], 1)
            dve.wait_ge(sems["setup_step"], 6)
            dve.tensor_scalar(neg_lam, lam4[:, 0:1], -LAM_INIT, None, ALU.add).then_inc(sems["setup_step"], 1)
            dve.wait_ge(sems["setup_step"], 7)
            dve.tensor_scalar(lam4[:, 1:2], neg_lam, -1.0, None, ALU.mult).then_inc(sems["setup_step"], 1)
            dve.wait_ge(sems["setup_step"], 8)
            dve.tensor_tensor(lam4[:, 1:2], lam4[:, 1:2], neg_lam, ALU.max).then_inc(sems["setup_step"], 1)
            dve.wait_ge(sems["setup_step"], 9)
            dve.tensor_scalar(lam4[:, 1:2], lam4[:, 1:2], 1.0, None, ALU.add).then_inc(sems["setup_step"], 1)
            dve.wait_ge(sems["setup_step"], 10)
            dve.reciprocal(map_gain[:, 0:1], lam4[:, 1:2]).then_inc(sems["setup_step"], 1)
            dve.wait_ge(sems["setup_step"], 11)
            dve.tensor_tensor(map_gain[:, 1:2], map_gain[:, 0:1], neg_lam, ALU.mult).then_inc(sems["setup_step"], 1)
            dve.wait_ge(sems["setup_step"], 12)
            dve.tensor_scalar(eps_o, map_gain[:, 0:1], EPS, None, ALU.mult).then_inc(sems["setup_step"], 1)
            dve.wait_ge(sems["setup_step"], 13)
            dve.tensor_tensor(eps_o, eps_o, map_gain[:, 0:1], ALU.mult).then_inc(sems["setup_step"], 1)
            dve.wait_ge(sems["setup_step"], 14)
            dve.tensor_tensor(row_sign, c("map0"), map_gain[:, 0:1], ALU.mult).then_inc(sems["setup_step"], 1)
            dve.wait_ge(sems["setup_step"], 15)
            dve.scalar_tensor_tensor(row_sign, c("map1"), map_gain[:, 1:2], row_sign, ALU.mult, ALU.add)\
               .then_inc(sems["setup_step"], 1)
            dve.wait_ge(sems["setup_step"], 16)
            dve.tensor_scalar(gain_o, c("subln_g"), 1.0 - LAM_INIT, None, ALU.mult).then_inc(sems["setup_step"], 1)
            dve.wait_ge(sems["setup_step"], 17)
            e, z, z2, acc = setup[0], setup[1], setup[3], setup[4]
            dve.tensor_scalar(z, e, 2.0, None, ALU.add).then_inc(sems["setup_step"], 1)
            dve.wait_ge(sems["setup_step"], 18)
            dve.reciprocal(z2, z).then_inc(sems["setup_step"], 1)
            dve.wait_ge(sems["setup_step"], 19)
            dve.tensor_tensor(z, z2, e, ALU.mult).then_inc(sems["setup_step"], 1)
            dve.wait_ge(sems["setup_step"], 20)
            dve.tensor_tensor(z2, z, z, ALU.mult).then_inc(sems["setup_step"], 1)
            dve.wait_ge(sems["setup_step"], 21)
            dve.tensor_scalar(acc, z2, 1.0 / 17, 1.0 / 15, ALU.mult, ALU.add).then_inc(sems["setup_step"], 1)
            dve.wait_ge(sems["setup_step"], 22)
            for i, n in enumerate((13, 11, 9, 7, 5, 3, 1)):
                dve.tensor_tensor(acc, acc, z2, ALU.mult).then_inc(sems["setup_step"], 1)
                dve.wait_ge(sems["setup_step"], 23 + 2 * i)
                dve.tensor_scalar(acc, acc, 1.0 / n, None, ALU.add).then_inc(sems["setup_step"], 1)
                dve.wait_ge(sems["setup_step"], 24 + 2 * i)
            dve.tensor_tensor(acc, acc, z, ALU.mult).then_inc(sems["setup_step"], 1)
            dve.wait_ge(sems["setup_step"], 37)
            dve.tensor_scalar(z, setup[2], 0.0, None, ALU.max).then_inc(sems["setup_step"], 1)
            dve.wait_ge(sems["setup_step"], 38)
            dve.scalar_tensor_tensor(acc, acc, 2.0, z, ALU.mult, ALU.add).then_inc(sems["setup_step"], 1)
            dve.wait_ge(sems["setup_step"], 39)
            dve.tensor_scalar(rg_c4, acc, 4.0, None, ALU.mult).then_inc(sems["setup_step"], 1)
            dve.wait_ge(sems["setup_step"], 40)
            dve.tensor_scalar(rg_nc4, acc, -4.0, None, ALU.mult).then_inc(sems["setup_step"], 1)
            dve.wait_ge(sems["setup_step"], 41)
            dve.tensor_scalar(rg_brh, c("b_rg"), 0.5, None, ALU.mult).then_inc(sems["setup_step"], 1)
            dve.wait_ge(sems["setup_step"], 42)
            dve.tensor_scalar(rg_bih, c("b_ig"), 0.5, None, ALU.mult).then_inc(sems["setup_done"], 1)

            def split_unit(u, j):
                dve.wait_ge(sems["w_hi"], u + 1)
                dve.wait_ge(sems["w_done"], u - 1 + CREDITS["w_done"])
                dve.tensor_tensor(w_lo[j][:, :, :].rearrange("p k n -> p (k n)"), raw[j][:, :],
                                  w_hi[j][:, :, :].rearrange("p k n -> p (k n)").bitcast(F32),
                                  ALU.subtract).then_inc(sems["w_lo"], 1)

            def ada_bias(a, j):
                dve.wait_ge(sems["ada_done"], a + 1 + CREDITS["ada_done"])
                dve.tensor_tensor(mods[:, bass.ds(2 * a, 2), :],
                                  ps[:, 4 + j, 0:2 * NC_].rearrange("p (t n) -> p t n", t=2),
                                  c("ada_b")[:, bass.ds(2 * a, 2)].unsqueeze(2).to_broadcast([P, 2, NC_]),
                                  ALU.add).then_inc(sems["ada_evac"], 1)

            with dve.Fori(0, ADA_FIRST // 2) as i:
                for j in range(2):
                    ada_bias(2 * i + j, j)
            split_unit(0, 0)

            def residual(u, k, t, res):
                dve.wait_ge(sems["w_done" if t else "out0_full"], count("w_done" if t else "out0_full", u + 1))
                dve.scalar_tensor_tensor(x[:, k, 0:TH], ps[:, 2 * t, 0:TH], mod_g[:, k, 0:1], x[:, k, 0:TH],
                                         ALU.mult, ALU.add)
                dve.scalar_tensor_tensor(x[:, k, TH:SEQ], ps[:, 2 * t + 1, 0:PB], mod_g[:, k, 0:1], x[:, k, TH:SEQ],
                                         ALU.mult, ALU.add)
                dve.wait_ge(sems["s0_free" if t else "s1_free"], count("s0_free" if t else "s1_free", u + t))
                dve.tensor_tensor(by_seq(r_tmp), by_seq(ps[:, 2 * t + 1, PB:TH]),
                                  mod_g[:, k, 1:NC_].unsqueeze(2).to_broadcast([P, DEC_BATCH, DEC_SEQ]),
                                  ALU.mult).then_inc(sems["res_tmp"], 1)
                dve.wait_ge(sems["res_tmp"], res + 1 + CREDITS["res_tmp"])
                dve.tensor_tensor(x[:, k, SEQ:T], r_tmp, x[:, k, SEQ:T], ALU.add)\
                   .then_inc(sems["s1_free" if t else "s0_free"], 1)

            def rope(u, t, r, scale, j):
                dve.wait_ge(sems["w_done" if t else "out0_full"], count("w_done" if t else "out0_full", u + 1))
                dve.wait_ge(sems["rope_swap"], r + 1)
                dve.scalar_tensor_tensor(halves(rope_a[:, :]), slot(t), scale, halves(c("cos")), ALU.mult, ALU.mult)\
                   .then_inc(sems["s1_free" if t else "s0_free"], 1)
                dve.scalar_tensor_tensor(rope_b[:, :], swapped[:, :], scale, c("sin"), ALU.mult, ALU.mult)\
                   .then_inc(sems["rope_t2"], 1)
                dve.wait_ge(sems["rope_t2"], r + 1)
                dve.tensor_tensor(rk[j][:, :], rope_a[:, :], rope_b[:, :], ALU.add).then_inc(sems["rope_done"], 1)

            for s in plan:
                u0, h0 = s["u"], s["h"]
                n0 = 8 * s["norm"]
                if s["kind"] in ("norm", "final"):
                    if s["kind"] == "norm":
                        dve.wait_ge(sems["ada_evac"], s["ada"] + CREDITS["ada_evac"])
                        dve.wait_ge(sems["norm_p"], n0 + CREDITS["norm_p"])
                        dve.wait_ge(sems["norm_s"], n0 + CREDITS["norm_s"])
                        dve.wait_ge(sems["s1_free"], u0 + CREDITS["s1_free"])
                        sc = mods[:, s["sc"]:s["sc"] + 8, :]
                        gain = dve.scalar_tensor_tensor(
                            mod_a[:, :, :], sc, 1.0,
                            cst[:, s["g"]:s["g"] + 8].unsqueeze(2).to_broadcast([P, 8, NC_]), ALU.add, ALU.mult)
                        if s["ga"] is None:
                            gain.then_inc(sems["mod_ready"], 1)
                        else:
                            dve.tensor_scalar(mod_g[:, :, :], mods[:, s["ga"]:s["ga"] + 8, :], s["half"], None,
                                              ALU.mult).then_inc(sems["mod_ready"], 1)
                        dve.wait_ge(sems["mod_ready"], s["norm"] + 1 + CREDITS["mod_ready"])
                    dve.wait_ge(sems["h_lo"], h0 + CREDITS["h_lo"])
                    dve.wait_ge(sems["rstd_ready"], s["norm"] + 1 + CREDITS["rstd_ready"])
                    with dve.Fori(0, 4) as i:
                        for j in range(2):
                            k = 2 * i + j
                            dve.wait_ge(sems["norm_p"], n0 + k - 1 + CREDITS["norm_p"])
                            if s["kind"] == "norm":
                                dve.wait_ge(sems["norm_s"], n0 + k - 1 + CREDITS["norm_s"])
                            dve.tensor_tensor(nt[j][:, :], x[:, k, :], rstd[:, :], ALU.mult)\
                               .then_inc(sems["norm_t"], 1)
                            if s["kind"] == "norm":
                                dve.wait_ge(sems["norm_t"], n0 + k + 1)
                                dve.wait_ge(sems["norm_s"], n0 + k + CREDITS["norm_s"])
                                dve.tensor_tensor(by_seq(s_tmp), by_seq(nt[j][:, SEQ:T]),
                                                  mod_a[:, k, 1:NC_].unsqueeze(2).to_broadcast([P, DEC_BATCH, DEC_SEQ]),
                                                  ALU.mult).then_inc(sems["norm_tmp"], 1)
                                dve.wait_ge(sems["norm_tmp"], n0 + k + 1)
                                dve.wait_ge(sems["norm_lo"], n0 + k - 1 + CREDITS["norm_lo"])
                                dve.tensor_tensor(by_seq(hf[j][:, SEQ:T]), by_seq(s_tmp),
                                                  mods[:, s["sh"] + k, 1:NC_].unsqueeze(2).to_broadcast(
                                                      [P, DEC_BATCH, DEC_SEQ]),
                                                  ALU.add).then_inc(sems["norm_s"], 1)
                if s["kind"] == "up":
                    with dve.Fori(0, s["units"] // 2) as i:
                        for j in range(2):
                            u, h = u0 + 2 * i + j, h0 + 2 * i + j
                            split_unit(u + 1, 1 - j)
                            dve.wait_ge(sems["w_done"], u + 1 + CREDITS["w_done"])
                            dve.wait_ge(sems["s0_free"], u + 1 + CREDITS["s0_free"])
                            dve.wait_ge(sems["h_lo"], h - 1 + CREDITS["h_lo"])
                            dve.tensor_tensor(halves(hf[j][:, :]), halves(sg[j][:, :]), slot(1), ALU.mult)\
                               .then_inc(sems["s1_free"], 1)
                            if s["has_ada"]:
                                ada_bias(s["ada"] + 2 * i + j, j)
                if s["kind"] == "down":
                    if s["last"]:
                        for n in range(s["units"]):
                            if n < s["units"] - 1:
                                split_unit(u0 + n + 1, 1 - n % 2)
                            for t in range(2):
                                residual(u0 + n, 2 * n + t, t, s["res"] + 2 * n + t)
                    else:
                        with dve.Fori(0, s["units"] // 2) as i:
                            for j in range(2):
                                split_unit(u0 + 2 * i + j + 1, 1 - j)
                                for t in range(2):
                                    n = 4 * i + 2 * j + t
                                    residual(u0 + 2 * i + j, n, t, s["res"] + n)
                if s["kind"] == "rglru":
                    dve.wait_ge(sems["norm_lo"], n0 + CREDITS["norm_lo"])
                    dve.memset(xp[:, 0:PADS], 0.0).then_inc(sems["rg_pad"], 1)
                    dve.wait_ge(sems["rg_pad"], 1)
                    with dve.Fori(0, 4) as i:
                        for j in range(2):
                            u, n = u0 + 2 * i + j, 2 * i + j
                            rg, ra = NRG * n, NRA * n
                            split_unit(u + 1, 1 - j)
                            dve.wait_ge(sems["rg_dve"], rg + CREDITS["rg_dve"])
                            dve.tensor_copy(seq_cols(xp, S0, PADS), c("st_conv")[:, bass.ds(24 * n, 24)].rearrange(
                                "p (b s) -> p b s", b=DEC_BATCH)).then_inc(sems["rg_dve"], 1)
                            dve.wait_ge(sems["s0_free"], u + 1 + CREDITS["s0_free"])
                            dve.tensor_copy(conv_sb[:, n, 0, :], xp[:, SEQ:SEQ + PADS])\
                               .then_inc(sems["rg_dve"], 1)
                            dve.tensor_copy(conv_sb[:, n, 1:NC_, :], seq_cols(xp, S0 + DEC_SEQ, PADS))\
                               .then_inc(sems["rg_dve"], 1)
                            dve.wait_ge(sems["gates_done"], n + CREDITS["gates_done"])
                            dve.wait_ge(sems["rg_dve"], rg + RG["state_in"] + CREDITS["rg_dve"])
                            cw = c("conv_w")
                            dve.tensor_scalar(xc[:, :], xp[:, 0:TC], cw[:, bass.ds(4 * n, 1)],
                                                  c("conv_b")[:, bass.ds(n, 1)], ALU.mult, ALU.add)\
                                                     .then_inc(sems["rg_dve"], 1)
                            for w in range(1, CONV_W):
                                dve.wait_ge(sems["rg_dve"], rg + RG[f"tap{w - 1}"] + CREDITS["rg_dve"])
                                dve.scalar_tensor_tensor(xc[:, :], xp[:, w:w + TC], cw[:, bass.ds(4 * n + w, 1)],
                                                             xc[:, :], ALU.mult, ALU.add)\
                                                                .then_inc(sems["rg_dve"], 1)
                            dve.wait_ge(sems["rg_act"], ra + RA["y2"] + CREDITS["rg_act"])
                            dve.tensor_scalar(gv[:, 0:T], gv[:, 0:T], 0.044715, 1.0, ALU.mult, ALU.add)\
                               .then_inc(sems["rg_dve"], 1)
                            dve.wait_ge(sems["rg_dve"], rg + RG["gelu_poly"] + CREDITS["rg_dve"])
                            dve.tensor_tensor(halves(gv[:, 0:T]), halves(gv[:, 0:T]), slot(1), ALU.mult)\
                               .then_inc(sems["rg_dve"], 1)
                            dve.wait_ge(sems["rg_act"], ra + RA["gelu_tanh"] + CREDITS["rg_act"])
                            dve.scalar_tensor_tensor(halves(gy[:, 0:T]), halves(gt[:, 0:T]), 1.0, slot(1), ALU.add,
                                                     ALU.mult).then_inc(sems["s1_free"], 1)
                            dve.wait_ge(sems["s1_free"], u + 1 + CREDITS["s1_free"])
                            dve.wait_ge(sems["rg_act"], ra + RA["tanh_i"] + CREDITS["rg_act"])
                            dve.scalar_tensor_tensor(xc[:, :], th_i[:, :], 1.0, xc[:, :], ALU.add, ALU.mult)\
                               .then_inc(sems["rg_dve"], 1)
                            dve.wait_ge(sems["rg_act"], ra + RA["a2"] + CREDITS["rg_act"])
                            dve.scalar_tensor_tensor(tau[:, :], dec2[:, :], 1.0, tau[:, :], ALU.add, ALU.mult)\
                               .then_inc(sems["rg_dve"], 1)
                            dve.wait_ge(sems["rg_act"], ra + RA["root"] + CREDITS["rg_act"])
                            dve.wait_ge(sems["rg_dve"], rg + RG["gated_x"] + CREDITS["rg_dve"])
                            dve.scalar_tensor_tensor(xc[:, :], dec2[:, :], 0.5, xc[:, :], ALU.mult, ALU.mult)\
                               .then_inc(sems["rg_dve"], 1)
                            dve.wait_ge(sems["rg_dve"], rg + RG["u"] + CREDITS["rg_dve"])
                            dve.memset(seq_cols(dec, S0 - 1, 1), 0.0).then_inc(sems["rg_dve"], 1)
                            dve.tensor_copy(seq_cols(xc, S0 - 1, 1),
                                                c("st_h")[:, bass.ds(8 * n, 8)].unsqueeze(2))\
                                                   .then_inc(sems["rg_dve"], 1)
                            dve.wait_ge(sems["rg_dve"], rg + RG["reset_u"] + CREDITS["rg_dve"])
                            dve.tensor_tensor_scan(hs[:, :], dec[:, :], xc[:, :], 0.0, ALU.mult, ALU.add)\
                               .then_inc(sems["rg_dve"], 1)
                            dve.wait_ge(sems["rg_dve"], rg + RG["scan"] + CREDITS["rg_dve"])
                            dve.tensor_copy(h_sb[:, n, 0:1], hs[:, SEQ - 1:SEQ])\
                               .then_inc(sems["rg_dve"], 1)
                            dve.tensor_copy(h_sb[:, n, 1:NC_].unsqueeze(2), seq_cols(hs, S0 + DEC_SEQ - 1, 1))\
                               .then_inc(sems["rg_dve"], 1)
                            dve.wait_ge(sems["h_lo"], h0 + n - 1 + CREDITS["h_lo"])
                            dve.scalar_tensor_tensor(hf[j][:, 0:SEQ], hs[:, 0:SEQ], 0.5, gy[:, 0:SEQ], ALU.mult,
                                                         ALU.mult).then_inc(sems["rg_dve"], 1)
                            dve.scalar_tensor_tensor(by_seq(hf[j][:, SEQ:T]), seq_cols(hs, S0, DEC_SEQ), 0.5,
                                                         by_seq(gy[:, SEQ:T]), ALU.mult, ALU.mult)\
                                                            .then_inc(sems["rg_dve"], 1)
                if s["kind"] in ("kv", "q"):
                    kv = s["kind"] == "kv"
                    with dve.Fori(0, s["units"] // 2) as i:
                        for j in range(2):
                            u = u0 + 2 * i + j
                            split_unit(u + 1, 1 - j)
                            for t in range(1 if kv else 2):
                                n = 2 * i + j if kv else 4 * i + 2 * j + t
                                rj = j if kv else t
                                dve.wait_ge(sems[f"k_out{rj}"], 16 * (i if kv else 4 + 2 * i + j) + CREDITS[f"k_out{rj}"])
                                rope(u, t, s["rope"] + n, 1.0 if kv else HEAD_DIM ** -0.5, rj)
                            if kv:
                                dve.wait_ge(sems["v_turned"], 2 * i + j + 1 + CREDITS["v_turned"])
                                dve.wait_ge(sems[f"v_out{j}"], 32 * i + CREDITS[f"v_out{j}"])
                                dve.tensor_copy(vt[j][:, :], ps[:, 4, :])
                                dve.tensor_copy(vts[j][:, :], ps[0:S_TOK, 5, 0:P]).then_inc(sems["v_ready"], 1)
                if s["kind"] == "attention":
                    causal = c("causal").unsqueeze(1).to_broadcast([P, 2, P])

                    def maximum(i, t):
                        n, b = P * (i + 1), 2 * (i % 2)
                        dve.wait_ge(sems["sc_full"], t + 1)
                        dve.tensor_tensor(ps[:, b:b + 2, P * i:P * i + P], ps[:, b:b + 2, P * i:P * i + P], causal,
                                          ALU.add).then_inc(sems["masked"], 1)
                        dve.wait_ge(sems["masked"], t + 1)
                        dve.wait_ge(sems["nmx_ready"], t + CREDITS["nmx_ready"])
                        dve.tensor_reduce(mx, ps[:, b:b + 2, 0:n], AXX, ALU.max).then_inc(sems["max_ready"], 1)
                        dve.wait_ge(sems["max_ready"], t + 1)
                        dve.wait_ge(sems["p_ready"], t + CREDITS["p_ready"])
                        dve.tensor_scalar(nmx, mx, -1.0, None, ALU.mult).then_inc(sems["nmx_ready"], 1)

                    def differ(i, t):
                        n = P * (i + 1)
                        dve.wait_ge(sems["p_ready"], t + 1 + CREDITS["p_ready"])
                        dve.wait_ge(sems["att_ready"], t + CREDITS["att_ready"])
                        dve.reciprocal(rsum, sums[i % 2]).then_inc(sems["coef_ready"], 1)
                        dve.wait_ge(sems["coef_ready"], 2 * t + 1)
                        dve.tensor_tensor(rsum, rsum, map_gain, ALU.mult)\
                           .then_inc(sems["coef_ready"], 1)
                        dve.wait_ge(sems["coef_ready"], 2 * t + 2)
                        dve.wait_ge(sems["tp_done"], t + CREDITS["tp_done"])
                        dve.tensor_scalar(att[:, 0:n], pp[i % 2][:, 0, 0:n], rsum[:, 0:1], None, ALU.mult)\
                           .then_inc(sems["att_part"], 1)
                        dve.wait_ge(sems["att_part"], t + 1)
                        dve.scalar_tensor_tensor(att[:, 0:n], pp[i % 2][:, 1, 0:n], rsum[:, 1:2], att[:, 0:n],
                                                 ALU.mult, ALU.add).then_inc(sems["att_ready"], 1)

                    def head_out(h, j):
                        dve.wait_ge(sems["pv_done"], 4 * h + 4 + CREDITS["pv_done"])
                        dve.tensor_copy(oT[:, h, 0:SEQ], ps[:, 6 + j, :]).then_inc(sems["o_evac"], 1)

                    for j in range(2):
                        dve.wait_ge(sems[f"k_out{j}"], 16 * 8 + CREDITS[f"k_out{j}"])
                    with dve.Fori(0, 4) as hp:
                        steps = [(i, 8 * hp + 4 * j + i) for j in range(2) for i in range(4)]
                        for n, st in enumerate(steps):
                            maximum(*st)
                            if n:
                                differ(*steps[n - 1])
                            if n == 5:
                                head_out(2 * hp, 0)
                        differ(*steps[-1])
                        head_out(2 * hp + 1, 1)

                    s_all = ps[:, 0:3, :].rearrange("p b n -> p (b n)")[:, 0:PAST_LEN + S_TOK]

                    def sample_max(b):
                        dve.wait_ge(sems["ss_full"], b + 1 + CREDITS["ss_full"])
                        dve.tensor_tensor(ps[:, 2, 0:S_TOK], ps[:, 2, 0:S_TOK],
                                          c("smask")[:, bass.ds(S_TOK * b, S_TOK)], ALU.add)\
                           .then_inc(sems["smasked"], 1)
                        dve.wait_ge(sems["smasked"], b + 1)
                        dve.tensor_reduce(mxs, s_all, AXX, ALU.max).then_inc(sems["smax"], 1)
                        dve.wait_ge(sems["smax"], b + 1)
                        dve.wait_ge(sems["sp_ready"], b + CREDITS["sp_ready"])
                        dve.tensor_scalar(nmxs, mxs, -1.0, None, ALU.mult).then_inc(sems["snmx"], 1)

                    def sample_coef(b):
                        dve.wait_ge(sems["sp_ready"], b + 1 + CREDITS["sp_ready"])
                        dve.reciprocal(rss, sumss).then_inc(sems["srs"], 1)
                        dve.wait_ge(sems["srs"], 2 * b + 1)
                        dve.tensor_tensor(coef, rss, row_sign, ALU.mult).then_inc(sems["srs"], 1)
                        dve.wait_ge(sems["srs"], 2 * b + 2)
                        dve.wait_ge(sems["at_done"], b + CREDITS["at_done"])
                        dve.tensor_scalar(cmat[:, :], c("comb"), coef, None, ALU.mult).then_inc(sems["c_ready"], 1)

                    def sample_out(b):
                        dve.wait_ge(sems["pvs_done"], b + 1 + CREDITS["pvs_done"])
                        dve.tensor_copy(oT[:, :, bass.ds(SEQ + DEC_SEQ * b, DEC_SEQ)],
                                        ps[:, 5, 0:S_TOK].rearrange("p (h s) -> p h s", h=N_HEADS))\
                           .then_inc(sems["os_evac"], 1)

                    sample_max(0)
                    sample_coef(0)
                    with dve.Fori(0, DEC_BATCH - 1) as b:
                        sample_max(b + 1)
                        sample_coef(b + 1)
                        sample_out(b)
                    sample_out(DEC_BATCH - 1)
                    with dve.Fori(0, 4) as i:
                        for j in range(2):
                            h = 2 * i + j
                            dve.wait_ge(sems["so_rs"], h + 1 + CREDITS["so_rs"])
                            dve.wait_ge(sems["h_lo"], h0 + h - 1 + CREDITS["h_lo"])
                            dve.scalar_tensor_tensor(hf[j][:, :], oT[:, h, :], gain_o, nt[j][:, :], ALU.mult,
                                                     ALU.mult).then_inc(sems["so_n"], 1)

        @block.gpsimd
        def _(pool):
            credit(pool, "norm_lo", "h_lo")

            def lo_part(j, k, hi, lo, hi_sem, n, lo_sem):
                pool.wait_ge(sems[hi_sem], count(hi_sem, n + 1))
                pool.tensor_tensor(lo[:, k, :], hf[j][:, :], hi[:, k, :].bitcast(F32), ALU.subtract)\
                    .then_inc(sems[lo_sem], 1)

            for s in plan:
                n0, h0 = 8 * s["norm"], s["h"]
                if s["kind"] == "norm":
                    with pool.Fori(0, 4) as i:
                        for j in range(2):
                            lo_part(j, 2 * i + j, hh_hi, hh_lo, "norm_hi", n0 + 2 * i + j, "norm_lo")
                if s["kind"] in ("up", "rglru"):
                    with pool.Fori(0, s["units"] // 2) as i:
                        for j in range(2):
                            lo_part(j, 2 * i + j, h_hi, h_lo, "h_hi", h0 + 2 * i + j, "h_lo")
                if s["kind"] == "attention":
                    pool.wait_ge(sems["o_evac"], N_HEADS + CREDITS["o_evac"])
                    pool.memset(qbd[:, :], 0.0).then_inc(sems["qbd_zero"], 1)
                    pool.wait_ge(sems["s_small"], 48)
                    pool.wait_ge(sems["qbd_zero"], 1)
                    with pool.Fori(0, DEC_BATCH) as b:
                        pool.wait_ge(sems["ss_full"], b + CREDITS["ss_full"])
                        for m in range(2):
                            base = qbd[64 * m:64 * m + 64, 8 * m:8 * m + 8]
                            out = bass.AP(base.tensor, base.offset, [list(base.ap[0]), [144, N_HEADS], [1, DEC_SEQ]])
                            pool.tensor_copy(out, qs[64 * m:64 * m + 64, :, bass.ds(DEC_SEQ * b, DEC_SEQ)])\
                                .then_inc(sems["qbd_ready"], 1)
                    with pool.Fori(0, 4) as i:
                        for j in range(2):
                            lo_part(j, 2 * i + j, h_hi, h_lo, "h_hi", h0 + 2 * i + j, "h_lo")


def constants():
    out = {"ident": np.eye(P), "ones": np.ones((P, P)), "causal": np.where(np.arange(P)[None] <= np.arange(P)[:, None], 0, NEG)}
    half = HEAD_DIM // 2
    inv = (1.0 / (np.float32(ROPE_THETA) ** (np.arange(half, dtype=np.float32) * np.float32(2.0 / HEAD_DIM))))
    pos = np.concatenate([np.arange(SEQ), np.tile(PAST_LEN + np.arange(DEC_SEQ), DEC_BATCH)]).astype(np.float32)
    ang = (inv.astype(np.float32)[:, None] * pos[None]).astype(np.float32)
    out["cos"] = np.tile(np.cos(ang), (4, 1))
    out["sin"] = np.tile(np.concatenate([-np.sin(ang), np.sin(ang)]), (2, 1))
    row = np.arange(P)
    h, m, q = row // 16, row // 8 % 2, row % 8
    key = np.arange(S_TOK)
    seen = (key[None, None] // 8 == np.arange(DEC_BATCH)[None, :, None]) & (key[None, None] % 8 <= q[:, None, None])
    out["smask"] = np.where(seen, 0, NEG).reshape(P, -1)
    out["comb"] = key[None] == (8 * h + q)[:, None]
    out["map0"], out["map1"] = (m == 0)[:, None], (m == 1)[:, None]
    return {k: v.astype(np.float32) for k, v in out.items()}


def kernel(**inputs):
    import concourse.bacc as bacc
    from concourse.bass_utils import run_bass_kernel_spmd

    a = {k: np.asarray(v) for k, v in inputs.items()}
    f32 = np.float32

    def rows(v):
        v = v.reshape(-1, KT, P)
        return v.transpose(2, 0, 1).reshape(P, -1)

    def units(w):
        k, n = w.shape
        return np.ascontiguousarray(w.reshape(k // P, P, n // 256, 256).transpose(2, 1, 0, 3)).reshape(n // 256, P, -1)

    def paired(wa, wb):
        k, n = wa.shape
        both = np.stack([w.reshape(k // P, P, n // P, P) for w in (wa, wb)], axis=3)
        return np.ascontiguousarray(both.transpose(2, 1, 0, 3, 4)).reshape(n // P, P, -1)

    k = constants()
    cond = np.concatenate([a["c_prompt"], a["c_sample"]])
    k["cond"] = cond.reshape(NC_, KT, P).transpose(2, 1, 0).reshape(P, -1)
    k["ada_b"] = rows(np.concatenate([a["ada_b"][0], a["kv_ada_b"], a["ada_b"][1]]))
    k["norm_g"], k["kv_g"], k["final_g"] = rows(a["norm_g"]), rows(a["kv_norm_g"]), rows(a["final_g"])
    k["conv_w"] = a["a_conv_w"][0].reshape(CONV_W, KT, P).transpose(2, 1, 0).reshape(P, -1)
    k["conv_b"], k["b_rg"], k["b_ig"] = rows(a["a_conv_b"]), rows(a["a_b_rg"]), rows(a["a_b_ig"])
    k["lru_lambda"] = rows(a["a_lambda"])
    k["subln_g"] = a["b_subln_g"].reshape(P, 1)
    k["lam_p"] = np.broadcast_to(a["b_lambda"].reshape(1, -1), (P, 4 * HEAD_DIM))
    k["st_conv"] = a["state_conv"][0].reshape(DEC_BATCH, PADS, KT, P).transpose(3, 2, 0, 1).reshape(P, -1)
    k["st_h"] = a["state_h"][0].reshape(DEC_BATCH, KT, P).transpose(2, 1, 0).reshape(P, -1)
    consts = np.concatenate([k[name].reshape(P, n) for name, (_, n) in CONST.items()], axis=1)

    tokens = np.concatenate([a["x_prompt"].reshape(SEQ, -1), a["x_sample"].reshape(S_TOK, -1)])
    gu, wd = a["ffn_w_gu"].reshape(4, D_MODEL, 2 * D_FF), a["ffn_w_d"].reshape(4, D_FF, D_MODEL)
    feeds = {
        "consts": consts,
        "xT": tokens.reshape(T, KT, P).transpose(2, 1, 0),
        "page_table": a["page_table"].reshape(1, -1),
        "ada_w": np.concatenate([units(a["ada_w"][0]), units(a["kv_ada_w"]), units(a["ada_w"][1])]),
        "w_gu": np.stack([paired(w[:, :D_FF], w[:, D_FF:]) for w in gu]),
        "w_d8": np.stack([np.stack([units(w[1024 * n:1024 * n + 1024]) for n in range(2)]) for w in wd]),
        "w_d6": np.stack([units(w[2048:]) for w in wd]),
        "w_in": paired(a["a_w_in"][0][:, :D_MODEL], a["a_w_in"][0][:, D_MODEL:]),
        "w_gate": np.concatenate([a["a_w_rg"][0], a["a_w_ig"][0]], axis=2),
        "w_out": units(a["a_w_out"][0]),
        "w_kv": paired(a["w_kv"][:, :D_MODEL], a["w_kv"][:, D_MODEL:]),
        "w_q": units(a["b_w_q"][0]),
        "w_o": units(a["b_w_o"][0]),
        "k_cache": a["cache_k"].transpose(0, 3, 4, 2, 1).reshape(-1, P, N_HEADS * PAGE),
        "v_cache": a["cache_v"].reshape(-1, PAGE, N_HEADS * P),
    }
    outs = {"yT": (KT, P, T), "conv_out": (P, KT, NC_, PADS), "h_out": (P, KT, NC_), "kT_out": (N_HEADS, P, T),
            "v_prompt": (N_HEADS, P, 4, P), "v_sample": (N_HEADS, S_TOK, P)}

    nc = bacc.Bacc("TRN2", target_bir_lowering=False, num_devices=1)
    arrays, args = {}, []
    for name, v in feeds.items():
        v = np.ascontiguousarray(v)
        arrays["in_" + name] = v
        args.append(nc.dram_tensor("in_" + name, v.shape, mybir.dt.from_np(v.dtype), kind="ExternalInput").ap())
    for name, shape in outs.items():
        args.append(nc.dram_tensor("out_" + name, shape, F32, kind="ExternalOutput").ap())
    trunk(nc, *args)
    r = run_bass_kernel_spmd(nc, [arrays], core_ids=[0]).results[0]
    o = {name: r["out_" + name] for name in outs}

    y = o["yT"].reshape(D_MODEL, T).transpose(1, 0)
    conv = o["conv_out"].transpose(2, 3, 1, 0).reshape(NC_, PADS, D_MODEL)
    h = o["h_out"].transpose(2, 1, 0).reshape(NC_, D_MODEL)
    kk = o["kT_out"].transpose(2, 0, 1).reshape(T, N_HEADS, 2, HEAD_DIM)
    vp = o["v_prompt"].transpose(2, 1, 0, 3)
    vs = o["v_sample"].transpose(1, 0, 2)
    got = (y[:SEQ].reshape(1, SEQ, D_MODEL), y[SEQ:].reshape(DEC_BATCH, DEC_SEQ, D_MODEL),
           conv[:1].reshape(1, 1, PADS, D_MODEL), h[:1].reshape(1, 1, D_MODEL),
           kk[:SEQ].reshape(1, SEQ, N_HEADS, 2, HEAD_DIM), vp.reshape(1, SEQ, N_HEADS, P),
           conv[1:].reshape(1, DEC_BATCH, PADS, D_MODEL), h[1:].reshape(1, DEC_BATCH, D_MODEL),
           kk[SEQ:].reshape(DEC_BATCH, DEC_SEQ, N_HEADS, 2, HEAD_DIM), vs.reshape(DEC_BATCH, DEC_SEQ, N_HEADS, P))
    return tuple(np.ascontiguousarray(v) for v in got)
```

```python
from contextlib import ExitStack
import math

import numpy as np
import concourse.bass as bass
from concourse import mybir

F32 = mybir.dt.float32
F32R = mybir.dt.float32r
I32 = mybir.dt.int32
ALU = mybir.AluOpType
ACT = mybir.ActivationFunctionType
AXX = mybir.AxisListType.X

P = 128
D_MODEL = 1024
SEQ = 512
DEC_BATCH = 8
DEC_SEQ = 8
PAST_LEN = 1024
PAGE = 128
N_HEADS = 8
HEAD_DIM = 64
D_FF = 2816
CONV_W = 4
N_ADA = 9
EPS = 1e-6
ROPE_THETA = 10000.0
LAM_INIT = 0.8 - 0.6 * math.exp(-0.3 * 1)
NEG = -1e30

KT = D_MODEL // P
FT = D_FF // P
S_TOK = DEC_BATCH * DEC_SEQ
T = SEQ + S_TOK
TH = T // 2
PB = SEQ - TH
NC_ = 1 + DEC_BATCH
N_PAGES = PAST_LEN // PAGE
PADS = CONV_W - 1
SEG = PADS + DEC_SEQ
TPAD = PADS + SEQ + DEC_BATCH * SEG
TC = TPAD - PADS
TCH = TC // 2
S0 = SEQ + PADS
UNIT = 8 * 256
CHUNKS = (8, 8, 6)
ADA_FIRST = 14
ADA_TILES = N_ADA * KT
KV_TILE0 = ADA_TILES
L1_TILE0 = ADA_TILES + 2 * KT
N_MOD_TILES = 2 * ADA_TILES + 2 * KT

CONST = {}
_at = 0
for _name, _n in (("ident", P), ("ones", P), ("cond", KT * NC_), ("ada_b", N_MOD_TILES), ("norm_g", 6 * KT),
                  ("kv_g", KT), ("final_g", KT), ("conv_w", KT * CONV_W), ("conv_b", KT), ("b_rg", KT), ("b_ig", KT),
                  ("lru_lambda", KT), ("subln_g", 1), ("lam_p", 4 * HEAD_DIM), ("st_conv", KT * DEC_BATCH * PADS),
                  ("st_h", KT * DEC_BATCH), ("cos", T), ("sin", T), ("causal", P), ("smask", DEC_BATCH * S_TOK),
                  ("comb", S_TOK), ("map0", 1), ("map1", 1), ("fold", NC_)):
    CONST[_name] = (_at, _n)
    _at += _n
N_CONST = _at

RG = {n: i + 1 for i, n in enumerate(
    ("state_in", "conv_prompt_out", "conv_sample_out", "tap0", "tap1", "tap2", "tap3", "gelu_poly", "gelu_arg",
     "gated_x", "one_minus_a2", "u", "reset_a", "reset_u", "scan", "h_prompt", "h_sample",
     "z_prompt", "z_sample"))}
NRG = len(RG)
RA = {n: i + 1 for i, n in enumerate(("y2", "gelu_tanh", "tanh_r", "tanh_i", "tau", "a", "a2", "root"))}
NRA = len(RA)

CREDITS = {"k_out0": 16, "k_out1": 16, "v_out0": 16, "v_out1": 16, "w_done": 2, "w_lo": 2, "s0_free": 2,
           "s1_free": 2, "ada_done": 2, "ada_rows": 2, "ada_evac": 2,
           "norm_p": 2, "norm_s": 2, "norm_lo": 2, "res_tmp": 1, "h_lo": 2, "mod_ready": 1,
           "rg_dve": NRG, "rg_act": NRA, "gates_done": 2, "rope_done": 2, "v_turned": 1,
           "v_ready": 2, "p_ready": 1, "att_ready": 2, "tp_done": 1, "attT_ready": 1, "pv_done": 8, "o_evac": 1,
           "nmx_ready": 1, "kg_done": 2, "v_used": 4, "ss_full": 1, "sp_ready": 1, "c_ready": 1, "at_done": 1,
           "at_ready": 1, "pvs_done": 1, "os_picked": 1, "os_evac": 1, "so_sum": 2, "so_rs": 2, "so_n": 2, "out_y0": 16, "out_y1": 16}


def trunk(nc, consts, xT, page_table, ada_w, w_gu, w_d8, w_d6, w_in, w_gate, w_out, w_kv, w_q, w_o, k_cache, v_cache,
          yT, conv_out, h_out, kT_out, v_prompt, v_sample):
    qT = nc.dram_tensor("qT", [N_HEADS, P, T], F32, kind="Internal").ap()

    plan = []
    count = {"u": 0, "ada": ADA_FIRST, "norm": 0, "stat": 1, "h": 0, "res": 0, "rope": 0}

    def stage(kind, units=0, **more):
        plan.append({"kind": kind, "units": units, **count, **more})
        count["u"] += units

    def norm(**more):
        stage("norm", **more)
        count["norm"] += 1

    def down(**more):
        stage("down", 4, row=0, **more)
        count["res"] += 8
        if more["sums"]:
            count["stat"] += 1

    def ffn(layer, which):
        tile0 = L1_TILE0 * layer
        chunk0 = 6 * which
        norm(sh=tile0 + 8 * chunk0, sc=tile0 + 8 * chunk0 + 8, ga=tile0 + 8 * chunk0 + 16,
             g=CONST["norm_g"][0] + 8 * (3 * layer + 2 * which), half=0.5)
        first = 0
        for c, tiles in enumerate(CHUNKS):
            has_ada = not (layer == 1 and which == 1)
            stage("up", tiles, src=w_gu[2 * layer + which], row=first, has_ada=has_ada)
            count["h"] += tiles
            count["ada"] += tiles if has_ada else 0
            first += tiles
            src = w_d8[2 * layer + which, c] if tiles == 8 else w_d6[2 * layer + which]
            down(src=src, k=tiles, sums=(c == len(CHUNKS) - 1), last=(layer == 1 and which == 1 and c == 2))

    def mixer_norm(tile0, g, gate):
        norm(sh=tile0, sc=tile0 + 8, ga=tile0 + 16 if gate else None, g=g, half=1.0)

    ffn(0, 0)
    mixer_norm(24, CONST["norm_g"][0] + 8, True)
    stage("rglru", 8, src=w_in, row=0)
    count["h"] += 8
    down(src=w_out, k=8, sums=True, last=False)
    ffn(0, 1)
    mixer_norm(KV_TILE0, CONST["kv_g"][0], False)
    stage("kv", 8, src=w_kv, row=0)
    count["rope"] += 8
    ffn(1, 0)
    mixer_norm(L1_TILE0 + 24, CONST["norm_g"][0] + 8 * 4, True)
    stage("q", 4, src=w_q, row=0)
    count["rope"] += 8
    stage("attention")
    count["h"] += 8
    down(src=w_o, k=8, sums=True, last=False, loaded=2)
    ffn(1, 1)
    stage("final")
    assert count["ada"] * 2 == N_MOD_TILES

    with ExitStack() as ctx:
        def sb(name, shape, dt=F32, where=None):
            return (where or ctx).enter_context(nc.sbuf_tensor(name, shape, dt))

        cst = sb("cst", [P, N_CONST])
        x = sb("x", [P, KT, T])
        raw = [sb(f"raw{j}", [P, UNIT]) for j in range(2)]
        w_hi = [sb(f"w_hi{j}", [P, 8, 256], F32R) for j in range(2)]
        w_lo = [sb(f"w_lo{j}", [P, 8, 256], F32R) for j in range(2)]
        mods = sb("mods", [P, N_MOD_TILES, NC_])
        act_c = sb("act_c", [P, KT, NC_])
        c_hl = sb("c_hl", [P, KT, 2 * NC_], F32R)
        mod_a = sb("mod_a", [P, KT, NC_])
        mod_g = sb("mod_g", [P, KT, NC_])
        sg = [sb(f"sg{j}", [P, T]) for j in range(2)]
        hf = [sb(f"hf{j}", [P, T]) for j in range(2)]
        nt = [sb(f"nt{j}", [P, T]) for j in range(2)]
        rstd = sb("rstd", [P, T])
        small = sb("small", [P, 256])
        s_tmp = small[:, 0:S_TOK]
        r_tmp = small[:, S_TOK:2 * S_TOK]
        rg_c4 = small[:, 128:136]
        rg_nc4 = small[:, 136:144]
        rg_brh = small[:, 144:152]
        rg_bih = small[:, 152:160]
        neg_lam = small[:, 160:161]
        map_gain = small[:, 241:243]
        eps_x = small[:, 240:241]
        eps_o = small[:, 243:244]
        row_sign = small[:, 161:162]
        gain_o = small[:, 162:163]
        mx = small[:, 164:166]
        nmx = small[:, 166:168]
        sums = [small[:, 168:170], small[:, 170:172]]
        rsum = small[:, 172:174]
        mxs = small[:, 174:175]
        nmxs = small[:, 175:176]
        sumss = small[:, 176:177]
        mxs2 = small[:, 244:246]
        sumss2 = small[:, 246:248]
        rss = small[:, 177:178]
        coef = small[:, 178:179]
        setup = [small[:, 180 + 8 * i:188 + 8 * i] for i in range(6)]
        lam4 = small[:, 228:232]
        pt_sb = sb("pt_sb", [1, DEC_BATCH * N_PAGES], I32)
        conv_sb = sb("conv_sb", [P, KT, NC_, PADS])
        h_sb = sb("h_sb", [P, KT, NC_])

        region = {}

        def laid(key, below, *tensors):
            with ExitStack() as part:
                if below:
                    sb("below_" + key, [P, below], F32, part)
                for name, shape, dt in tensors:
                    region[name] = sb(name, shape, dt, part)

        hh = KT * T
        laid("linear", 0, ("hh_hi", [P, KT, T], F32R), ("hh_lo", [P, KT, T], F32R),
             ("h_hi", [P, KT, T], F32R), ("h_lo", [P, KT, T], F32R),
             ("ada0", [P, KT, 256], F32), ("ada1", [P, KT, 256], F32),
             ("ada_hi0", [P, KT, 256], F32R), ("ada_hi1", [P, KT, 256], F32R))
        laid("ada_lo", 4 * hh, ("ada_lo0", [P, KT, 256], F32R), ("ada_lo1", [P, KT, 256], F32R))
        laid("rglru", 4 * hh, *[(n, [P, TPAD if n == "xp" else TC], F32) for n in
                                ("xp", "xc", "th_r", "th_i", "tau", "a", "a2", "hs", "gv", "gt", "gy")],
             ("gw0", [P, 256], F32), ("gw1", [P, 256], F32))
        laid("rope", 4 * hh + 2 * UNIT, ("swapped", [P, T], F32), ("rope_a", [P, T], F32),
             ("rope_b", [P, T], F32))
        laid("rope_out", 2 * hh, ("rk0", [P, T], F32), ("rk1", [P, T], F32), ("vraw", [P, T], F32),
             ("vt0", [P, SEQ], F32), ("vt1", [P, SEQ], F32), ("vts0", [S_TOK, P], F32), ("vts1", [S_TOK, P], F32))
        laid("attention", 0, ("kr0", [P, 4, N_HEADS, PAGE], F32), ("kr1", [P, 4, N_HEADS, PAGE], F32),
             *[(f"vr{i}", [P, N_HEADS * P], F32) for i in range(4)],
             ("qs", [P, N_HEADS, S_TOK], F32), ("ks", [P, N_HEADS, S_TOK], F32),
             ("vs", [S_TOK, N_HEADS, P], F32))
        att0 = 8192 + 4096 + 2 * N_HEADS * S_TOK + N_HEADS * P
        laid("att_prompt", att0, ("qh0", [P, SEQ], F32), ("qh1", [P, SEQ], F32), ("kh0", [P, SEQ], F32),
             ("kh1", [P, SEQ], F32), ("vh0", [P, 4, P], F32), ("vh1", [P, 4, P], F32), ("pp0", [P, 2, SEQ], F32),
             ("pp1", [P, 2, SEQ], F32), ("oT", [P, N_HEADS, T], F32), ("qbd", [P, N_HEADS * 144], F32), ("probs", [P, PAST_LEN + S_TOK], F32))
        R = region
        hh_hi, hh_lo, h_hi, h_lo = R["hh_hi"], R["hh_lo"], R["h_hi"], R["h_lo"]
        ada, ada_hi, ada_lo = ([R[f"{name}{j}"] for j in range(2)] for name in ("ada", "ada_hi", "ada_lo"))
        xp, xc, th_r, th_i = R["xp"], R["xc"], R["th_r"], R["th_i"]
        tau, dec, dec2, hs, gv, gt, gy = R["tau"], R["a"], R["a2"], R["hs"], R["gv"], R["gt"], R["gy"]
        gw = [R["gw0"], R["gw1"]]
        swapped, rope_a, rope_b = R["swapped"], R["rope_a"], R["rope_b"]
        rk, vraw, vt, vts = [R["rk0"], R["rk1"]], R["vraw"], [R["vt0"], R["vt1"]], [R["vts0"], R["vts1"]]
        kr, vr = [R["kr0"], R["kr1"]], [R[f"vr{i}"] for i in range(4)]
        oT, qs, ks, vs = R["oT"], R["qs"], R["ks"], R["vs"]
        qh, kh, vh = [R["qh0"], R["qh1"]], [R["kh0"], R["kh1"]], [R["vh0"], R["vh1"]]
        pp, att, attT = [R["pp0"], R["pp1"]], nt[0][:, 0:SEQ], nt[1][:, 0:SEQ]
        qbd, probs, cmat, aT = R["qbd"], R["probs"], s_tmp, rstd
        new_sc, o_rows = hf[0][:, 0:S_TOK], [sg[0][0:S_TOK, 0:512], sg[1][0:S_TOK, 0:512]]

        ps = ctx.enter_context(nc.psum_tensor("ps", [P, 8, 512], F32))
        page_sc = ps[:, 0:2, :].rearrange("p b n -> p (b n)")

        def slot(s):
            return ps[:, 2 * s:2 * s + 2, 0:TH]

        def halves(tile):
            return tile.rearrange("p (a b) -> p a b", a=2)

        def c(name, a=0, b=None):
            at, n = CONST[name]
            return cst[:, at + a:at + (n if b is None else b)]

        def by_seq(ap):
            return ap.rearrange("p (b s) -> p b s", b=DEC_BATCH)

        def seq_cols(tile, first, n, seg=SEG):
            base = tile[:, first:first + (DEC_BATCH - 1) * seg + n]
            return bass.AP(base.tensor, base.offset, [list(base.ap[0]), [seg, DEC_BATCH], [1, n]])

        ident, ones = c("ident"), c("ones")

        sems = {}

        def sem(name):
            if name not in sems:
                sems[name] = ctx.enter_context(nc.semaphore("s_" + name))
            return sems[name]

        for name in ("cst_in", "x_in", "pt_in", "cond_ready", "setup_done", "setup_exp", "setup_step", "raw_full0",
                     "raw_full1", "w_hi", "out0_full", "ada_full0", "ada_full1", "c_split", "os_rows",
                     "ada_hi", "ada_lo", "ada_turned", "sq_full", "sq_sum",
                     "sums_full", "rstd_ready", "ln_ready", "norm_t",
                     "norm_tmp", "norm_hi", "h_hi", "gw_full0", "gw_full1", "rope_swap", "rope_t2",
                     "ph_full0", "ph_full1", "sc_full", "masked", "max_ready",
                     "coef_ready", "att_part", "s_small", "k_full0", "k_full1", *[f"v_full{i}" for i in range(4)],
                     "qbd_zero", "qbd_ready", "smasked", "smax", "snmx", "srs", "so_sq", "so_ln", "state_out",
                     "rg_pad", *CREDITS):
            sem(name)

        def count(name, n):
            return n + CREDITS.get(name, 0)

        def credit(eng, *names):
            for name in names:
                eng.sem_inc(sems[name], CREDITS[name])

        block = ctx.enter_context(nc.Block())

        @block.sync
        def _(sp):
            credit(sp, "k_out0", "k_out1", "v_out0", "v_out1", "out_y0", "out_y1")
            sp.dma_start(cst[:, :], consts).then_inc(sems["cst_in"], 16)

            def ada_load(a, j):
                sp.wait_ge(sems["ada_done"], a - 1 + CREDITS["ada_done"])
                sp.dma_start(ada[j][:, :, :].rearrange("p k n -> p (k n)"), ada_w[a])\
                   .then_inc(sems[f"ada_full{j}"], 16)

            def unit_load(src, row, u, j):
                sp.wait_ge(sems["w_lo"], u - 1 + CREDITS["w_lo"])
                sp.dma_start(raw[j][:, 0:src.shape[-1]], src[row]).then_inc(sems[f"raw_full{j}"], 16)

            for j in range(2):
                ada_load(j, j)
            sp.dma_start(x[:, :, :], xT).then_inc(sems["x_in"], 16)
            sp.dma_start(pt_sb[:, :], page_table).then_inc(sems["pt_in"], 16)
            with sp.Fori(1, ADA_FIRST // 2) as i:
                for j in range(2):
                    ada_load(2 * i + j, j)

            for s in plan:
                u0, a0 = s["u"], s["ada"]
                if s["kind"] == "up" and s["has_ada"] and s["row"] == 0 and u0 > 0:
                    sp.wait_ge(sems["rg_dve"], NRG * KT + CREDITS["rg_dve"])
                if s["units"]:
                    with sp.Fori(s.get("loaded", 0) // 2, s["units"] // 2) as i:
                        for j in range(2):
                            unit_load(s["src"], s["row"] + 2 * i + j, u0 + 2 * i + j, j)
                            if s["kind"] == "up" and s["has_ada"]:
                                ada_load(a0 + 2 * i + j, j)
                            if s["kind"] == "rglru":
                                sp.wait_ge(sems["gates_done"], 2 * i + j - 1 + CREDITS["gates_done"])
                                sp.dma_start(gw[j][:, :], w_gate[2 * i + j]).then_inc(sems[f"gw_full{j}"], 16)
                if s["kind"] == "attention":
                    for j in range(2):
                        unit_load(w_o, j, u0 + j, j)
                    for j in range(2):
                        sp.wait_ge(sems[f"k_out{j}"], 16 * 8 + CREDITS[f"k_out{j}"])
                        sp.wait_ge(sems[f"v_out{j}"], 16 * 8 + CREDITS[f"v_out{j}"])
                    sp.wait_ge(sems["w_done"], u0 + CREDITS["w_done"])
                    sp.dma_start(qs[:, :, :], qT[:, :, SEQ:T].rearrange("h p s -> p h s")).then_inc(sems["s_small"], 16)
                    sp.dma_start(ks[:, :, :], kT_out[:, :, SEQ:T].rearrange("h p s -> p h s"))\
                        .then_inc(sems["s_small"], 16)
                    sp.dma_start(vs[:, :, :], v_sample.rearrange("h s e -> s h e")).then_inc(sems["s_small"], 16)

                    def head_load(h, j):
                        sp.wait_ge(sems["pv_done"], 4 * (h - 1) + CREDITS["pv_done"])
                        f = sems[f"ph_full{j}"]
                        sp.dma_start(qh[j][:, :], qT[h, :, 0:SEQ]).then_inc(f, 16)
                        sp.dma_start(kh[j][:, :], kT_out[h, :, 0:SEQ]).then_inc(f, 16)
                        sp.dma_start(vh[j][:, :, :], v_prompt[h]).then_inc(f, 16)

                    def page_of(b, p, cache):
                        return sp.value_load(pt_sb[0:1, bass.ds(b * N_PAGES + p, 1)], min_val=0,
                                             max_val=cache.shape[0] - 1)

                    def k_load(b, g):
                        pages = [page_of(b, 4 * g + p, k_cache) for p in range(4)]
                        sp.wait_ge(sems["kg_done"], 2 * (b - 1) + g + 1 + CREDITS["kg_done"])
                        for p in range(4):
                            sp.dma_start(kr[g][:, p, :, :], k_cache[bass.ds(pages[p], 1)].rearrange(
                                "o p (h n) -> p (o h) n", h=N_HEADS)).then_inc(sems[f"k_full{g}"], 16)

                    def v_load(b, g):
                        for p in range(4 * g, 4 * g + 4):
                            page = page_of(b, p, v_cache)
                            sp.wait_ge(sems["v_used"], N_PAGES * b + p - 3 + CREDITS["v_used"])
                            sp.dma_start(vr[p % 4][:, :], v_cache[bass.ds(page, 1)].rearrange(
                                "o p n -> p (o n)")).then_inc(sems[f"v_full{p % 4}"], 16)

                    def loads(n, j):
                        for g in range(2):
                            k_load(n + 2, g)
                        v_load(n, 1)
                        v_load(n + 1, 0)
                        head_load(n + 2, j)

                    sp.wait_ge(sems["pt_in"], 16)
                    for g in range(2):
                        k_load(0, g)
                    for j in range(2):
                        head_load(j, j)
                    v_load(0, 0)
                    for g in range(2):
                        k_load(1, g)
                    with sp.Fori(0, (DEC_BATCH - 2) // 2) as i:
                        for j in range(2):
                            loads(2 * i + j, j)
                    v_load(DEC_BATCH - 2, 1)
                    v_load(DEC_BATCH - 1, 0)
                    v_load(DEC_BATCH - 1, 1)
                if s["kind"] == "final":
                    n0 = 8 * s["norm"]
                    with sp.Fori(0, 4) as i:
                        for j in range(2):
                            sp.wait_ge(sems["norm_p"], n0 + 2 * i + j + 1 + CREDITS["norm_p"])
                            sp.dma_start(yT[2 * i + j], hf[j][:, :]).then_inc(sems[f"out_y{j}"], 16)
                    sp.wait_ge(sems["rg_dve"], NRG * 8 + CREDITS["rg_dve"])
                    sp.dma_start(conv_out, conv_sb[:, :, :, :]).then_inc(sems["state_out"], 16)
                    sp.dma_start(h_out, h_sb[:, :, :]).then_inc(sems["state_out"], 16)
                    sp.wait_ge(sems["state_out"], 32)
                    for j in range(2):
                        sp.wait_ge(sems[f"out_y{j}"], 16 * 4 + CREDITS[f"out_y{j}"])

        @block.tensor
        def _(pe):
            credit(pe, "os_picked", "w_done", "ada_done", "gates_done", "v_turned", "tp_done", "pv_done", "kg_done",
                   "v_used", "ss_full", "at_done", "pvs_done", "so_sum")

            def ada_products(a, j):
                pe.wait_ge(sems["ada_lo"], a + 1)
                pe.wait_ge(sems["ada_evac"], a - 1 + CREDITS["ada_evac"])
                for k in range(KT):
                    pe.matmul(ps[0:2 * NC_, 4 + j, 0:256], c_hl[:, k, :], ada_hi[j][:, k, :],
                              start=(k == 0), stop=False)
                    mm = pe.matmul(ps[0:NC_, 4 + j, 0:256], c_hl[:, k, 0:NC_], ada_lo[j][:, k, :],
                                   start=False, stop=(k == KT - 1))
                mm.then_inc(sems["ada_done"], 1)

            def ada_turn(a, j):
                pe.wait_ge(sems["ada_rows"], a + 1 + CREDITS["ada_rows"])
                for t in range(2):
                    mm = pe.matmul(ps[:, 4 + j, 256 + NC_ * t:256 + NC_ * t + NC_],
                                   nt[j][0:2 * NC_, P * t:P * t + P], c("fold")[0:2 * NC_], start=True, stop=True)
                mm.then_inc(sems["ada_turned"], 1)

            def tile_products(j, half_tile, rhs_hi, rhs_lo, s, k_tiles, ready, first, done):
                for k in range(k_tiles):
                    if ready:
                        pe.wait_ge(sems[ready], first + k + 1 + CREDITS[ready])
                    whi = w_hi[j][:, k, P * half_tile:P * half_tile + P]
                    wlo = w_lo[j][:, k, P * half_tile:P * half_tile + P]
                    for n in range(2):
                        for r in (rhs_hi, rhs_lo):
                            pe.matmul(ps[:, 2 * s + n, 0:TH], whi, r[:, k, TH * n:TH * n + TH],
                                      start=(k == 0 and r is rhs_hi), stop=False)
                    for n in range(2):
                        mm = pe.matmul(ps[:, 2 * s + n, 0:TH], wlo, rhs_hi[:, k, TH * n:TH * n + TH],
                                       start=False, stop=(k == k_tiles - 1))
                mm.then_inc(sems[done], 1)

            def unit(u, j, rhs_hi, rhs_lo, k_tiles, ready, first, a=None):
                pe.wait_ge(sems["w_lo"], u + 1 + CREDITS["w_lo"])
                pe.wait_ge(sems["s0_free"], u + CREDITS["s0_free"])
                tile_products(j, 0, rhs_hi, rhs_lo, 0, k_tiles, ready if j == 0 else None, first, "out0_full")
                if a is not None:
                    ada_products(a, j)
                pe.wait_ge(sems["s1_free"], u + CREDITS["s1_free"])
                tile_products(j, 1, rhs_hi, rhs_lo, 1, k_tiles, None, 0, "w_done")
                if a is not None:
                    ada_turn(a, j)

            def column_sums(st):
                pe.wait_ge(sems["sq_sum"], 9 * st + 9)
                for n in range(2):
                    mm = pe.matmul(ps[:, 6 + n, 0:TH], ones, rstd[:, TH * n:TH * n + TH], start=True, stop=True)
                mm.then_inc(sems["sums_full"], 1)

            pe.wait_ge(sems["cst_in"], 16)
            pe.wait_ge(sems["c_split"], 2)
            ada_products(0, 0)
            with pe.Fori(0, ADA_FIRST // 2 - 1) as i:
                for j in range(2):
                    ada_products(2 * i + j + 1, 1 - j)
                    ada_turn(2 * i + j, j)
            ada_products(ADA_FIRST - 1, 1)
            for j in range(2):
                ada_turn(ADA_FIRST - 2 + j, j)

            for s in plan:
                u0, a0, n0 = s["u"], s["ada"], 8 * s["norm"]
                if s["kind"] == "norm" and s["norm"] == 0:
                    column_sums(0)
                if s["kind"] in ("up", "rglru", "kv", "q"):
                    with pe.Fori(0, s["units"] // 2) as i:
                        for j in range(2):
                            u = u0 + 2 * i + j
                            unit(u, j, hh_hi, hh_lo, KT, "norm_lo", n0 - 8,
                                 a0 + 2 * i + j if s["kind"] == "up" and s["has_ada"] else None)
                            if s["kind"] == "rglru":
                                n = 2 * i + j
                                pe.wait_ge(sems[f"gw_full{j}"], 16 * i + 16)
                                pe.wait_ge(sems["rg_dve"], NRG * n + RG["tap3"] + CREDITS["rg_dve"])
                                pe.wait_ge(sems["rg_act"], NRA * (n - 1) + RA["tanh_i"] + CREDITS["rg_act"])
                                for g in range(2):
                                    for q in range(2):
                                        mm = pe.matmul(ps[:, 4 + 2 * g + q, 0:TCH], gw[j][:, P * g:P * g + P],
                                                       xc[:, TCH * q:TCH * q + TCH], start=True, stop=True)
                                mm.then_inc(sems["gates_done"], 1)
                            if s["kind"] == "kv":
                                pe.wait_ge(sems["s1_free"], u + 1 + CREDITS["s1_free"])
                                pe.wait_ge(sems["v_ready"], 2 * i + j + CREDITS["v_ready"])
                                for b in range(4):
                                    pe.transpose(ps[:, 4, P * b:P * b + P], vraw[:, P * b:P * b + P], ident)
                                pe.transpose(ps[0:S_TOK, 5, 0:P], vraw[:, SEQ:T], ident)\
                                    .then_inc(sems["v_turned"], 1)
                if s["kind"] == "down":
                    h_all = s["h"]
                    with pe.Fori(0, s["units"] // 2) as i:
                        for j in range(2):
                            kt = s["k"]
                            unit(u0 + 2 * i + j, j, h_hi, h_lo, kt, "h_lo", h_all - kt)
                    if s["sums"]:
                        column_sums(s["stat"])
                if s["kind"] == "attention":
                    def scores(i, j, t):
                        n = P * (i + 1)
                        pe.wait_ge(sems["p_ready"], t + CREDITS["p_ready"])
                        for m in range(2):
                            rows = slice(64 * m, 64 * m + 64)
                            mm = pe.matmul(ps[:, 4 + m, 0:n], qh[j][rows, P * i:P * i + P], kh[j][rows, 0:n],
                                           start=True, stop=True)
                        mm.then_inc(sems["sc_full"], 1)

                    def turn(n, i, t, more):
                        if i == 0 or (i == 1 and more):
                            pe.wait_ge(sems["smasked"], n + 1 + i)
                        pe.wait_ge(sems["att_ready"], t + 1 + CREDITS["att_ready"])
                        pe.wait_ge(sems["attT_ready"], t + CREDITS["attT_ready"])
                        for b in range(i + 1):
                            mm = pe.transpose(ps[:, 6, P * b:P * b + P], att[:, P * b:P * b + P], ident)
                        mm.then_inc(sems["tp_done"], 1)

                    def weigh(h, i, j, t):
                        pe.wait_ge(sems["attT_ready"], t + 1 + CREDITS["attT_ready"])
                        if i == 0:
                            pe.wait_ge(sems["o_evac"], h + CREDITS["o_evac"])
                        for b in range(i + 1):
                            mm = pe.matmul(ps[:, 7, P * i:P * i + P], vh[j][:, b, :], attT[:, P * b:P * b + P],
                                           start=(b == 0), stop=(b == i))
                        mm.then_inc(sems["pv_done"], 1)

                    def page_scores(b, g):
                        pe.wait_ge(sems["qbd_ready"], 2 * b + 2)
                        pe.wait_ge(sems["sp_ready"], b + CREDITS["sp_ready"])
                        pe.wait_ge(sems[f"k_full{g}"], 64 * b + 64)
                        for h in range(N_HEADS):
                            mm = pe.matmul(ps[:, g, :].rearrange("p (n k) -> p n k", k=PAGE),
                                           qbd[:, P * h:P * h + P], kr[g][:, :, h, :],
                                           start=(h == 0), stop=(h == N_HEADS - 1))
                        mm.then_inc(sems["kg_done"], 1)

                    def new_scores(b, t):
                        pe.wait_ge(sems["attT_ready"], t + CREDITS["attT_ready"])
                        for h in range(N_HEADS):
                            mm = pe.matmul(ps[:, 6, 0:S_TOK], qbd[:, P * h:P * h + P], ks[:, h, :],
                                           start=(h == 0), stop=(h == N_HEADS - 1))
                        mm.then_inc(sems["ss_full"], 1)

                    def sample_turn(b):
                        pe.wait_ge(sems["c_ready"], b + 1 + CREDITS["c_ready"])
                        pe.wait_ge(sems["os_evac"], b + CREDITS["os_evac"])
                        for p in range(N_PAGES):
                            pe.matmul(ps[:, 3, S_TOK * p:S_TOK * p + S_TOK], probs[:, PAGE * p:PAGE * p + PAGE],
                                      cmat, start=True, stop=True)
                        pe.matmul(ps[0:S_TOK, 2, 0:S_TOK], probs[:, PAST_LEN:PAST_LEN + S_TOK], cmat,
                                  start=True, stop=True).then_inc(sems["at_done"], 1)

                    def page_outputs(b, g):
                        if g == 0:
                            pe.wait_ge(sems["at_ready"], b + 1 + CREDITS["at_ready"])
                        for p in range(4 * g, 4 * g + 4):
                            pe.wait_ge(sems[f"v_full{p % 4}"], 32 * b + 16 * g + 16)
                            for q in range(2):
                                mm = pe.matmul(ps[0:S_TOK, 2 + q, :], aT[:, S_TOK * p:S_TOK * p + S_TOK],
                                               vr[p % 4][:, 512 * q:512 * q + 512], start=(p == 0), stop=False)
                            mm.then_inc(sems["v_used"], 1)
                        if g == 1:
                            for q in range(2):
                                mm = pe.matmul(ps[0:S_TOK, 2 + q, :], aT[0:S_TOK, PAST_LEN // 2:PAST_LEN // 2 + S_TOK],
                                               vs[:, 4 * q:4 * q + 4, :].rearrange("s h e -> s (h e)"),
                                               start=False, stop=True)
                            mm.then_inc(sems["pvs_done"], 1)

                    def pick(b):
                        pe.wait_ge(sems["os_rows"], b + 1)
                        for h in range(N_HEADS):
                            mm = pe.matmul(ps[:, 3, 8 * h:8 * h + 8], o_rows[h // 4][:, P * (h % 4):P * (h % 4) + P],
                                           ident[0:S_TOK, 8 * h:8 * h + 8], start=True, stop=True)
                        mm.then_inc(sems["os_picked"], 1)

                    def round_(n, j, more):
                        pe.wait_ge(sems[f"ph_full{j}"], 48 * (n // 2 if isinstance(n, int) else n_half[0]) + 48)
                        for i in range(4):
                            t = 4 * n + i
                            scores(i, j, t)
                            if i == 0 and more:
                                page_scores(n + 1, 0)
                            if i == 1:
                                if more:
                                    page_scores(n + 1, 1)
                                    new_scores(n + 1, t)
                                sample_turn(n)
                            if i >= 2:
                                page_outputs(n, i - 2)
                            turn(n, i, t, more)
                            weigh(n, i, j, t)
                        pick(n)

                    n_half = [0]
                    pe.wait_ge(sems["w_done"], u0 + CREDITS["w_done"])
                    pe.wait_ge(sems["s_small"], 48)
                    for g in range(2):
                        page_scores(0, g)
                    new_scores(0, 0)
                    with pe.Fori(0, (N_HEADS - 2) // 2) as i:
                        n_half[0] = i
                        for j in range(2):
                            round_(2 * i + j, j, True)
                    round_(N_HEADS - 2, 0, True)
                    round_(N_HEADS - 1, 1, False)
                    with pe.Fori(0, 4) as i:
                        for j in range(2):
                            h = 2 * i + j
                            pe.wait_ge(sems["so_sq"], h + 1)
                            pe.wait_ge(sems["so_rs"], h - 1 + CREDITS["so_rs"])
                            for n in range(2):
                                mm = pe.matmul(ps[:, 2 * j + n, 0:TH], ones, sg[j][:, TH * n:TH * n + TH],
                                               start=True, stop=True)
                            mm.then_inc(sems["so_sum"], 1)

        @block.scalar
        def _(act):
            credit(act, "ada_rows", "norm_p", "rg_act", "p_ready", "attT_ready", "sp_ready", "at_ready", "so_rs")

            def split_unit(u, j):
                act.wait_ge(sems[f"raw_full{j}"], 16 * (u[0] + 1))
                act.wait_ge(sems["w_done"], u[1] - 1 + CREDITS["w_done"])
                act.activation(w_hi[j][:, :, :].rearrange("p k n -> p (k n)"), raw[j][:, :], ACT.Copy)\
                   .then_inc(sems["w_hi"], 1)

            def look_ahead(u0, i, j):
                split_unit((u0 // 2 + i + j, u0 + 2 * i + j + 1), 1 - j)

            act.wait_ge(sems["cst_in"], 16)
            act.activation(act_c[:, :, :].rearrange("p k n -> p (k n)"), c("cond"), ACT.Silu)\
               .then_inc(sems["cond_ready"], 1)
            act.wait_ge(sems["cond_ready"], 1)
            act.activation(c_hl[:, :, 0:NC_], act_c[:, :, :], ACT.Copy).then_inc(sems["c_split"], 1)
            act.wait_ge(sems["setup_step"], 5)
            act.activation(setup[0], setup[1], ACT.Exp).then_inc(sems["setup_exp"], 1)
            act.activation(lam4[:, 2:4], lam4[:, 0:2], ACT.Exp).then_inc(sems["setup_exp"], 1)

            def ada_split(a, j, turn):
                act.wait_ge(sems[f"ada_full{j}"], 16 * (turn + 1))
                act.activation(ada_hi[j][:, :, :], ada[j][:, :, :], ACT.Copy).then_inc(sems["ada_hi"], 1)

            def ada_rows(a, j):
                act.wait_ge(sems["ada_done"], a + 1 + CREDITS["ada_done"])
                act.activation(nt[j][0:2 * NC_, 0:256], ps[0:2 * NC_, 4 + j, 0:256], ACT.Copy)\
                   .then_inc(sems["ada_rows"], 1)

            def square(st, k, j):
                act.wait_ge(sems["sq_sum"], 9 * st + k)
                act.activation(sg[j][:, :], x[:, k, :], ACT.Square).then_inc(sems["sq_full"], 1)

            def statistics(st):
                act.wait_ge(sems["sums_full"], st + 1)
                act.activation(halves(rstd[:, :]), ps[:, 6:8, 0:TH], ACT.Ln, scale=1.0 / D_MODEL,
                               bias=eps_x).then_inc(sems["ln_ready"], 1)
                act.wait_ge(sems["ln_ready"], st + 1)
                act.activation(rstd[:, :], rstd[:, :], ACT.Exp, scale=-0.5).then_inc(sems["rstd_ready"], 1)

            act.wait_ge(sems["x_in"], 16)
            act.wait_ge(sems["sq_sum"], 1)
            for k in range(2):
                act.activation(sg[k][:, :], x[:, k, :], ACT.Square).then_inc(sems["sq_full"], 1)
            with act.Fori(1, KT // 2) as i:
                for j in range(2):
                    square(0, 2 * i + j, j)
            ada_split(0, 0, 0)
            ada_split(1, 1, 0)
            ada_rows(0, 0)
            with act.Fori(1, ADA_FIRST // 2) as i:
                for j in range(2):
                    ada_split(2 * i + j, j, i)
                    ada_rows(2 * i + j - 1, 1 - j)
            ada_rows(ADA_FIRST - 1, 1)
            split_unit((0, 0), 0)
            act.wait_ge(sems["setup_done"], 1)
            statistics(0)
            for s in plan:
                u0, h0 = s["u"], s["h"]
                n0 = 8 * s["norm"]
                if s["kind"] == "norm":
                    act.wait_ge(sems["mod_ready"], s["norm"] + 1 + CREDITS["mod_ready"])
                    with act.Fori(0, 4) as i:
                        for j in range(2):
                            k = 2 * i + j
                            act.wait_ge(sems["norm_t"], n0 + k + 1)
                            act.wait_ge(sems["norm_lo"], n0 + k - 1 + CREDITS["norm_lo"])
                            act.activation(hf[j][:, 0:SEQ], nt[j][:, 0:SEQ], ACT.Identity, scale=mod_a[:, k, 0:1],
                                           bias=mods[:, s["sh"] + k, 0:1]).then_inc(sems["norm_p"], 1)
                            act.wait_ge(sems["norm_p"], n0 + k + 1 + CREDITS["norm_p"])
                            act.wait_ge(sems["norm_s"], n0 + k + 1 + CREDITS["norm_s"])
                            act.activation(hh_hi[:, k, :], hf[j][:, :], ACT.Copy).then_inc(sems["norm_hi"], 1)
                if s["kind"] == "up":
                    if s["rope"] == 8 and s["row"] == 0:
                        for j in range(2):
                            act.wait_ge(sems[f"k_out{j}"], 16 * 4 + CREDITS[f"k_out{j}"])
                            act.wait_ge(sems[f"v_out{j}"], 32 * 4 + CREDITS[f"v_out{j}"])
                    with act.Fori(0, s["units"] // 2) as i:
                        for j in range(2):
                            u, h = u0 + 2 * i + j, h0 + 2 * i + j
                            if s["has_ada"]:
                                ada_split(s["ada"] + 2 * i + j, j, s["ada"] // 2 + i)
                            look_ahead(u0, i, j)
                            act.wait_ge(sems["out0_full"], u + 1)
                            act.wait_ge(sems["s1_free"], u - 1 + CREDITS["s1_free"])
                            act.activation(halves(sg[j][:, :]), slot(0), ACT.Silu).then_inc(sems["s0_free"], 1)
                            if s["has_ada"]:
                                ada_rows(s["ada"] + 2 * i + j, j)
                            act.wait_ge(sems["s1_free"], u + 1 + CREDITS["s1_free"])
                            act.activation(h_hi[:, 2 * i + j, :], hf[j][:, :], ACT.Copy).then_inc(sems["h_hi"], 1)
                if s["kind"] == "down":
                    def squares(u, k):
                        act.wait_ge(sems["s0_free"], u + 1 + CREDITS["s0_free"])
                        square(s["stat"], k, 0)
                        act.wait_ge(sems["s1_free"], u + 1 + CREDITS["s1_free"])
                        square(s["stat"], k + 1, 1)

                    if s["last"]:
                        for n in range(s["units"]):
                            if n < s["units"] - 1:
                                look_ahead(u0, n // 2, n % 2)
                            squares(u0 + n, 2 * n)
                    else:
                        with act.Fori(0, s["units"] // 2) as i:
                            for j in range(2):
                                look_ahead(u0, i, j)
                                if s["sums"]:
                                    squares(u0 + 2 * i + j, 4 * i + 2 * j)
                    if s["sums"]:
                        statistics(s["stat"])
                if s["kind"] == "rglru":
                    with act.Fori(0, 4) as i:
                        for j in range(2):
                            u, n = u0 + 2 * i + j, 2 * i + j
                            ra, rg = NRA * n, NRG * n

                            look_ahead(u0, i, j)
                            act.wait_ge(sems["out0_full"], u + 1)
                            act.wait_ge(sems["rg_dve"], NRG * (n - 1) + RG["tap3"] + CREDITS["rg_dve"])
                            act.activation(xp[:, PADS:PADS + TH], ps[:, 0, 0:TH], ACT.Copy)
                            act.activation(xp[:, PADS + TH:S0], ps[:, 1, 0:PB], ACT.Copy)
                            act.activation(seq_cols(xp, S0 + PADS, DEC_SEQ), by_seq(ps[:, 1, PB:TH]), ACT.Copy)\
                               .then_inc(sems["s0_free"], 1)
                            act.wait_ge(sems["w_done"], u + 1 + CREDITS["w_done"])
                            act.wait_ge(sems["s1_free"], u + CREDITS["s1_free"])
                            act.activation(halves(gv[:, 0:T]), slot(1), ACT.Square).then_inc(sems["rg_act"], 1)
                            act.wait_ge(sems["rg_dve"], rg + RG["gelu_arg"] + CREDITS["rg_dve"])
                            act.activation(gt[:, 0:T], gv[:, 0:T], ACT.Tanh, scale=math.sqrt(2.0 / math.pi))\
                               .then_inc(sems["rg_act"], 1)
                            act.wait_ge(sems["gates_done"], n + 1 + CREDITS["gates_done"])
                            act.wait_ge(sems["rg_dve"], NRG * (n - 1) + RG["z_sample"] + CREDITS["rg_dve"])
                            act.activation(halves(th_r[:, :]), ps[:, 4:6, 0:TCH], ACT.Tanh, scale=0.5,
                                           bias=rg_brh[:, bass.ds(n, 1)]).then_inc(sems["rg_act"], 1)
                            act.activation(halves(th_i[:, :]), ps[:, 6:8, 0:TCH], ACT.Tanh, scale=0.5,
                                           bias=rg_bih[:, bass.ds(n, 1)]).then_inc(sems["rg_act"], 1)
                            act.wait_ge(sems["rg_act"], ra + RA["tanh_r"] + CREDITS["rg_act"])
                            act.activation(tau[:, :], th_r[:, :], ACT.Tanh, scale=rg_c4[:, bass.ds(n, 1)],
                                           bias=rg_c4[:, bass.ds(n, 1)]).then_inc(sems["rg_act"], 1)
                            act.activation(dec[:, :], th_r[:, :], ACT.Exp, scale=rg_nc4[:, bass.ds(n, 1)],
                                           bias=rg_nc4[:, bass.ds(n, 1)]).then_inc(sems["rg_act"], 1)
                            act.wait_ge(sems["rg_act"], ra + RA["a"] + CREDITS["rg_act"])
                            act.activation(dec2[:, :], dec[:, :], ACT.Square).then_inc(sems["rg_act"], 1)
                            act.wait_ge(sems["rg_dve"], rg + RG["one_minus_a2"] + CREDITS["rg_dve"])
                            act.activation(dec2[:, :], tau[:, :], ACT.Sqrt).then_inc(sems["rg_act"], 1)
                            act.wait_ge(sems["rg_dve"], rg + RG["z_sample"] + CREDITS["rg_dve"])
                            act.activation(h_hi[:, n, :], hf[j][:, :], ACT.Copy).then_inc(sems["h_hi"], 1)
                if s["kind"] in ("kv", "q"):
                    kv = s["kind"] == "kv"
                    with act.Fori(0, s["units"] // 2) as i:
                        for j in range(2):
                            u = u0 + 2 * i + j
                            look_ahead(u0, i, j)
                            for t in range(1 if kv else 2):
                                r = s["rope"] + (2 * i + j if kv else 4 * i + 2 * j + t)
                                full = "w_done" if t else "out0_full"
                                act.wait_ge(sems[full], count(full, u + 1))
                                act.wait_ge(sems["rope_done"], r + CREDITS["rope_done"])
                                for q in range(4):
                                    cp = act.activation(halves(swapped[32 * q:32 * q + 32, :]),
                                                        ps[32 * (q ^ 1):32 * (q ^ 1) + 32, 2 * t:2 * t + 2, 0:TH],
                                                        ACT.Copy)
                                cp.then_inc(sems["rope_swap"], 1)
                            if kv:
                                act.wait_ge(sems["w_done"], u + 1 + CREDITS["w_done"])
                                act.wait_ge(sems["v_turned"], 2 * i + j + CREDITS["v_turned"])
                                act.activation(halves(vraw[:, :]), slot(1), ACT.Copy).then_inc(sems["s1_free"], 1)
                            for t in range(1 if kv else 2):
                                n, rj = (2 * i + j, j) if kv else (4 * i + 2 * j + t, t)
                                act.wait_ge(sems["rope_done"], s["rope"] + n + 1 + CREDITS["rope_done"])
                                act.dma_start((kT_out if kv else qT)[n], rk[rj][:, :])\
                                   .then_inc(sems[f"k_out{rj}"], 16)
                            if kv:
                                act.wait_ge(sems["v_ready"], 2 * i + j + 1 + CREDITS["v_ready"])
                                act.dma_start(v_prompt[2 * i + j], vt[j][:, :].rearrange("p (b e) -> p b e", e=P))\
                                   .then_inc(sems[f"v_out{j}"], 16)
                                act.dma_start(v_sample[2 * i + j], vts[j][:, :]).then_inc(sems[f"v_out{j}"], 16)
                if s["kind"] == "attention":
                    def exps(i, t):
                        n = P * (i + 1)
                        act.wait_ge(sems["nmx_ready"], t + 1 + CREDITS["nmx_ready"])
                        act.wait_ge(sems["att_ready"], t - 1 + CREDITS["att_ready"])
                        for m in range(2):
                            e = act.activation(pp[i % 2][:, m, 0:n], ps[:, 4 + m, 0:n], ACT.Exp,
                                               bias=nmx[:, m:m + 1], accum_out=sums[i % 2][:, m:m + 1])
                        e.then_inc(sems["p_ready"], 1)

                    def turned(i, t):
                        n = P * (i + 1)
                        act.wait_ge(sems["tp_done"], t + 1 + CREDITS["tp_done"])
                        act.wait_ge(sems["pv_done"], t + CREDITS["pv_done"])
                        act.activation(attT[:, 0:n], ps[:, 6, 0:n], ACT.Copy).then_inc(sems["attT_ready"], 1)

                    def sample_exp(b):
                        act.wait_ge(sems["snmx"], b + 1)
                        act.wait_ge(sems["at_done"], b + CREDITS["at_done"])
                        act.activation(probs[:, 0:PAST_LEN], page_sc, ACT.Exp, bias=nmxs, accum_out=sumss2[:, 0:1])
                        act.activation(probs[:, PAST_LEN:PAST_LEN + S_TOK], new_sc, ACT.Exp, bias=nmxs,
                                       accum_out=sumss2[:, 1:2]).then_inc(sems["sp_ready"], 1)

                    def sample_turned(b):
                        act.wait_ge(sems["at_done"], b + 1 + CREDITS["at_done"])
                        act.wait_ge(sems["pvs_done"], b + CREDITS["pvs_done"])
                        act.activation(aT[:, 0:512], ps[:, 3, :], ACT.Copy)
                        act.activation(aT[0:S_TOK, 512:512 + S_TOK], ps[0:S_TOK, 2, 0:S_TOK], ACT.Copy)\
                           .then_inc(sems["at_ready"], 1)

                    def sample_rows(b):
                        act.wait_ge(sems["pvs_done"], b + 1 + CREDITS["pvs_done"])
                        act.wait_ge(sems["os_picked"], b + CREDITS["os_picked"])
                        act.activation(o_rows[0], ps[0:S_TOK, 2, :], ACT.Copy)
                        act.activation(o_rows[1], ps[0:S_TOK, 3, :], ACT.Copy).then_inc(sems["os_rows"], 1)

                    def round_(n, more):
                        for i in range(4):
                            exps(i, 4 * n + i)
                            if i == 3:
                                if more:
                                    sample_exp(n + 1)
                                sample_rows(n)
                            if i == 1:
                                sample_turned(n)
                            turned(i, 4 * n + i)

                    sample_exp(0)
                    with act.Fori(0, N_HEADS - 1) as n:
                        round_(n, True)
                    round_(N_HEADS - 1, False)
                    act.wait_ge(sems["os_evac"], DEC_BATCH + CREDITS["os_evac"])
                    with act.Fori(0, 4) as i:
                        for j in range(2):
                            h = 2 * i + j
                            act.wait_ge(sems["so_sum"], h - 1 + CREDITS["so_sum"])
                            act.activation(sg[j][:, :], oT[:, h, :], ACT.Square).then_inc(sems["so_sq"], 1)
                            act.wait_ge(sems["so_sum"], h + 1 + CREDITS["so_sum"])
                            act.wait_ge(sems["so_n"], h - 1 + CREDITS["so_n"])
                            act.activation(halves(nt[j][:, :]), ps[:, 2 * j:2 * j + 2, 0:TH], ACT.Ln, scale=1.0 / P,
                                           bias=eps_o).then_inc(sems["so_ln"], 1)
                            act.wait_ge(sems["so_ln"], h + 1)
                            act.activation(nt[j][:, :], nt[j][:, :], ACT.Exp, scale=-0.5).then_inc(sems["so_rs"], 1)
                            act.wait_ge(sems["so_n"], h + 1 + CREDITS["so_n"])
                            act.activation(h_hi[:, h, :], hf[j][:, :], ACT.Copy).then_inc(sems["h_hi"], 1)
                if s["kind"] == "final":
                    with act.Fori(0, 4) as i:
                        for j in range(2):
                            k = 2 * i + j
                            act.wait_ge(sems["norm_t"], n0 + k + 1)
                            act.wait_ge(sems[f"out_y{j}"], 16 * i + CREDITS[f"out_y{j}"])
                            act.activation(hf[j][:, :], nt[j][:, :], ACT.Copy, scale=c("final_g")[:, bass.ds(k, 1)])\
                               .then_inc(sems["norm_p"], 1)

        @block.vector
        def _(dve):
            credit(dve, "w_lo", "s0_free", "s1_free", "ada_evac", "norm_s", "res_tmp", "mod_ready", "rg_dve", "rope_done",
                   "v_ready", "att_ready", "o_evac", "nmx_ready", "c_ready", "os_evac", "so_n")
            dve.wait_ge(sems["c_split"], 1)
            dve.tensor_tensor(c_hl[:, :, NC_:2 * NC_], act_c[:, :, :], c_hl[:, :, 0:NC_].bitcast(F32), ALU.subtract)\
               .then_inc(sems["c_split"], 1)
            dve.memset(eps_x, EPS).then_inc(sems["setup_step"], 1)
            dve.wait_ge(sems["setup_step"], 1)
            dve.wait_ge(sems["cst_in"], 16)
            lam_in = c("lru_lambda")
            dve.tensor_scalar(setup[2], lam_in, -1.0, None, ALU.mult).then_inc(sems["setup_step"], 1)
            dve.wait_ge(sems["setup_step"], 2)
            dve.tensor_tensor(setup[1], setup[2], lam_in, ALU.min).then_inc(sems["setup_step"], 1)
            dve.wait_ge(sems["setup_step"], 3)
            lp = c("lam_p").rearrange("p (a b d) -> p a b d", a=2, b=2)
            dots = sg[0][:, 0:2 * HEAD_DIM].rearrange("p (a d) -> p a d", a=2)
            dve.tensor_tensor(dots, lp[:, :, 0, :], lp[:, :, 1, :], ALU.mult).then_inc(sems["setup_step"], 1)
            dve.wait_ge(sems["setup_step"], 4)
            dve.tensor_reduce(lam4[:, 0:2], dots, AXX, ALU.add).then_inc(sems["setup_step"], 1)
            dve.wait_ge(sems["setup_step"], 5)
            dve.wait_ge(sems["setup_exp"], 2)
            dve.tensor_tensor(lam4[:, 0:1], lam4[:, 3:4], lam4[:, 2:3], ALU.subtract).then_inc(sems["setup_step"], 1)
            dve.wait_ge(sems["setup_step"], 6)
            dve.tensor_scalar(neg_lam, lam4[:, 0:1], -LAM_INIT, None, ALU.add).then_inc(sems["setup_step"], 1)
            dve.wait_ge(sems["setup_step"], 7)
            dve.tensor_scalar(lam4[:, 1:2], neg_lam, -1.0, None, ALU.mult).then_inc(sems["setup_step"], 1)
            dve.wait_ge(sems["setup_step"], 8)
            dve.tensor_tensor(lam4[:, 1:2], lam4[:, 1:2], neg_lam, ALU.max).then_inc(sems["setup_step"], 1)
            dve.wait_ge(sems["setup_step"], 9)
            dve.tensor_scalar(lam4[:, 1:2], lam4[:, 1:2], 1.0, None, ALU.add).then_inc(sems["setup_step"], 1)
            dve.wait_ge(sems["setup_step"], 10)
            dve.reciprocal(map_gain[:, 0:1], lam4[:, 1:2]).then_inc(sems["setup_step"], 1)
            dve.wait_ge(sems["setup_step"], 11)
            dve.tensor_tensor(map_gain[:, 1:2], map_gain[:, 0:1], neg_lam, ALU.mult).then_inc(sems["setup_step"], 1)
            dve.wait_ge(sems["setup_step"], 12)
            dve.tensor_scalar(eps_o, map_gain[:, 0:1], EPS, None, ALU.mult).then_inc(sems["setup_step"], 1)
            dve.wait_ge(sems["setup_step"], 13)
            dve.tensor_tensor(eps_o, eps_o, map_gain[:, 0:1], ALU.mult).then_inc(sems["setup_step"], 1)
            dve.wait_ge(sems["setup_step"], 14)
            dve.tensor_tensor(row_sign, c("map0"), map_gain[:, 0:1], ALU.mult).then_inc(sems["setup_step"], 1)
            dve.wait_ge(sems["setup_step"], 15)
            dve.scalar_tensor_tensor(row_sign, c("map1"), map_gain[:, 1:2], row_sign, ALU.mult, ALU.add)\
               .then_inc(sems["setup_step"], 1)
            dve.wait_ge(sems["setup_step"], 16)
            dve.tensor_scalar(gain_o, c("subln_g"), 1.0 - LAM_INIT, None, ALU.mult).then_inc(sems["setup_step"], 1)
            dve.wait_ge(sems["setup_step"], 17)
            e, z, z2, acc = setup[0], setup[1], setup[3], setup[4]
            dve.tensor_scalar(z, e, 2.0, None, ALU.add).then_inc(sems["setup_step"], 1)
            dve.wait_ge(sems["setup_step"], 18)
            dve.reciprocal(z2, z).then_inc(sems["setup_step"], 1)
            dve.wait_ge(sems["setup_step"], 19)
            dve.tensor_tensor(z, z2, e, ALU.mult).then_inc(sems["setup_step"], 1)
            dve.wait_ge(sems["setup_step"], 20)
            dve.tensor_tensor(z2, z, z, ALU.mult).then_inc(sems["setup_step"], 1)
            dve.wait_ge(sems["setup_step"], 21)
            dve.tensor_scalar(acc, z2, 1.0 / 17, 1.0 / 15, ALU.mult, ALU.add).then_inc(sems["setup_step"], 1)
            dve.wait_ge(sems["setup_step"], 22)
            for i, n in enumerate((13, 11, 9, 7, 5, 3, 1)):
                dve.tensor_tensor(acc, acc, z2, ALU.mult).then_inc(sems["setup_step"], 1)
                dve.wait_ge(sems["setup_step"], 23 + 2 * i)
                dve.tensor_scalar(acc, acc, 1.0 / n, None, ALU.add).then_inc(sems["setup_step"], 1)
                dve.wait_ge(sems["setup_step"], 24 + 2 * i)
            dve.tensor_tensor(acc, acc, z, ALU.mult).then_inc(sems["setup_step"], 1)
            dve.wait_ge(sems["setup_step"], 37)
            dve.tensor_scalar(z, setup[2], 0.0, None, ALU.max).then_inc(sems["setup_step"], 1)
            dve.wait_ge(sems["setup_step"], 38)
            dve.scalar_tensor_tensor(acc, acc, 2.0, z, ALU.mult, ALU.add).then_inc(sems["setup_step"], 1)
            dve.wait_ge(sems["setup_step"], 39)
            dve.tensor_scalar(rg_c4, acc, 4.0, None, ALU.mult).then_inc(sems["setup_step"], 1)
            dve.wait_ge(sems["setup_step"], 40)
            dve.tensor_scalar(rg_nc4, acc, -4.0, None, ALU.mult).then_inc(sems["setup_step"], 1)
            dve.wait_ge(sems["setup_step"], 41)
            dve.tensor_scalar(rg_brh, c("b_rg"), 0.5, None, ALU.mult).then_inc(sems["setup_step"], 1)
            dve.wait_ge(sems["setup_step"], 42)
            dve.tensor_scalar(rg_bih, c("b_ig"), 0.5, None, ALU.mult).then_inc(sems["setup_done"], 1)

            def split_unit(u, j):
                dve.wait_ge(sems["w_hi"], u + 1)
                dve.wait_ge(sems["w_done"], u - 1 + CREDITS["w_done"])
                dve.tensor_tensor(w_lo[j][:, :, :].rearrange("p k n -> p (k n)"), raw[j][:, :],
                                  w_hi[j][:, :, :].rearrange("p k n -> p (k n)").bitcast(F32),
                                  ALU.subtract).then_inc(sems["w_lo"], 1)

            def ada_split(a, j):
                dve.wait_ge(sems["ada_hi"], a + 1)
                dve.tensor_tensor(ada_lo[j][:, :, :], ada[j][:, :, :], ada_hi[j][:, :, :].bitcast(F32),
                                  ALU.subtract).then_inc(sems["ada_lo"], 1)

            def ada_bias(a, j):
                dve.wait_ge(sems["ada_turned"], a + 1)
                dve.tensor_tensor(mods[:, bass.ds(2 * a, 2), :],
                                  ps[:, 4 + j, 256:256 + 2 * NC_].rearrange("p (t n) -> p t n", t=2),
                                  c("ada_b")[:, bass.ds(2 * a, 2)].unsqueeze(2).to_broadcast([P, 2, NC_]),
                                  ALU.add).then_inc(sems["ada_evac"], 1)

            def clear_sums(n0):
                dve.wait_ge(sems["norm_t"], n0)
                dve.memset(rstd[:, :], 0.0).then_inc(sems["sq_sum"], 1)

            def add_square(st, k, j):
                dve.wait_ge(sems["sq_full"], 8 * st + k + 1)
                dve.wait_ge(sems["sq_sum"], 9 * st + k + 1)
                dve.tensor_tensor(rstd[:, :], rstd[:, :], sg[j][:, :], ALU.add).then_inc(sems["sq_sum"], 1)

            dve.memset(rstd[:, :], 0.0).then_inc(sems["sq_sum"], 1)
            with dve.Fori(0, KT // 2) as i:
                for j in range(2):
                    add_square(0, 2 * i + j, j)
            ada_split(0, 0)
            with dve.Fori(0, ADA_FIRST // 2 - 1) as i:
                for j in range(2):
                    ada_split(2 * i + j + 1, 1 - j)
                    ada_bias(2 * i + j, j)
            ada_split(ADA_FIRST - 1, 1)
            for j in range(2):
                ada_bias(ADA_FIRST - 2 + j, j)
            split_unit(0, 0)

            def residual(u, k, t, res):
                dve.wait_ge(sems["w_done" if t else "out0_full"], count("w_done" if t else "out0_full", u + 1))
                dve.scalar_tensor_tensor(x[:, k, 0:TH], ps[:, 2 * t, 0:TH], mod_g[:, k, 0:1], x[:, k, 0:TH],
                                         ALU.mult, ALU.add)
                dve.scalar_tensor_tensor(x[:, k, TH:SEQ], ps[:, 2 * t + 1, 0:PB], mod_g[:, k, 0:1], x[:, k, TH:SEQ],
                                         ALU.mult, ALU.add)
                dve.wait_ge(sems["s0_free" if t else "s1_free"], count("s0_free" if t else "s1_free", u + t))
                dve.tensor_tensor(by_seq(r_tmp), by_seq(ps[:, 2 * t + 1, PB:TH]),
                                  mod_g[:, k, 1:NC_].unsqueeze(2).to_broadcast([P, DEC_BATCH, DEC_SEQ]),
                                  ALU.mult).then_inc(sems["res_tmp"], 1)
                dve.wait_ge(sems["res_tmp"], res + 1 + CREDITS["res_tmp"])
                dve.tensor_tensor(x[:, k, SEQ:T], r_tmp, x[:, k, SEQ:T], ALU.add)\
                   .then_inc(sems["s1_free" if t else "s0_free"], 1)

            def rope(u, t, r, scale, j):
                dve.wait_ge(sems["w_done" if t else "out0_full"], count("w_done" if t else "out0_full", u + 1))
                dve.wait_ge(sems["rope_swap"], r + 1)
                dve.scalar_tensor_tensor(halves(rope_a[:, :]), slot(t), scale, halves(c("cos")), ALU.mult, ALU.mult)\
                   .then_inc(sems["s1_free" if t else "s0_free"], 1)
                dve.scalar_tensor_tensor(rope_b[:, :], swapped[:, :], scale, c("sin"), ALU.mult, ALU.mult)\
                   .then_inc(sems["rope_t2"], 1)
                dve.wait_ge(sems["rope_t2"], r + 1)
                dve.tensor_tensor(rk[j][:, :], rope_a[:, :], rope_b[:, :], ALU.add).then_inc(sems["rope_done"], 1)

            for s in plan:
                u0, h0 = s["u"], s["h"]
                n0 = 8 * s["norm"]
                if s["kind"] in ("norm", "final"):
                    if s["kind"] == "norm":
                        dve.wait_ge(sems["ada_evac"], s["ada"] + CREDITS["ada_evac"])
                        dve.wait_ge(sems["norm_p"], n0 + CREDITS["norm_p"])
                        dve.wait_ge(sems["norm_s"], n0 + CREDITS["norm_s"])
                        dve.wait_ge(sems["s1_free"], u0 + CREDITS["s1_free"])
                        sc = mods[:, s["sc"]:s["sc"] + 8, :]
                        gain = dve.scalar_tensor_tensor(
                            mod_a[:, :, :], sc, 1.0,
                            cst[:, s["g"]:s["g"] + 8].unsqueeze(2).to_broadcast([P, 8, NC_]), ALU.add, ALU.mult)
                        if s["ga"] is None:
                            gain.then_inc(sems["mod_ready"], 1)
                        else:
                            dve.tensor_scalar(mod_g[:, :, :], mods[:, s["ga"]:s["ga"] + 8, :], s["half"], None,
                                              ALU.mult).then_inc(sems["mod_ready"], 1)
                        dve.wait_ge(sems["mod_ready"], s["norm"] + 1 + CREDITS["mod_ready"])
                    dve.wait_ge(sems["h_lo"], h0 + CREDITS["h_lo"])
                    dve.wait_ge(sems["rstd_ready"], s["stat"])
                    with dve.Fori(0, 4) as i:
                        for j in range(2):
                            k = 2 * i + j
                            dve.wait_ge(sems["norm_p"], n0 + k - 1 + CREDITS["norm_p"])
                            if s["kind"] == "norm":
                                dve.wait_ge(sems["norm_s"], n0 + k - 1 + CREDITS["norm_s"])
                            dve.tensor_tensor(nt[j][:, :], x[:, k, :], rstd[:, :], ALU.mult)\
                               .then_inc(sems["norm_t"], 1)
                            if s["kind"] == "norm":
                                dve.wait_ge(sems["norm_t"], n0 + k + 1)
                                dve.wait_ge(sems["norm_s"], n0 + k + CREDITS["norm_s"])
                                dve.tensor_tensor(by_seq(s_tmp), by_seq(nt[j][:, SEQ:T]),
                                                  mod_a[:, k, 1:NC_].unsqueeze(2).to_broadcast([P, DEC_BATCH, DEC_SEQ]),
                                                  ALU.mult).then_inc(sems["norm_tmp"], 1)
                                dve.wait_ge(sems["norm_tmp"], n0 + k + 1)
                                dve.wait_ge(sems["norm_lo"], n0 + k - 1 + CREDITS["norm_lo"])
                                dve.tensor_tensor(by_seq(hf[j][:, SEQ:T]), by_seq(s_tmp),
                                                  mods[:, s["sh"] + k, 1:NC_].unsqueeze(2).to_broadcast(
                                                      [P, DEC_BATCH, DEC_SEQ]),
                                                  ALU.add).then_inc(sems["norm_s"], 1)
                if s["kind"] == "up":
                    with dve.Fori(0, s["units"] // 2) as i:
                        for j in range(2):
                            u, h = u0 + 2 * i + j, h0 + 2 * i + j
                            if s["has_ada"]:
                                ada_split(s["ada"] + 2 * i + j, j)
                            split_unit(u + 1, 1 - j)
                            dve.wait_ge(sems["w_done"], u + 1 + CREDITS["w_done"])
                            dve.wait_ge(sems["s0_free"], u + 1 + CREDITS["s0_free"])
                            dve.wait_ge(sems["h_lo"], h - 1 + CREDITS["h_lo"])
                            dve.tensor_tensor(halves(hf[j][:, :]), halves(sg[j][:, :]), slot(1), ALU.mult)\
                               .then_inc(sems["s1_free"], 1)
                            if s["has_ada"]:
                                ada_bias(s["ada"] + 2 * i + j, j)
                if s["kind"] == "down":
                    if s["sums"]:
                        clear_sums(n0)
                    if s["last"]:
                        for n in range(s["units"]):
                            if n < s["units"] - 1:
                                split_unit(u0 + n + 1, 1 - n % 2)
                            for t in range(2):
                                residual(u0 + n, 2 * n + t, t, s["res"] + 2 * n + t)
                                add_square(s["stat"], 2 * n + t, t)
                    else:
                        with dve.Fori(0, s["units"] // 2) as i:
                            for j in range(2):
                                split_unit(u0 + 2 * i + j + 1, 1 - j)
                                for t in range(2):
                                    n = 4 * i + 2 * j + t
                                    residual(u0 + 2 * i + j, n, t, s["res"] + n)
                                    if s["sums"]:
                                        add_square(s["stat"], n, t)
                if s["kind"] == "rglru":
                    dve.wait_ge(sems["norm_lo"], n0 + CREDITS["norm_lo"])
                    dve.memset(xp[:, 0:PADS], 0.0).then_inc(sems["rg_pad"], 1)
                    dve.wait_ge(sems["rg_pad"], 1)
                    with dve.Fori(0, 4) as i:
                        for j in range(2):
                            u, n = u0 + 2 * i + j, 2 * i + j
                            rg, ra = NRG * n, NRA * n
                            split_unit(u + 1, 1 - j)
                            dve.wait_ge(sems["rg_dve"], rg + CREDITS["rg_dve"])
                            dve.tensor_copy(seq_cols(xp, S0, PADS), c("st_conv")[:, bass.ds(24 * n, 24)].rearrange(
                                "p (b s) -> p b s", b=DEC_BATCH)).then_inc(sems["rg_dve"], 1)
                            dve.wait_ge(sems["s0_free"], u + 1 + CREDITS["s0_free"])
                            dve.tensor_copy(conv_sb[:, n, 0, :], xp[:, SEQ:SEQ + PADS])\
                               .then_inc(sems["rg_dve"], 1)
                            dve.tensor_copy(conv_sb[:, n, 1:NC_, :], seq_cols(xp, S0 + DEC_SEQ, PADS))\
                               .then_inc(sems["rg_dve"], 1)
                            dve.wait_ge(sems["gates_done"], n + CREDITS["gates_done"])
                            dve.wait_ge(sems["rg_dve"], rg + RG["state_in"] + CREDITS["rg_dve"])
                            cw = c("conv_w")
                            dve.tensor_scalar(xc[:, :], xp[:, 0:TC], cw[:, bass.ds(4 * n, 1)],
                                                  c("conv_b")[:, bass.ds(n, 1)], ALU.mult, ALU.add)\
                                                     .then_inc(sems["rg_dve"], 1)
                            for w in range(1, CONV_W):
                                dve.wait_ge(sems["rg_dve"], rg + RG[f"tap{w - 1}"] + CREDITS["rg_dve"])
                                dve.scalar_tensor_tensor(xc[:, :], xp[:, w:w + TC], cw[:, bass.ds(4 * n + w, 1)],
                                                             xc[:, :], ALU.mult, ALU.add)\
                                                                .then_inc(sems["rg_dve"], 1)
                            dve.wait_ge(sems["rg_act"], ra + RA["y2"] + CREDITS["rg_act"])
                            dve.tensor_scalar(gv[:, 0:T], gv[:, 0:T], 0.044715, 1.0, ALU.mult, ALU.add)\
                               .then_inc(sems["rg_dve"], 1)
                            dve.wait_ge(sems["rg_dve"], rg + RG["gelu_poly"] + CREDITS["rg_dve"])
                            dve.tensor_tensor(halves(gv[:, 0:T]), halves(gv[:, 0:T]), slot(1), ALU.mult)\
                               .then_inc(sems["rg_dve"], 1)
                            dve.wait_ge(sems["rg_act"], ra + RA["gelu_tanh"] + CREDITS["rg_act"])
                            dve.scalar_tensor_tensor(halves(gy[:, 0:T]), halves(gt[:, 0:T]), 1.0, slot(1), ALU.add,
                                                     ALU.mult).then_inc(sems["s1_free"], 1)
                            dve.wait_ge(sems["s1_free"], u + 1 + CREDITS["s1_free"])
                            dve.wait_ge(sems["rg_act"], ra + RA["tanh_i"] + CREDITS["rg_act"])
                            dve.scalar_tensor_tensor(xc[:, :], th_i[:, :], 1.0, xc[:, :], ALU.add, ALU.mult)\
                               .then_inc(sems["rg_dve"], 1)
                            dve.wait_ge(sems["rg_act"], ra + RA["a2"] + CREDITS["rg_act"])
                            dve.scalar_tensor_tensor(tau[:, :], dec2[:, :], 1.0, tau[:, :], ALU.add, ALU.mult)\
                               .then_inc(sems["rg_dve"], 1)
                            dve.wait_ge(sems["rg_act"], ra + RA["root"] + CREDITS["rg_act"])
                            dve.wait_ge(sems["rg_dve"], rg + RG["gated_x"] + CREDITS["rg_dve"])
                            dve.scalar_tensor_tensor(xc[:, :], dec2[:, :], 0.5, xc[:, :], ALU.mult, ALU.mult)\
                               .then_inc(sems["rg_dve"], 1)
                            dve.wait_ge(sems["rg_dve"], rg + RG["u"] + CREDITS["rg_dve"])
                            dve.memset(seq_cols(dec, S0 - 1, 1), 0.0).then_inc(sems["rg_dve"], 1)
                            dve.tensor_copy(seq_cols(xc, S0 - 1, 1),
                                                c("st_h")[:, bass.ds(8 * n, 8)].unsqueeze(2))\
                                                   .then_inc(sems["rg_dve"], 1)
                            dve.wait_ge(sems["rg_dve"], rg + RG["reset_u"] + CREDITS["rg_dve"])
                            dve.tensor_tensor_scan(hs[:, :], dec[:, :], xc[:, :], 0.0, ALU.mult, ALU.add)\
                               .then_inc(sems["rg_dve"], 1)
                            dve.wait_ge(sems["rg_dve"], rg + RG["scan"] + CREDITS["rg_dve"])
                            dve.tensor_copy(h_sb[:, n, 0:1], hs[:, SEQ - 1:SEQ])\
                               .then_inc(sems["rg_dve"], 1)
                            dve.tensor_copy(h_sb[:, n, 1:NC_].unsqueeze(2), seq_cols(hs, S0 + DEC_SEQ - 1, 1))\
                               .then_inc(sems["rg_dve"], 1)
                            dve.wait_ge(sems["h_lo"], h0 + n - 1 + CREDITS["h_lo"])
                            dve.scalar_tensor_tensor(hf[j][:, 0:SEQ], hs[:, 0:SEQ], 0.5, gy[:, 0:SEQ], ALU.mult,
                                                         ALU.mult).then_inc(sems["rg_dve"], 1)
                            dve.scalar_tensor_tensor(by_seq(hf[j][:, SEQ:T]), seq_cols(hs, S0, DEC_SEQ), 0.5,
                                                         by_seq(gy[:, SEQ:T]), ALU.mult, ALU.mult)\
                                                            .then_inc(sems["rg_dve"], 1)
                if s["kind"] in ("kv", "q"):
                    kv = s["kind"] == "kv"
                    with dve.Fori(0, s["units"] // 2) as i:
                        for j in range(2):
                            u = u0 + 2 * i + j
                            split_unit(u + 1, 1 - j)
                            for t in range(1 if kv else 2):
                                n = 2 * i + j if kv else 4 * i + 2 * j + t
                                rj = j if kv else t
                                dve.wait_ge(sems[f"k_out{rj}"], 16 * (i if kv else 4 + 2 * i + j) + CREDITS[f"k_out{rj}"])
                                rope(u, t, s["rope"] + n, 1.0 if kv else HEAD_DIM ** -0.5, rj)
                            if kv:
                                dve.wait_ge(sems["v_turned"], 2 * i + j + 1 + CREDITS["v_turned"])
                                dve.wait_ge(sems[f"v_out{j}"], 32 * i + CREDITS[f"v_out{j}"])
                                dve.tensor_copy(vt[j][:, :], ps[:, 4, :])
                                dve.tensor_copy(vts[j][:, :], ps[0:S_TOK, 5, 0:P]).then_inc(sems["v_ready"], 1)
                if s["kind"] == "attention":
                    causal = c("causal").unsqueeze(1).to_broadcast([P, 2, P])

                    def maximum(i, t):
                        n = P * (i + 1)
                        dve.wait_ge(sems["sc_full"], t + 1)
                        dve.tensor_tensor(ps[:, 4:6, P * i:P * i + P], ps[:, 4:6, P * i:P * i + P], causal,
                                          ALU.add).then_inc(sems["masked"], 1)
                        dve.wait_ge(sems["masked"], t + 1)
                        dve.wait_ge(sems["nmx_ready"], t + CREDITS["nmx_ready"])
                        dve.tensor_reduce(mx, ps[:, 4:6, 0:n], AXX, ALU.max).then_inc(sems["max_ready"], 1)
                        dve.wait_ge(sems["max_ready"], t + 1)
                        dve.wait_ge(sems["p_ready"], t + CREDITS["p_ready"])
                        dve.tensor_scalar(nmx, mx, -1.0, None, ALU.mult).then_inc(sems["nmx_ready"], 1)

                    def differ(i, t):
                        n = P * (i + 1)
                        dve.wait_ge(sems["p_ready"], t + 1 + CREDITS["p_ready"])
                        dve.wait_ge(sems["att_ready"], t + CREDITS["att_ready"])
                        dve.reciprocal(rsum, sums[i % 2]).then_inc(sems["coef_ready"], 1)
                        dve.wait_ge(sems["coef_ready"], 2 * t + 1)
                        dve.tensor_tensor(rsum, rsum, map_gain, ALU.mult)\
                           .then_inc(sems["coef_ready"], 1)
                        dve.wait_ge(sems["coef_ready"], 2 * t + 2)
                        dve.wait_ge(sems["tp_done"], t + CREDITS["tp_done"])
                        dve.tensor_scalar(att[:, 0:n], pp[i % 2][:, 0, 0:n], rsum[:, 0:1], None, ALU.mult)\
                           .then_inc(sems["att_part"], 1)
                        dve.wait_ge(sems["att_part"], t + 1)
                        dve.scalar_tensor_tensor(att[:, 0:n], pp[i % 2][:, 1, 0:n], rsum[:, 1:2], att[:, 0:n],
                                                 ALU.mult, ALU.add).then_inc(sems["att_ready"], 1)

                    def head_out(h):
                        dve.wait_ge(sems["pv_done"], 4 * h + 4 + CREDITS["pv_done"])
                        dve.tensor_copy(oT[:, h, 0:SEQ], ps[:, 7, :]).then_inc(sems["o_evac"], 1)

                    def sample_mask(b):
                        dve.wait_ge(sems["ss_full"], b + 1 + CREDITS["ss_full"])
                        dve.wait_ge(sems["sp_ready"], b + CREDITS["sp_ready"])
                        dve.tensor_tensor(new_sc, ps[:, 6, 0:S_TOK], c("smask")[:, bass.ds(S_TOK * b, S_TOK)], ALU.add)\
                           .then_inc(sems["smasked"], 1)

                    def sample_max(b):
                        dve.wait_ge(sems["smasked"], b + 1)
                        dve.tensor_reduce(mxs2[:, 0:1], page_sc, AXX, ALU.max).then_inc(sems["smax"], 1)
                        dve.tensor_reduce(mxs2[:, 1:2], new_sc, AXX, ALU.max).then_inc(sems["smax"], 1)
                        dve.wait_ge(sems["smax"], 3 * b + 2)
                        dve.tensor_tensor(mxs, mxs2[:, 0:1], mxs2[:, 1:2], ALU.max).then_inc(sems["smax"], 1)
                        dve.wait_ge(sems["smax"], 3 * b + 3)
                        dve.tensor_scalar(nmxs, mxs, -1.0, None, ALU.mult).then_inc(sems["snmx"], 1)

                    def sample_coef(b):
                        dve.wait_ge(sems["sp_ready"], b + 1 + CREDITS["sp_ready"])
                        dve.tensor_tensor(sumss, sumss2[:, 0:1], sumss2[:, 1:2], ALU.add).then_inc(sems["srs"], 1)
                        dve.wait_ge(sems["srs"], 3 * b + 1)
                        dve.reciprocal(rss, sumss).then_inc(sems["srs"], 1)
                        dve.wait_ge(sems["srs"], 3 * b + 2)
                        dve.tensor_tensor(coef, rss, row_sign, ALU.mult).then_inc(sems["srs"], 1)
                        dve.wait_ge(sems["srs"], 3 * b + 3)
                        dve.wait_ge(sems["at_done"], b + CREDITS["at_done"])
                        dve.tensor_scalar(cmat, c("comb"), coef, None, ALU.mult).then_inc(sems["c_ready"], 1)

                    def sample_out(b):
                        dve.wait_ge(sems["os_picked"], b + 1 + CREDITS["os_picked"])
                        dve.tensor_copy(oT[:, :, bass.ds(SEQ + DEC_SEQ * b, DEC_SEQ)],
                                        ps[:, 3, 0:S_TOK].rearrange("p (h s) -> p h s", h=N_HEADS))\
                           .then_inc(sems["os_evac"], 1)

                    def round_(n, more):
                        for i in range(4):
                            maximum(i, 4 * n + i)
                            if i == 1 and more:
                                sample_mask(n + 1)
                            differ(i, 4 * n + i)
                            if i == 1 and more:
                                sample_max(n + 1)
                        if more:
                            sample_coef(n + 1)
                        head_out(n)
                        sample_out(n)

                    for j in range(2):
                        dve.wait_ge(sems[f"k_out{j}"], 16 * 8 + CREDITS[f"k_out{j}"])
                    sample_mask(0)
                    sample_max(0)
                    sample_coef(0)
                    with dve.Fori(0, N_HEADS - 1) as n:
                        round_(n, True)
                    round_(N_HEADS - 1, False)
                    with dve.Fori(0, 4) as i:
                        for j in range(2):
                            h = 2 * i + j
                            dve.wait_ge(sems["so_rs"], h + 1 + CREDITS["so_rs"])
                            dve.wait_ge(sems["h_lo"], h0 + h - 1 + CREDITS["h_lo"])
                            dve.scalar_tensor_tensor(hf[j][:, :], oT[:, h, :], gain_o, nt[j][:, :], ALU.mult,
                                                     ALU.mult).then_inc(sems["so_n"], 1)

        @block.gpsimd
        def _(pool):
            credit(pool, "norm_lo", "h_lo")

            def lo_part(j, k, hi, lo, hi_sem, n, lo_sem):
                pool.wait_ge(sems[hi_sem], count(hi_sem, n + 1))
                pool.tensor_tensor(lo[:, k, :], hf[j][:, :], hi[:, k, :].bitcast(F32), ALU.subtract)\
                    .then_inc(sems[lo_sem], 1)

            for s in plan:
                n0, h0 = 8 * s["norm"], s["h"]
                if s["kind"] == "norm":
                    with pool.Fori(0, 4) as i:
                        for j in range(2):
                            lo_part(j, 2 * i + j, hh_hi, hh_lo, "norm_hi", n0 + 2 * i + j, "norm_lo")
                if s["kind"] in ("up", "rglru"):
                    with pool.Fori(0, s["units"] // 2) as i:
                        for j in range(2):
                            lo_part(j, 2 * i + j, h_hi, h_lo, "h_hi", h0 + 2 * i + j, "h_lo")
                if s["kind"] == "attention":
                    pool.wait_ge(sems["s_small"], 48)
                    pool.memset(qbd[:, :], 0.0).then_inc(sems["qbd_zero"], 1)
                    pool.wait_ge(sems["qbd_zero"], 1)
                    with pool.Fori(0, DEC_BATCH) as b:
                        pool.wait_ge(sems["ss_full"], b + CREDITS["ss_full"])
                        for m in range(2):
                            base = qbd[64 * m:64 * m + 64, 8 * m:8 * m + 8]
                            out = bass.AP(base.tensor, base.offset, [list(base.ap[0]), [144, N_HEADS], [1, DEC_SEQ]])
                            pool.tensor_copy(out, qs[64 * m:64 * m + 64, :, bass.ds(DEC_SEQ * b, DEC_SEQ)])\
                                .then_inc(sems["qbd_ready"], 1)
                    with pool.Fori(0, 4) as i:
                        for j in range(2):
                            lo_part(j, 2 * i + j, h_hi, h_lo, "h_hi", h0 + 2 * i + j, "h_lo")


def constants():
    out = {"ident": np.eye(P), "ones": np.ones((P, P)), "causal": np.where(np.arange(P)[None] <= np.arange(P)[:, None], 0, NEG)}
    half = HEAD_DIM // 2
    inv = (1.0 / (np.float32(ROPE_THETA) ** (np.arange(half, dtype=np.float32) * np.float32(2.0 / HEAD_DIM))))
    pos = np.concatenate([np.arange(SEQ), np.tile(PAST_LEN + np.arange(DEC_SEQ), DEC_BATCH)]).astype(np.float32)
    ang = (inv.astype(np.float32)[:, None] * pos[None]).astype(np.float32)
    out["cos"] = np.tile(np.cos(ang), (4, 1))
    out["sin"] = np.tile(np.concatenate([-np.sin(ang), np.sin(ang)]), (2, 1))
    row = np.arange(P)
    h, m, q = row // 16, row // 8 % 2, row % 8
    key = np.arange(S_TOK)
    seen = (key[None, None] // 8 == np.arange(DEC_BATCH)[None, :, None]) & (key[None, None] % 8 <= q[:, None, None])
    out["smask"] = np.where(seen, 0, NEG).reshape(P, -1)
    out["comb"] = key[None] == (8 * h + q)[:, None]
    out["fold"] = (np.arange(NC_)[None] == row[:, None] % NC_) & (row < 2 * NC_)[:, None]
    out["map0"], out["map1"] = (m == 0)[:, None], (m == 1)[:, None]
    return {k: v.astype(np.float32) for k, v in out.items()}


def kernel(**inputs):
    import concourse.bacc as bacc
    from concourse.bass_utils import run_bass_kernel_spmd

    a = {k: np.asarray(v) for k, v in inputs.items()}
    f32 = np.float32

    def rows(v):
        v = v.reshape(-1, KT, P)
        return v.transpose(2, 0, 1).reshape(P, -1)

    def units(w):
        k, n = w.shape
        return np.ascontiguousarray(w.reshape(k // P, P, n // 256, 256).transpose(2, 1, 0, 3)).reshape(n // 256, P, -1)

    def paired(wa, wb):
        k, n = wa.shape
        both = np.stack([w.reshape(k // P, P, n // P, P) for w in (wa, wb)], axis=3)
        return np.ascontiguousarray(both.transpose(2, 1, 0, 3, 4)).reshape(n // P, P, -1)

    k = constants()
    cond = np.concatenate([a["c_prompt"], a["c_sample"]])
    k["cond"] = cond.reshape(NC_, KT, P).transpose(2, 1, 0).reshape(P, -1)
    k["ada_b"] = rows(np.concatenate([a["ada_b"][0], a["kv_ada_b"], a["ada_b"][1]]))
    k["norm_g"], k["kv_g"], k["final_g"] = rows(a["norm_g"]), rows(a["kv_norm_g"]), rows(a["final_g"])
    k["conv_w"] = a["a_conv_w"][0].reshape(CONV_W, KT, P).transpose(2, 1, 0).reshape(P, -1)
    k["conv_b"], k["b_rg"], k["b_ig"] = rows(a["a_conv_b"]), rows(a["a_b_rg"]), rows(a["a_b_ig"])
    k["lru_lambda"] = rows(a["a_lambda"])
    k["subln_g"] = a["b_subln_g"].reshape(P, 1)
    k["lam_p"] = np.broadcast_to(a["b_lambda"].reshape(1, -1), (P, 4 * HEAD_DIM))
    k["st_conv"] = a["state_conv"][0].reshape(DEC_BATCH, PADS, KT, P).transpose(3, 2, 0, 1).reshape(P, -1)
    k["st_h"] = a["state_h"][0].reshape(DEC_BATCH, KT, P).transpose(2, 1, 0).reshape(P, -1)
    consts = np.concatenate([k[name].reshape(P, n) for name, (_, n) in CONST.items()], axis=1)

    tokens = np.concatenate([a["x_prompt"].reshape(SEQ, -1), a["x_sample"].reshape(S_TOK, -1)])
    gu, wd = a["ffn_w_gu"].reshape(4, D_MODEL, 2 * D_FF), a["ffn_w_d"].reshape(4, D_FF, D_MODEL)
    feeds = {
        "consts": consts,
        "xT": tokens.reshape(T, KT, P).transpose(2, 1, 0),
        "page_table": a["page_table"].reshape(1, -1),
        "ada_w": np.concatenate([units(a["ada_w"][0]), units(a["kv_ada_w"]), units(a["ada_w"][1])]),
        "w_gu": np.stack([paired(w[:, :D_FF], w[:, D_FF:]) for w in gu]),
        "w_d8": np.stack([np.stack([units(w[1024 * n:1024 * n + 1024]) for n in range(2)]) for w in wd]),
        "w_d6": np.stack([units(w[2048:]) for w in wd]),
        "w_in": paired(a["a_w_in"][0][:, :D_MODEL], a["a_w_in"][0][:, D_MODEL:]),
        "w_gate": np.concatenate([a["a_w_rg"][0], a["a_w_ig"][0]], axis=2),
        "w_out": units(a["a_w_out"][0]),
        "w_kv": paired(a["w_kv"][:, :D_MODEL], a["w_kv"][:, D_MODEL:]),
        "w_q": units(a["b_w_q"][0]),
        "w_o": units(a["b_w_o"][0]),
        "k_cache": a["cache_k"].transpose(0, 3, 4, 2, 1).reshape(-1, P, N_HEADS * PAGE),
        "v_cache": a["cache_v"].reshape(-1, PAGE, N_HEADS * P),
    }
    outs = {"yT": (KT, P, T), "conv_out": (P, KT, NC_, PADS), "h_out": (P, KT, NC_), "kT_out": (N_HEADS, P, T),
            "v_prompt": (N_HEADS, P, 4, P), "v_sample": (N_HEADS, S_TOK, P)}

    nc = bacc.Bacc("TRN2", target_bir_lowering=False, num_devices=1)
    arrays, args = {}, []
    for name, v in feeds.items():
        v = np.ascontiguousarray(v)
        arrays["in_" + name] = v
        args.append(nc.dram_tensor("in_" + name, v.shape, mybir.dt.from_np(v.dtype), kind="ExternalInput").ap())
    for name, shape in outs.items():
        args.append(nc.dram_tensor("out_" + name, shape, F32, kind="ExternalOutput").ap())
    trunk(nc, *args)
    r = run_bass_kernel_spmd(nc, [arrays], core_ids=[0]).results[0]
    o = {name: r["out_" + name] for name in outs}

    y = o["yT"].reshape(D_MODEL, T).transpose(1, 0)
    conv = o["conv_out"].transpose(2, 3, 1, 0).reshape(NC_, PADS, D_MODEL)
    h = o["h_out"].transpose(2, 1, 0).reshape(NC_, D_MODEL)
    kk = o["kT_out"].transpose(2, 0, 1).reshape(T, N_HEADS, 2, HEAD_DIM)
    vp = o["v_prompt"].transpose(2, 1, 0, 3)
    vs = o["v_sample"].transpose(1, 0, 2)
    got = (y[:SEQ].reshape(1, SEQ, D_MODEL), y[SEQ:].reshape(DEC_BATCH, DEC_SEQ, D_MODEL),
           conv[:1].reshape(1, 1, PADS, D_MODEL), h[:1].reshape(1, 1, D_MODEL),
           kk[:SEQ].reshape(1, SEQ, N_HEADS, 2, HEAD_DIM), vp.reshape(1, SEQ, N_HEADS, P),
           conv[1:].reshape(1, DEC_BATCH, PADS, D_MODEL), h[1:].reshape(1, DEC_BATCH, D_MODEL),
           kk[SEQ:].reshape(DEC_BATCH, DEC_SEQ, N_HEADS, 2, HEAD_DIM), vs.reshape(DEC_BATCH, DEC_SEQ, N_HEADS, P))
    return tuple(np.ascontiguousarray(v) for v in got)
```

```python
from contextlib import ExitStack
import math

import numpy as np
import concourse.bass as bass
from concourse import mybir

F32 = mybir.dt.float32
F32R = mybir.dt.float32r
I32 = mybir.dt.int32
ALU = mybir.AluOpType
ACT = mybir.ActivationFunctionType
AXX = mybir.AxisListType.X

P = 128
D_MODEL = 1024
SEQ = 512
DEC_BATCH = 8
DEC_SEQ = 8
PAST_LEN = 1024
PAGE = 128
N_HEADS = 8
HEAD_DIM = 64
D_FF = 2816
CONV_W = 4
N_ADA = 9
EPS = 1e-6
ROPE_THETA = 10000.0
LAM_INIT = 0.8 - 0.6 * math.exp(-0.3 * 1)
NEG = -1e30

KT = D_MODEL // P
FT = D_FF // P
S_TOK = DEC_BATCH * DEC_SEQ
T = SEQ + S_TOK
TH = T // 2
PB = SEQ - TH
NC_ = 1 + DEC_BATCH
N_PAGES = PAST_LEN // PAGE
PADS = CONV_W - 1
SEG = PADS + DEC_SEQ
TPAD = PADS + SEQ + DEC_BATCH * SEG
TC = TPAD - PADS
TCH = TC // 2
S0 = SEQ + PADS
UNIT = 8 * 256
CHUNKS = (8, 8, 6)
ADA_FIRST = 14
ADA_TILES = N_ADA * KT
KV_TILE0 = ADA_TILES
L1_TILE0 = ADA_TILES + 2 * KT
N_MOD_TILES = 2 * ADA_TILES + 2 * KT

CONST = {}
_at = 0
for _name, _n in (("ident", P), ("ones", P), ("cond", KT * NC_), ("ada_b", N_MOD_TILES), ("norm_g", 6 * KT),
                  ("kv_g", KT), ("final_g", KT), ("conv_w", KT * CONV_W), ("conv_b", KT), ("b_rg", KT), ("b_ig", KT),
                  ("lru_lambda", KT), ("subln_g", 1), ("lam_p", 4 * HEAD_DIM), ("st_conv", KT * DEC_BATCH * PADS),
                  ("st_h", KT * DEC_BATCH), ("cos", T), ("sin", T), ("causal", P), ("smask", DEC_BATCH * S_TOK),
                  ("comb", S_TOK), ("map0", 1), ("map1", 1), ("fold", NC_)):
    CONST[_name] = (_at, _n)
    _at += _n
N_CONST = _at

CV = {n: i + 1 for i, n in enumerate(
    ("state_in", "conv_prompt_out", "conv_sample_out", "tap0", "tap1", "tap2", "tap3", "gelu_poly", "gelu_arg"))}
SC = {n: i + 1 for i, n in enumerate(
    ("gated_x", "one_minus_a2", "u", "reset_a", "reset_u", "scan", "h_prompt", "h_sample", "z_prompt", "z_sample"))}
NCV, NSC = len(CV), len(SC)
GE = {n: i + 1 for i, n in enumerate(("y2", "gelu_tanh"))}
GA = {n: i + 1 for i, n in enumerate(("tanh_r", "tanh_i", "tau", "a", "a2", "root"))}
NGE, NGA = len(GE), len(GA)

CREDITS = {"k_out0": 16, "k_out1": 16, "v_out0": 16, "v_out1": 16, "w_done": 2, "w_lo": 2, "s0_free": 2,
           "s1_free": 2, "ada_done": 2, "ada_rows": 2, "ada_evac": 2,
           "norm_p": 2, "norm_s": 2, "norm_lo": 4, "res_tmp": 1, "h_lo": 2, "mod_ready": 1,
           "rg_conv": NCV, "rg_scan": 2 * NSC, "rg_gate": NGA, "gates_done": 2, "rope_done": 2, "v_turned": 1,
           "v_ready": 2, "p_ready": 1, "att_ready": 2, "tp_done": 1, "attT_ready": 1, "pv_done": 8, "o_evac": 1,
           "nmx_ready": 1, "kg_done": 2, "v_used": 4, "ss_full": 1, "sp_ready": 1, "c_ready": 1, "at_done": 1,
           "at_ready": 1, "pvs_done": 1, "os_picked": 1, "os_evac": 1, "out_y0": 16, "out_y1": 16}


def trunk(nc, consts, xT, page_table, ada_w, w_gu, w_d8, w_d6, w_in, w_gate, w_out, w_kv, w_q, w_o, k_cache, v_cache,
          yT, conv_out, h_out, kT_out, v_prompt, v_sample):
    qT = nc.dram_tensor("qT", [N_HEADS, P, T], F32, kind="Internal").ap()

    plan = []
    count = {"u": 0, "ada": ADA_FIRST, "norm": 0, "stat": 1, "h": 0, "res": 0, "rope": 0}

    def stage(kind, units=0, **more):
        plan.append({"kind": kind, "units": units, **count, **more})
        count["u"] += units

    def norm(**more):
        stage("norm", **more)
        count["norm"] += 1

    def down(**more):
        stage("down", 4, row=0, **more)
        count["res"] += 8
        if more["sums"]:
            count["stat"] += 1

    def ffn(layer, which):
        tile0 = L1_TILE0 * layer
        chunk0 = 6 * which
        norm(sh=tile0 + 8 * chunk0, sc=tile0 + 8 * chunk0 + 8, ga=tile0 + 8 * chunk0 + 16,
             g=CONST["norm_g"][0] + 8 * (3 * layer + 2 * which), half=0.5)
        first = 0
        for c, tiles in enumerate(CHUNKS):
            has_ada = not (layer == 1 and which == 1)
            stage("up", tiles, src=w_gu[2 * layer + which], row=first, has_ada=has_ada)
            count["h"] += tiles
            count["ada"] += tiles if has_ada else 0
            first += tiles
            src = w_d8[2 * layer + which, c] if tiles == 8 else w_d6[2 * layer + which]
            down(src=src, k=tiles, sums=(c == len(CHUNKS) - 1), last=(layer == 1 and which == 1 and c == 2))

    def mixer_norm(tile0, g, gate):
        norm(sh=tile0, sc=tile0 + 8, ga=tile0 + 16 if gate else None, g=g, half=1.0)

    ffn(0, 0)
    mixer_norm(24, CONST["norm_g"][0] + 8, True)
    stage("rglru", 8, src=w_in, row=0)
    count["h"] += 8
    down(src=w_out, k=8, sums=True, last=False)
    ffn(0, 1)
    mixer_norm(KV_TILE0, CONST["kv_g"][0], False)
    stage("kv", 8, src=w_kv, row=0)
    count["rope"] += 8
    ffn(1, 0)
    mixer_norm(L1_TILE0 + 24, CONST["norm_g"][0] + 8 * 4, True)
    stage("q", 4, src=w_q, row=0)
    count["rope"] += 8
    stage("attention")
    count["h"] += 8
    down(src=w_o, k=8, sums=True, last=False, loaded=2)
    ffn(1, 1)
    stage("final")
    assert count["ada"] * 2 == N_MOD_TILES

    with ExitStack() as ctx:
        def sb(name, shape, dt=F32, where=None):
            return (where or ctx).enter_context(nc.sbuf_tensor(name, shape, dt))

        cst = sb("cst", [P, N_CONST])
        x = sb("x", [P, KT, T])
        raw = [sb(f"raw{j}", [P, UNIT]) for j in range(2)]
        w_hi = [sb(f"w_hi{j}", [P, 8, 256], F32R) for j in range(2)]
        w_lo = [sb(f"w_lo{j}", [P, 8, 256], F32R) for j in range(2)]
        mods = sb("mods", [P, N_MOD_TILES, NC_])
        act_c = sb("act_c", [P, KT, NC_])
        c_hl = sb("c_hl", [P, KT, 2 * NC_], F32R)
        mod_a = sb("mod_a", [P, KT, NC_])
        mod_g = sb("mod_g", [P, KT, NC_])
        sg = [sb(f"sg{j}", [P, T]) for j in range(2)]
        hf = [sb(f"hf{j}", [P, T]) for j in range(2)]
        nt = [sb(f"nt{j}", [P, T]) for j in range(2)]
        mt = [*hf, *sg]
        rstd = sb("rstd", [P, T])
        small = sb("small", [P, 256])
        s_tmp = small[:, 0:S_TOK]
        r_tmp = small[:, S_TOK:2 * S_TOK]
        m_tmp = [s_tmp, r_tmp]
        rg_c4 = small[:, 128:136]
        rg_nc4 = small[:, 136:144]
        rg_brh = small[:, 144:152]
        rg_bih = small[:, 152:160]
        neg_lam = small[:, 160:161]
        map_gain = small[:, 241:243]
        eps_x = small[:, 240:241]
        eps_o = small[:, 243:244]
        row_sign = small[:, 161:162]
        gain_o = small[:, 162:163]
        mx = small[:, 164:166]
        nmx = small[:, 166:168]
        sums = [small[:, 168:170], small[:, 170:172]]
        rsum = small[:, 172:174]
        mxs = small[:, 174:175]
        nmxs = small[:, 175:176]
        sumss = small[:, 176:177]
        mxs2 = small[:, 244:246]
        sumss2 = small[:, 246:248]
        rss = small[:, 177:178]
        coef = small[:, 178:179]
        setup = [small[:, 180 + 8 * i:188 + 8 * i] for i in range(6)]
        lam4 = small[:, 228:232]
        pt_sb = sb("pt_sb", [1, DEC_BATCH * N_PAGES], I32)
        conv_sb = sb("conv_sb", [P, KT, NC_, PADS])
        h_sb = sb("h_sb", [P, KT, NC_])

        region = {}

        def laid(key, below, *tensors):
            with ExitStack() as part:
                if below:
                    sb("below_" + key, [P, below], F32, part)
                for name, shape, dt in tensors:
                    region[name] = sb(name, shape, dt, part)

        hh = KT * T
        laid("linear", 0, ("hh_hi", [P, KT, T], F32R), ("hh_lo", [P, KT, T], F32R),
             ("h_hi", [P, KT, T], F32R), ("h_lo", [P, KT, T], F32R),
             ("ada0", [P, KT, 256], F32), ("ada1", [P, KT, 256], F32),
             ("ada_hi0", [P, KT, 256], F32R), ("ada_hi1", [P, KT, 256], F32R))
        laid("ada_first", 2 * hh, *[(f"pro{j}", [P, KT, 256], F32) for j in range(4)])
        laid("ada_lo", 4 * hh, ("ada_lo0", [P, KT, 256], F32R), ("ada_lo1", [P, KT, 256], F32R))
        laid("rglru", 4 * hh, *[(n, [P, TPAD if n == "xp" else TC], F32) for n in
                                ("xp", "xc0", "xc1", "th_r", "th_i", "tau", "a", "a2", "hs", "gv", "gt", "gy0",
                                 "gy1")],
             ("gw0", [P, 256], F32), ("gw1", [P, 256], F32))
        laid("rope", 4 * hh + 2 * UNIT, ("swapped", [P, T], F32), ("rope_a", [P, T], F32),
             ("rope_b", [P, T], F32))
        laid("rope_out", 2 * hh, ("rk0", [P, T], F32), ("rk1", [P, T], F32), ("vraw", [P, T], F32),
             ("vt0", [P, SEQ], F32), ("vt1", [P, SEQ], F32), ("vts0", [S_TOK, P], F32), ("vts1", [S_TOK, P], F32))
        laid("attention", 0, ("kr0", [P, 4, N_HEADS, PAGE], F32), ("kr1", [P, 4, N_HEADS, PAGE], F32),
             *[(f"vr{i}", [P, N_HEADS * P], F32) for i in range(4)],
             ("qs", [P, N_HEADS, S_TOK], F32), ("ks", [P, N_HEADS, S_TOK], F32),
             ("vs", [S_TOK, N_HEADS, P], F32))
        att0 = 8192 + 4096 + 2 * N_HEADS * S_TOK + N_HEADS * P
        laid("att_prompt", att0, ("qh0", [P, SEQ], F32), ("qh1", [P, SEQ], F32), ("kh0", [P, SEQ], F32),
             ("kh1", [P, SEQ], F32), ("vh0", [P, 4, P], F32), ("vh1", [P, 4, P], F32), ("pp0", [P, 2, SEQ], F32),
             ("pp1", [P, 2, SEQ], F32), ("oT", [P, N_HEADS, T], F32), ("qbd", [P, N_HEADS * 144], F32),
             ("probs", [P, PAST_LEN + S_TOK], F32))
        laid("subln", 0, *[(f"sq{j}", [P, T], F32) for j in range(4)],
             *[(f"rs{j}", [P, T], F32) for j in range(N_HEADS)])
        R = region
        hh_hi, hh_lo, h_hi, h_lo = R["hh_hi"], R["hh_lo"], R["h_hi"], R["h_lo"]
        pro = [R[f"pro{j}"] for j in range(4)]
        ada, ada_hi, ada_lo = ([R[f"{name}{j}"] for j in range(2)] for name in ("ada", "ada_hi", "ada_lo"))
        xp, xc, th_r, th_i = R["xp"], [R["xc0"], R["xc1"]], R["th_r"], R["th_i"]
        tau, dec, dec2, hs, gv, gt, gy = R["tau"], R["a"], R["a2"], R["hs"], R["gv"], R["gt"], [R["gy0"], R["gy1"]]
        gw = [R["gw0"], R["gw1"]]
        swapped, rope_a, rope_b = R["swapped"], R["rope_a"], R["rope_b"]
        rk, vraw, vt, vts = [R["rk0"], R["rk1"]], R["vraw"], [R["vt0"], R["vt1"]], [R["vts0"], R["vts1"]]
        kr, vr = [R["kr0"], R["kr1"]], [R[f"vr{i}"] for i in range(4)]
        oT, qs, ks, vs = R["oT"], R["qs"], R["ks"], R["vs"]
        qh, kh, vh = [R["qh0"], R["qh1"]], [R["kh0"], R["kh1"]], [R["vh0"], R["vh1"]]
        pp, att, attT = [R["pp0"], R["pp1"]], nt[0][:, 0:SEQ], nt[1][:, 0:SEQ]
        sq, rs = [R[f"sq{j}"] for j in range(4)], [R[f"rs{j}"] for j in range(N_HEADS)]
        qbd, probs, cmat, aT = R["qbd"], R["probs"], s_tmp, rstd
        new_sc, o_rows = hf[0][:, 0:S_TOK], [sg[0][0:S_TOK, 0:512], sg[1][0:S_TOK, 0:512]]

        ps = ctx.enter_context(nc.psum_tensor("ps", [P, 8, 512], F32))
        page_sc = ps[:, 0:2, :].rearrange("p b n -> p (b n)")

        def slot(s):
            return ps[:, 2 * s:2 * s + 2, 0:TH]

        def halves(tile):
            return tile.rearrange("p (a b) -> p a b", a=2)

        def c(name, a=0, b=None):
            at, n = CONST[name]
            return cst[:, at + a:at + (n if b is None else b)]

        def by_seq(ap):
            return ap.rearrange("p (b s) -> p b s", b=DEC_BATCH)

        def seq_cols(tile, first, n, seg=SEG):
            base = tile[:, first:first + (DEC_BATCH - 1) * seg + n]
            return bass.AP(base.tensor, base.offset, [list(base.ap[0]), [seg, DEC_BATCH], [1, n]])

        ident, ones = c("ident"), c("ones")

        sems = {}

        def sem(name):
            if name not in sems:
                sems[name] = ctx.enter_context(nc.semaphore("s_" + name))
            return sems[name]

        for name in ("cst_in", "x_in", "pt_in", "cond_ready", "setup_done", "setup_exp", "setup_step", "raw_full0",
                     "raw_full1", "w_hi", "out0_full", "ada_full0", "ada_full1", *[f"pro_full{j}" for j in range(4)],
                     "c_split", "os_rows", "rg_gelu",
                     "ada_hi", "ada_lo", "ada_turned", "sq_full", "sq_sum",
                     "sums_full", "rstd_ready", "ln_ready", "norm_t",
                     "norm_tmp", "norm_hi", "h_hi", "gw_full0", "gw_full1", "rope_swap", "rope_t2",
                     "ph_full0", "ph_full1", "sc_full", "masked", "max_ready",
                     "coef_ready", "att_part", "s_small", "k_full0", "k_full1", *[f"v_full{i}" for i in range(4)],
                     "qbd_zero", "qbd_ready", "smasked", "smax", "snmx", "srs", "so_sq", "so_ln", "so_sum",
                     "so_rs", "so_n", "qs_in", "state_out",
                     "rg_pad", *CREDITS):
            sem(name)

        def count(name, n):
            return n + CREDITS.get(name, 0)

        def credit(eng, *names):
            for name in names:
                eng.sem_inc(sems[name], CREDITS[name])

        block = ctx.enter_context(nc.Block())

        @block.sync
        def _(sp):
            credit(sp, "k_out0", "k_out1", "v_out0", "v_out1", "out_y0", "out_y1")
            sp.dma_start(cst[:, :], consts).then_inc(sems["cst_in"], 16)

            def ada_load(a, j):
                sp.wait_ge(sems["ada_done"], a - 1 + CREDITS["ada_done"])
                sp.dma_start(ada[j][:, :, :].rearrange("p k n -> p (k n)"), ada_w[a])\
                   .then_inc(sems[f"ada_full{j}"], 16)

            def unit_load(src, row, u, j):
                sp.wait_ge(sems["w_lo"], u - 1 + CREDITS["w_lo"])
                sp.dma_start(raw[j][:, 0:src.shape[-1]], src[row]).then_inc(sems[f"raw_full{j}"], 16)

            def first_load(a, j):
                sp.dma_start(pro[j][:, :, :].rearrange("p k n -> p (k n)"), ada_w[a]).then_inc(sems[f"pro_full{j}"], 16)

            for j in range(4):
                first_load(j, j)
            sp.dma_start(x[:, :, :], xT).then_inc(sems["x_in"], 16)
            sp.dma_start(pt_sb[:, :], page_table).then_inc(sems["pt_in"], 16)
            with sp.Fori(1, ADA_FIRST // 4) as i:
                for j in range(4):
                    sp.wait_ge(sems["ada_lo"], 4 * i + j - 3)
                    first_load(4 * i + j, j)
            for a in range(ADA_FIRST // 4 * 4, ADA_FIRST):
                sp.wait_ge(sems["ada_lo"], a - 3)
                first_load(a, a % 4)

            for s in plan:
                u0, a0 = s["u"], s["ada"]
                if s["kind"] == "up" and s["has_ada"] and s["row"] == 0 and u0 > 0:
                    sp.wait_ge(sems["rg_scan"], NSC * KT + CREDITS["rg_scan"])
                if s["units"]:
                    with sp.Fori(s.get("loaded", 0) // 2, s["units"] // 2) as i:
                        for j in range(2):
                            unit_load(s["src"], s["row"] + 2 * i + j, u0 + 2 * i + j, j)
                            if s["kind"] == "up" and s["has_ada"]:
                                ada_load(a0 + 2 * i + j, j)
                            if s["kind"] == "rglru":
                                sp.wait_ge(sems["gates_done"], 2 * i + j - 1 + CREDITS["gates_done"])
                                sp.dma_start(gw[j][:, :], w_gate[2 * i + j]).then_inc(sems[f"gw_full{j}"], 16)
                if s["kind"] == "attention":
                    for j in range(2):
                        unit_load(w_o, j, u0 + j, j)
                    def head_load(h, j):
                        sp.wait_ge(sems["pv_done"], 4 * (h - 1) + CREDITS["pv_done"])
                        f = sems[f"ph_full{j}"]
                        sp.dma_start(qh[j][:, :], qT[h, :, 0:SEQ]).then_inc(f, 16)
                        sp.dma_start(kh[j][:, :], kT_out[h, :, 0:SEQ]).then_inc(f, 16)
                        sp.dma_start(vh[j][:, :, :], v_prompt[h]).then_inc(f, 16)

                    def page_of(b, p, cache):
                        return sp.value_load(pt_sb[0:1, bass.ds(b * N_PAGES + p, 1)], min_val=0,
                                             max_val=cache.shape[0] - 1)

                    def k_load(b, g):
                        pages = [page_of(b, 4 * g + p, k_cache) for p in range(4)]
                        sp.wait_ge(sems["kg_done"], 2 * (b - 1) + g + 1 + CREDITS["kg_done"])
                        for p in range(4):
                            sp.dma_start(kr[g][:, p, :, :], k_cache[bass.ds(pages[p], 1)].rearrange(
                                "o p (h n) -> p (o h) n", h=N_HEADS)).then_inc(sems[f"k_full{g}"], 16)

                    def v_load(b, g):
                        for p in range(4 * g, 4 * g + 4):
                            page = page_of(b, p, v_cache)
                            sp.wait_ge(sems["v_used"], N_PAGES * b + p - 3 + CREDITS["v_used"])
                            sp.dma_start(vr[p % 4][:, :], v_cache[bass.ds(page, 1)].rearrange(
                                "o p n -> p (o n)")).then_inc(sems[f"v_full{p % 4}"], 16)

                    def loads(n, j):
                        for g in range(2):
                            k_load(n + 2, g)
                        v_load(n, 1)
                        v_load(n + 1, 0)
                        head_load(n + 2, j)

                    sp.wait_ge(sems["pt_in"], 16)
                    sp.wait_ge(sems["w_done"], u0 + CREDITS["w_done"])
                    k_load(0, 0)
                    for j in range(2):
                        sp.wait_ge(sems[f"k_out{j}"], 16 * 8 + CREDITS[f"k_out{j}"])
                        sp.wait_ge(sems[f"v_out{j}"], 16 * 8 + CREDITS[f"v_out{j}"])
                    sp.dma_start(qs[:, :, :], qT[:, :, SEQ:T].rearrange("h p s -> p h s")).then_inc(sems["qs_in"], 16)
                    sp.dma_start(ks[:, :, :], kT_out[:, :, SEQ:T].rearrange("h p s -> p h s"))\
                        .then_inc(sems["s_small"], 16)
                    sp.dma_start(vs[:, :, :], v_sample.rearrange("h s e -> s h e")).then_inc(sems["s_small"], 16)
                    k_load(0, 1)
                    for j in range(2):
                        head_load(j, j)
                    v_load(0, 0)
                    for g in range(2):
                        k_load(1, g)
                    with sp.Fori(0, (DEC_BATCH - 2) // 2) as i:
                        for j in range(2):
                            loads(2 * i + j, j)
                    v_load(DEC_BATCH - 2, 1)
                    v_load(DEC_BATCH - 1, 0)
                    v_load(DEC_BATCH - 1, 1)
                if s["kind"] == "final":
                    n0 = 8 * s["norm"]
                    with sp.Fori(0, 4) as i:
                        for j in range(2):
                            sp.wait_ge(sems["norm_p"], n0 + 2 * i + j + 1 + CREDITS["norm_p"])
                            sp.dma_start(yT[2 * i + j], hf[j][:, :]).then_inc(sems[f"out_y{j}"], 16)
                    sp.wait_ge(sems["rg_conv"], NCV * KT + CREDITS["rg_conv"])
                    sp.wait_ge(sems["rg_scan"], NSC * KT + CREDITS["rg_scan"])
                    sp.dma_start(conv_out, conv_sb[:, :, :, :]).then_inc(sems["state_out"], 16)
                    sp.dma_start(h_out, h_sb[:, :, :]).then_inc(sems["state_out"], 16)
                    sp.wait_ge(sems["state_out"], 32)
                    for j in range(2):
                        sp.wait_ge(sems[f"out_y{j}"], 16 * 4 + CREDITS[f"out_y{j}"])

        @block.tensor
        def _(pe):
            credit(pe, "os_picked", "w_done", "ada_done", "gates_done", "v_turned", "tp_done", "pv_done", "kg_done",
                   "v_used", "ss_full", "at_done", "pvs_done")

            def ada_products(a, j):
                pe.wait_ge(sems["ada_lo"], a + 1)
                pe.wait_ge(sems["ada_evac"], a - 1 + CREDITS["ada_evac"])
                for k in range(KT):
                    pe.matmul(ps[0:2 * NC_, 4 + j, 0:256], c_hl[:, k, :], ada_hi[j][:, k, :],
                              start=(k == 0), stop=False)
                    mm = pe.matmul(ps[0:NC_, 4 + j, 0:256], c_hl[:, k, 0:NC_], ada_lo[j][:, k, :],
                                   start=False, stop=(k == KT - 1))
                mm.then_inc(sems["ada_done"], 1)

            def ada_turn(a, j):
                pe.wait_ge(sems["ada_rows"], a + 1 + CREDITS["ada_rows"])
                for t in range(2):
                    mm = pe.matmul(ps[:, 4 + j, 256 + NC_ * t:256 + NC_ * t + NC_],
                                   nt[j][0:2 * NC_, P * t:P * t + P], c("fold")[0:2 * NC_], start=True, stop=True)
                mm.then_inc(sems["ada_turned"], 1)

            def tile_products(j, half_tile, rhs_hi, rhs_lo, s, k_tiles, ready, first, done):
                for k in range(k_tiles):
                    if ready:
                        pe.wait_ge(sems[ready], first + k + 1 + CREDITS[ready])
                    whi = w_hi[j][:, k, P * half_tile:P * half_tile + P]
                    wlo = w_lo[j][:, k, P * half_tile:P * half_tile + P]
                    for n in range(2):
                        for r in (rhs_hi, rhs_lo):
                            pe.matmul(ps[:, 2 * s + n, 0:TH], whi, r[:, k, TH * n:TH * n + TH],
                                      start=(k == 0 and r is rhs_hi), stop=False)
                    for n in range(2):
                        mm = pe.matmul(ps[:, 2 * s + n, 0:TH], wlo, rhs_hi[:, k, TH * n:TH * n + TH],
                                       start=False, stop=(k == k_tiles - 1))
                mm.then_inc(sems[done], 1)

            def unit(u, j, rhs_hi, rhs_lo, k_tiles, ready, first, a=None, between=None):
                pe.wait_ge(sems["w_lo"], u + 1 + CREDITS["w_lo"])
                pe.wait_ge(sems["s0_free"], u + CREDITS["s0_free"])
                tile_products(j, 0, rhs_hi, rhs_lo, 0, k_tiles, ready if j == 0 else None, first, "out0_full")
                if a is not None:
                    ada_products(a, j)
                if between:
                    between()
                pe.wait_ge(sems["s1_free"], u + CREDITS["s1_free"])
                tile_products(j, 1, rhs_hi, rhs_lo, 1, k_tiles, None, 0, "w_done")
                if a is not None:
                    ada_turn(a, j)

            def column_sums(st):
                pe.wait_ge(sems["sq_sum"], 9 * st + 9)
                for n in range(2):
                    mm = pe.matmul(ps[:, 6 + n, 0:TH], ones, rstd[:, TH * n:TH * n + TH], start=True, stop=True)
                mm.then_inc(sems["sums_full"], 1)

            pe.wait_ge(sems["cst_in"], 16)
            pe.wait_ge(sems["c_split"], 2)
            with pe.Fori(0, ADA_FIRST // 2) as i:
                for j in range(2):
                    ada_products(2 * i + j, j)
                    ada_turn(2 * i + j, j)

            for s in plan:
                u0, a0, n0 = s["u"], s["ada"], 8 * s["norm"]
                if s["kind"] == "norm" and s["norm"] == 0:
                    column_sums(0)
                if s["kind"] == "rglru":
                    def gates(n, j, i):
                        pe.wait_ge(sems[f"gw_full{j}"], 16 * i + 16)
                        pe.wait_ge(sems["rg_conv"], NCV * n + CV["tap3"] + CREDITS["rg_conv"])
                        pe.wait_ge(sems["rg_gate"], NGA * (n - 1) + GA["tanh_i"] + CREDITS["rg_gate"])
                        for g in range(2):
                            for q in range(2):
                                mm = pe.matmul(ps[:, 4 + 2 * g + q, 0:TCH], gw[j][:, P * g:P * g + P],
                                               xc[j][:, TCH * q:TCH * q + TCH], start=True, stop=True)
                        mm.then_inc(sems["gates_done"], 1)

                    unit(u0, 0, hh_hi, hh_lo, KT, "norm_lo", n0 - 8)
                    with pe.Fori(0, KT // 2 - 1) as i:
                        for j in range(2):
                            unit(u0 + 2 * i + j + 1, 1 - j, hh_hi, hh_lo, KT, None, 0,
                                 between=lambda: gates(2 * i + j, j, i))
                    unit(u0 + KT - 1, 1, hh_hi, hh_lo, KT, None, 0, between=lambda: gates(KT - 2, 0, KT // 2 - 1))
                    gates(KT - 1, 1, KT // 2 - 1)
                if s["kind"] in ("up", "kv", "q"):
                    with pe.Fori(0, s["units"] // 2) as i:
                        for j in range(2):
                            u = u0 + 2 * i + j
                            unit(u, j, hh_hi, hh_lo, KT, "norm_lo", n0 - 8,
                                 a0 + 2 * i + j if s["kind"] == "up" and s["has_ada"] else None)
                            if s["kind"] == "kv":
                                pe.wait_ge(sems["s1_free"], u + 1 + CREDITS["s1_free"])
                                pe.wait_ge(sems["v_ready"], 2 * i + j + CREDITS["v_ready"])
                                for b in range(4):
                                    pe.transpose(ps[:, 4, P * b:P * b + P], vraw[:, P * b:P * b + P], ident)
                                pe.transpose(ps[0:S_TOK, 5, 0:P], vraw[:, SEQ:T], ident)\
                                    .then_inc(sems["v_turned"], 1)
                if s["kind"] == "down":
                    h_all = s["h"]
                    with pe.Fori(0, s["units"] // 2) as i:
                        for j in range(2):
                            kt = s["k"]
                            unit(u0 + 2 * i + j, j, h_hi, h_lo, kt, "h_lo", h_all - kt)
                    if s["sums"]:
                        column_sums(s["stat"])
                if s["kind"] == "attention":
                    def scores(i, j, t):
                        n = P * (i + 1)
                        pe.wait_ge(sems["p_ready"], t + CREDITS["p_ready"])
                        for m in range(2):
                            rows = slice(64 * m, 64 * m + 64)
                            mm = pe.matmul(ps[:, 4 + m, 0:n], qh[j][rows, P * i:P * i + P], kh[j][rows, 0:n],
                                           start=True, stop=True)
                        mm.then_inc(sems["sc_full"], 1)

                    def turn(n, i, t, more):
                        if i == 0 or (i == 1 and more):
                            pe.wait_ge(sems["smasked"], n + 1 + i)
                        pe.wait_ge(sems["att_ready"], t + 1 + CREDITS["att_ready"])
                        pe.wait_ge(sems["attT_ready"], t + CREDITS["attT_ready"])
                        for b in range(i + 1):
                            mm = pe.transpose(ps[:, 6, P * b:P * b + P], att[:, P * b:P * b + P], ident)
                        mm.then_inc(sems["tp_done"], 1)

                    def weigh(h, i, j, t):
                        pe.wait_ge(sems["attT_ready"], t + 1 + CREDITS["attT_ready"])
                        if i == 0:
                            pe.wait_ge(sems["o_evac"], h + CREDITS["o_evac"])
                        for b in range(i + 1):
                            mm = pe.matmul(ps[:, 7, P * i:P * i + P], vh[j][:, b, :], attT[:, P * b:P * b + P],
                                           start=(b == 0), stop=(b == i))
                        mm.then_inc(sems["pv_done"], 1)

                    def page_scores(b, g):
                        pe.wait_ge(sems["qbd_ready"], 2 * b + 2)
                        pe.wait_ge(sems["sp_ready"], b + CREDITS["sp_ready"])
                        pe.wait_ge(sems[f"k_full{g}"], 64 * b + 64)
                        for h in range(N_HEADS):
                            mm = pe.matmul(ps[:, g, :].rearrange("p (n k) -> p n k", k=PAGE),
                                           qbd[:, P * h:P * h + P], kr[g][:, :, h, :],
                                           start=(h == 0), stop=(h == N_HEADS - 1))
                        mm.then_inc(sems["kg_done"], 1)

                    def new_scores(b, t):
                        pe.wait_ge(sems["attT_ready"], t + CREDITS["attT_ready"])
                        for h in range(N_HEADS):
                            mm = pe.matmul(ps[:, 6, 0:S_TOK], qbd[:, P * h:P * h + P], ks[:, h, :],
                                           start=(h == 0), stop=(h == N_HEADS - 1))
                        mm.then_inc(sems["ss_full"], 1)

                    def sample_turn(b):
                        pe.wait_ge(sems["c_ready"], b + 1 + CREDITS["c_ready"])
                        pe.wait_ge(sems["os_evac"], b + CREDITS["os_evac"])
                        for p in range(N_PAGES):
                            pe.matmul(ps[:, 3, S_TOK * p:S_TOK * p + S_TOK], probs[:, PAGE * p:PAGE * p + PAGE],
                                      cmat, start=True, stop=True)
                        pe.matmul(ps[0:S_TOK, 2, 0:S_TOK], probs[:, PAST_LEN:PAST_LEN + S_TOK], cmat,
                                  start=True, stop=True).then_inc(sems["at_done"], 1)

                    def page_outputs(b, g):
                        if g == 0:
                            pe.wait_ge(sems["at_ready"], b + 1 + CREDITS["at_ready"])
                        for p in range(4 * g, 4 * g + 4):
                            pe.wait_ge(sems[f"v_full{p % 4}"], 32 * b + 16 * g + 16)
                            for q in range(2):
                                mm = pe.matmul(ps[0:S_TOK, 2 + q, :], aT[:, S_TOK * p:S_TOK * p + S_TOK],
                                               vr[p % 4][:, 512 * q:512 * q + 512], start=(p == 0), stop=False)
                            mm.then_inc(sems["v_used"], 1)
                        if g == 1:
                            for q in range(2):
                                mm = pe.matmul(ps[0:S_TOK, 2 + q, :], aT[0:S_TOK, PAST_LEN // 2:PAST_LEN // 2 + S_TOK],
                                               vs[:, 4 * q:4 * q + 4, :].rearrange("s h e -> s (h e)"),
                                               start=False, stop=True)
                            mm.then_inc(sems["pvs_done"], 1)

                    def pick(b):
                        pe.wait_ge(sems["os_rows"], b + 1)
                        for h in range(N_HEADS):
                            mm = pe.matmul(ps[:, 3, 8 * h:8 * h + 8], o_rows[h // 4][:, P * (h % 4):P * (h % 4) + P],
                                           ident[0:S_TOK, 8 * h:8 * h + 8], start=True, stop=True)
                        mm.then_inc(sems["os_picked"], 1)

                    def round_(n, half, j, more):
                        pe.wait_ge(sems[f"ph_full{j}"], 48 * half + 48)
                        for i in range(4):
                            t = 4 * n + i
                            scores(i, j, t)
                            if i == 0 and more:
                                page_scores(n + 1, 0)
                            if i == 1:
                                if more:
                                    page_scores(n + 1, 1)
                                    new_scores(n + 1, t)
                                sample_turn(n)
                            if i >= 2:
                                page_outputs(n, i - 2)
                            turn(n, i, t, more)
                            weigh(n, i, j, t)
                        pick(n)

                    pe.wait_ge(sems["w_done"], u0 + CREDITS["w_done"])
                    pe.wait_ge(sems["s_small"], 32)
                    for g in range(2):
                        page_scores(0, g)
                    new_scores(0, 0)
                    with pe.Fori(0, (N_HEADS - 2) // 2) as i:
                        for j in range(2):
                            round_(2 * i + j, i, j, True)
                    round_(N_HEADS - 2, N_HEADS // 2 - 1, 0, True)
                    round_(N_HEADS - 1, N_HEADS // 2 - 1, 1, False)
                    for h in range(N_HEADS):
                        pe.wait_ge(sems["so_sq"], h + 1)
                        if h >= 4:
                            pe.wait_ge(sems["so_ln"], h - 3)
                        for n in range(2):
                            mm = pe.matmul(ps[:, 2 * (h % 4) + n, 0:TH], ones, sq[h % 4][:, TH * n:TH * n + TH],
                                           start=True, stop=True)
                        mm.then_inc(sems["so_sum"], 1)

        @block.scalar
        def _(act):
            credit(act, "ada_rows", "norm_p", "rg_gate", "p_ready", "attT_ready", "sp_ready", "at_ready")

            def split_unit(u, j):
                act.wait_ge(sems[f"raw_full{j}"], 16 * (u[0] + 1))
                act.wait_ge(sems["w_done"], u[1] - 1 + CREDITS["w_done"])
                act.activation(w_hi[j][:, :, :].rearrange("p k n -> p (k n)"), raw[j][:, :], ACT.Copy)\
                   .then_inc(sems["w_hi"], 1)

            def look_ahead(u0, i, j):
                split_unit((u0 // 2 + i + j, u0 + 2 * i + j + 1), 1 - j)

            act.wait_ge(sems["cst_in"], 16)
            act.activation(act_c[:, :, :].rearrange("p k n -> p (k n)"), c("cond"), ACT.Silu)\
               .then_inc(sems["cond_ready"], 1)
            act.wait_ge(sems["cond_ready"], 1)
            act.activation(c_hl[:, :, 0:NC_], act_c[:, :, :], ACT.Copy).then_inc(sems["c_split"], 1)
            act.wait_ge(sems["setup_step"], 5)
            act.activation(setup[0], setup[1], ACT.Exp).then_inc(sems["setup_exp"], 1)
            act.activation(lam4[:, 2:4], lam4[:, 0:2], ACT.Exp).then_inc(sems["setup_exp"], 1)

            def first_split(a, j, turn):
                act.wait_ge(sems[f"pro_full{j}"], 16 * (turn + 1))
                act.wait_ge(sems["ada_done"], a - 1 + CREDITS["ada_done"])
                act.activation(ada_hi[j % 2][:, :, :], pro[j][:, :, :], ACT.Copy).then_inc(sems["ada_hi"], 1)

            def ada_split(a, j, turn):
                act.wait_ge(sems[f"ada_full{j}"], 16 * (turn + 1))
                act.activation(ada_hi[j][:, :, :], ada[j][:, :, :], ACT.Copy).then_inc(sems["ada_hi"], 1)

            def ada_rows(a, j):
                act.wait_ge(sems["ada_done"], a + 1 + CREDITS["ada_done"])
                act.activation(nt[j][0:2 * NC_, 0:256], ps[0:2 * NC_, 4 + j, 0:256], ACT.Copy)\
                   .then_inc(sems["ada_rows"], 1)

            def square(st, k, j):
                act.wait_ge(sems["sq_sum"], 9 * st + k)
                act.activation(sg[j][:, :], x[:, k, :], ACT.Square).then_inc(sems["sq_full"], 1)

            def statistics(st):
                act.wait_ge(sems["sums_full"], st + 1)
                act.activation(halves(rstd[:, :]), ps[:, 6:8, 0:TH], ACT.Ln, scale=1.0 / D_MODEL,
                               bias=eps_x).then_inc(sems["ln_ready"], 1)
                act.wait_ge(sems["ln_ready"], st + 1)
                act.activation(rstd[:, :], rstd[:, :], ACT.Exp, scale=-0.5).then_inc(sems["rstd_ready"], 1)

            first_split(0, 0, 0)
            with act.Fori(0, ADA_FIRST // 4) as i:
                for j in range(4):
                    first_split(4 * i + j + 1, (j + 1) % 4, i + (j + 1) // 4)
                    ada_rows(4 * i + j, j % 2)
            for a in range(ADA_FIRST // 4 * 4, ADA_FIRST - 1):
                first_split(a + 1, (a + 1) % 4, (a + 1) // 4)
                ada_rows(a, a % 2)
            ada_rows(ADA_FIRST - 1, (ADA_FIRST - 1) % 2)
            act.wait_ge(sems["x_in"], 16)
            act.wait_ge(sems["sq_sum"], 1)
            for k in range(2):
                act.activation(sg[k][:, :], x[:, k, :], ACT.Square).then_inc(sems["sq_full"], 1)
            with act.Fori(1, KT // 2) as i:
                for j in range(2):
                    square(0, 2 * i + j, j)
            split_unit((0, 0), 0)
            act.wait_ge(sems["setup_done"], 1)
            statistics(0)
            for s in plan:
                u0, h0 = s["u"], s["h"]
                n0 = 8 * s["norm"]
                if s["kind"] == "norm":
                    act.wait_ge(sems["mod_ready"], s["norm"] + 1 + CREDITS["mod_ready"])
                    with act.Fori(0, 2) as i:
                        for j in range(4):
                            k = 4 * i + j
                            act.wait_ge(sems["norm_t"], n0 + k + 1)
                            act.wait_ge(sems["norm_lo"], n0 + k - 3 + CREDITS["norm_lo"])
                            act.activation(mt[j][:, 0:SEQ], nt[j % 2][:, 0:SEQ], ACT.Identity, scale=mod_a[:, k, 0:1],
                                           bias=mods[:, s["sh"] + k, 0:1]).then_inc(sems["norm_p"], 1)
                            act.wait_ge(sems["norm_p"], n0 + k + 1 + CREDITS["norm_p"])
                            act.wait_ge(sems["norm_s"], n0 + k + 1 + CREDITS["norm_s"])
                            act.activation(hh_hi[:, k, :], mt[j][:, :], ACT.Copy).then_inc(sems["norm_hi"], 1)
                if s["kind"] == "up":
                    if s["rope"] == 8 and s["row"] == 0:
                        for j in range(2):
                            act.wait_ge(sems[f"k_out{j}"], 16 * 4 + CREDITS[f"k_out{j}"])
                            act.wait_ge(sems[f"v_out{j}"], 32 * 4 + CREDITS[f"v_out{j}"])
                    with act.Fori(0, s["units"] // 2) as i:
                        for j in range(2):
                            u, h = u0 + 2 * i + j, h0 + 2 * i + j
                            if s["has_ada"]:
                                ada_split(s["ada"] + 2 * i + j, j, (s["ada"] - ADA_FIRST) // 2 + i)
                            look_ahead(u0, i, j)
                            act.wait_ge(sems["out0_full"], u + 1)
                            act.wait_ge(sems["s1_free"], u - 1 + CREDITS["s1_free"])
                            act.activation(halves(sg[j][:, :]), slot(0), ACT.Silu).then_inc(sems["s0_free"], 1)
                            if s["has_ada"]:
                                ada_rows(s["ada"] + 2 * i + j, j)
                            act.wait_ge(sems["s1_free"], u + 1 + CREDITS["s1_free"])
                            act.activation(h_hi[:, 2 * i + j, :], hf[j][:, :], ACT.Copy).then_inc(sems["h_hi"], 1)
                if s["kind"] == "down":
                    def squares(u, k):
                        act.wait_ge(sems["s0_free"], u + 1 + CREDITS["s0_free"])
                        square(s["stat"], k, 0)
                        act.wait_ge(sems["s1_free"], u + 1 + CREDITS["s1_free"])
                        square(s["stat"], k + 1, 1)

                    if s["last"]:
                        for n in range(s["units"]):
                            if n < s["units"] - 1:
                                look_ahead(u0, n // 2, n % 2)
                            squares(u0 + n, 2 * n)
                    else:
                        with act.Fori(0, s["units"] // 2) as i:
                            for j in range(2):
                                look_ahead(u0, i, j)
                                if s["sums"]:
                                    squares(u0 + 2 * i + j, 4 * i + 2 * j)
                    if s["sums"]:
                        statistics(s["stat"])
                if s["kind"] == "rglru":
                    def conv_in(n):
                        u = u0 + n
                        act.wait_ge(sems["out0_full"], u + 1)
                        act.wait_ge(sems["rg_conv"], NCV * (n - 1) + CV["tap3"] + CREDITS["rg_conv"])
                        act.activation(xp[:, PADS:PADS + TH], ps[:, 0, 0:TH], ACT.Copy)
                        act.activation(xp[:, PADS + TH:S0], ps[:, 1, 0:PB], ACT.Copy)
                        act.activation(seq_cols(xp, S0 + PADS, DEC_SEQ), by_seq(ps[:, 1, PB:TH]), ACT.Copy)\
                           .then_inc(sems["s0_free"], 1)

                    def square_y(n):
                        u = u0 + n
                        act.wait_ge(sems["w_done"], u + 1 + CREDITS["w_done"])
                        act.wait_ge(sems["s1_free"], u + CREDITS["s1_free"])
                        act.activation(halves(gv[:, 0:T]), slot(1), ACT.Square).then_inc(sems["rg_gelu"], 1)

                    def gelu(n):
                        act.wait_ge(sems["rg_conv"], NCV * n + CV["gelu_arg"] + CREDITS["rg_conv"])
                        act.activation(gt[:, 0:T], gv[:, 0:T], ACT.Tanh, scale=math.sqrt(2.0 / math.pi))\
                           .then_inc(sems["rg_gelu"], 1)

                    def back(n, j):
                        ga = NGA * n + CREDITS["rg_gate"]
                        sc = NSC * n + CREDITS["rg_scan"]
                        act.wait_ge(sems["gates_done"], n + 1 + CREDITS["gates_done"])
                        act.wait_ge(sems["rg_scan"], sc)
                        act.activation(halves(th_r[:, :]), ps[:, 4:6, 0:TCH], ACT.Tanh, scale=0.5,
                                       bias=rg_brh[:, bass.ds(n, 1)]).then_inc(sems["rg_gate"], 1)
                        act.activation(halves(th_i[:, :]), ps[:, 6:8, 0:TCH], ACT.Tanh, scale=0.5,
                                       bias=rg_bih[:, bass.ds(n, 1)]).then_inc(sems["rg_gate"], 1)
                        act.wait_ge(sems["rg_gate"], ga + GA["tanh_r"])
                        act.activation(tau[:, :], th_r[:, :], ACT.Tanh, scale=rg_c4[:, bass.ds(n, 1)],
                                       bias=rg_c4[:, bass.ds(n, 1)]).then_inc(sems["rg_gate"], 1)
                        act.activation(dec[:, :], th_r[:, :], ACT.Exp, scale=rg_nc4[:, bass.ds(n, 1)],
                                       bias=rg_nc4[:, bass.ds(n, 1)]).then_inc(sems["rg_gate"], 1)
                        act.wait_ge(sems["rg_gate"], ga + GA["a"])
                        act.activation(dec2[:, :], dec[:, :], ACT.Square).then_inc(sems["rg_gate"], 1)
                        act.wait_ge(sems["rg_scan"], sc + SC["one_minus_a2"])
                        act.activation(dec2[:, :], tau[:, :], ACT.Sqrt).then_inc(sems["rg_gate"], 1)

                    def product_hi(n, j):
                        act.wait_ge(sems["rg_scan"], NSC * n + SC["z_sample"] + CREDITS["rg_scan"])
                        act.activation(h_hi[:, n, :], hf[j][:, :], ACT.Copy).then_inc(sems["h_hi"], 1)

                    split_unit((u0 // 2, u0 + 1), 1)
                    conv_in(0)
                    square_y(0)
                    gelu(0)
                    with act.Fori(0, KT // 2 - 1) as i:
                        for j in range(2):
                            split_unit((u0 // 2 + i + 1, u0 + 2 * i + j + 2), j)
                            n = 2 * i + j
                            conv_in(n + 1)
                            back(n, j)
                            square_y(n + 1)
                            product_hi(n, j)
                            gelu(n + 1)
                    split_unit((u0 // 2 + KT // 2, u0 + KT), 0)
                    conv_in(KT - 1)
                    back(KT - 2, 0)
                    square_y(KT - 1)
                    product_hi(KT - 2, 0)
                    gelu(KT - 1)
                    back(KT - 1, 1)
                    product_hi(KT - 1, 1)
                if s["kind"] in ("kv", "q"):
                    kv = s["kind"] == "kv"
                    with act.Fori(0, s["units"] // 2) as i:
                        for j in range(2):
                            u = u0 + 2 * i + j
                            look_ahead(u0, i, j)
                            for t in range(1 if kv else 2):
                                r = s["rope"] + (2 * i + j if kv else 4 * i + 2 * j + t)
                                full = "w_done" if t else "out0_full"
                                act.wait_ge(sems[full], count(full, u + 1))
                                act.wait_ge(sems["rope_done"], r + CREDITS["rope_done"])
                                for q in range(4):
                                    cp = act.activation(halves(swapped[32 * q:32 * q + 32, :]),
                                                        ps[32 * (q ^ 1):32 * (q ^ 1) + 32, 2 * t:2 * t + 2, 0:TH],
                                                        ACT.Copy)
                                cp.then_inc(sems["rope_swap"], 1)
                            if kv:
                                act.wait_ge(sems["w_done"], u + 1 + CREDITS["w_done"])
                                act.wait_ge(sems["v_turned"], 2 * i + j + CREDITS["v_turned"])
                                act.activation(halves(vraw[:, :]), slot(1), ACT.Copy).then_inc(sems["s1_free"], 1)
                            for t in range(1 if kv else 2):
                                n, rj = (2 * i + j, j) if kv else (4 * i + 2 * j + t, t)
                                act.wait_ge(sems["rope_done"], s["rope"] + n + 1 + CREDITS["rope_done"])
                                act.dma_start((kT_out if kv else qT)[n], rk[rj][:, :])\
                                   .then_inc(sems[f"k_out{rj}"], 16)
                            if kv:
                                act.wait_ge(sems["v_ready"], 2 * i + j + 1 + CREDITS["v_ready"])
                                act.dma_start(v_prompt[2 * i + j], vt[j][:, :].rearrange("p (b e) -> p b e", e=P))\
                                   .then_inc(sems[f"v_out{j}"], 16)
                                act.dma_start(v_sample[2 * i + j], vts[j][:, :]).then_inc(sems[f"v_out{j}"], 16)
                if s["kind"] == "attention":
                    def exps(i, t):
                        n = P * (i + 1)
                        act.wait_ge(sems["nmx_ready"], t + 1 + CREDITS["nmx_ready"])
                        act.wait_ge(sems["att_ready"], t - 1 + CREDITS["att_ready"])
                        for m in range(2):
                            e = act.activation(pp[i % 2][:, m, 0:n], ps[:, 4 + m, 0:n], ACT.Exp,
                                               bias=nmx[:, m:m + 1], accum_out=sums[i % 2][:, m:m + 1])
                        e.then_inc(sems["p_ready"], 1)

                    def turned(i, t):
                        n = P * (i + 1)
                        act.wait_ge(sems["tp_done"], t + 1 + CREDITS["tp_done"])
                        act.wait_ge(sems["pv_done"], t + CREDITS["pv_done"])
                        act.activation(attT[:, 0:n], ps[:, 6, 0:n], ACT.Copy).then_inc(sems["attT_ready"], 1)

                    def sample_exp(b):
                        act.wait_ge(sems["snmx"], b + 1)
                        act.wait_ge(sems["at_done"], b + CREDITS["at_done"])
                        act.activation(probs[:, 0:PAST_LEN], page_sc, ACT.Exp, bias=nmxs, accum_out=sumss2[:, 0:1])
                        act.activation(probs[:, PAST_LEN:PAST_LEN + S_TOK], new_sc, ACT.Exp, bias=nmxs,
                                       accum_out=sumss2[:, 1:2]).then_inc(sems["sp_ready"], 1)

                    def sample_turned(b):
                        act.wait_ge(sems["at_done"], b + 1 + CREDITS["at_done"])
                        act.wait_ge(sems["pvs_done"], b + CREDITS["pvs_done"])
                        act.activation(aT[:, 0:512], ps[:, 3, :], ACT.Copy)
                        act.activation(aT[0:S_TOK, 512:512 + S_TOK], ps[0:S_TOK, 2, 0:S_TOK], ACT.Copy)\
                           .then_inc(sems["at_ready"], 1)

                    def sample_rows(b):
                        act.wait_ge(sems["pvs_done"], b + 1 + CREDITS["pvs_done"])
                        act.wait_ge(sems["os_picked"], b + CREDITS["os_picked"])
                        act.activation(o_rows[0], ps[0:S_TOK, 2, :], ACT.Copy)
                        act.activation(o_rows[1], ps[0:S_TOK, 3, :], ACT.Copy).then_inc(sems["os_rows"], 1)

                    def round_(n, more):
                        for i in range(4):
                            exps(i, 4 * n + i)
                            if i == 3:
                                if more:
                                    sample_exp(n + 1)
                                sample_rows(n)
                            if i == 1:
                                sample_turned(n)
                            turned(i, 4 * n + i)

                    sample_exp(0)
                    with act.Fori(0, N_HEADS - 1) as n:
                        round_(n, True)
                    round_(N_HEADS - 1, False)
                    for h in range(N_HEADS):
                        act.wait_ge(sems["so_sum"], h + 1)
                        act.activation(halves(rs[h][:, :]), ps[:, 2 * (h % 4):2 * (h % 4) + 2, 0:TH], ACT.Ln,
                                       scale=1.0 / P, bias=eps_o).then_inc(sems["so_ln"], 1)

                    def head_rs(h):
                        act.wait_ge(sems["so_ln"], h + 1)
                        act.activation(rs[h][:, :], rs[h][:, :], ACT.Exp, scale=-0.5).then_inc(sems["so_rs"], 1)

                    def head_hi(h):
                        act.wait_ge(sems["so_n"], h + 1)
                        act.activation(h_hi[:, h, :], hf[h % 2][:, :], ACT.Copy).then_inc(sems["h_hi"], 1)

                    head_rs(0)
                    for h in range(1, N_HEADS):
                        head_rs(h)
                        head_hi(h - 1)
                    head_hi(N_HEADS - 1)
                if s["kind"] == "final":
                    with act.Fori(0, 4) as i:
                        for j in range(2):
                            k = 2 * i + j
                            act.wait_ge(sems["norm_t"], n0 + k + 1)
                            act.wait_ge(sems[f"out_y{j}"], 16 * i + CREDITS[f"out_y{j}"])
                            act.activation(hf[j][:, :], nt[j][:, :], ACT.Copy, scale=c("final_g")[:, bass.ds(k, 1)])\
                               .then_inc(sems["norm_p"], 1)

        @block.vector
        def _(dve):
            credit(dve, "w_lo", "s0_free", "s1_free", "ada_evac", "norm_s", "res_tmp", "mod_ready", "rg_conv",
                   "rg_scan", "rope_done",
                   "v_ready", "att_ready", "o_evac", "nmx_ready", "c_ready", "os_evac")
            dve.wait_ge(sems["c_split"], 1)
            dve.tensor_tensor(c_hl[:, :, NC_:2 * NC_], act_c[:, :, :], c_hl[:, :, 0:NC_].bitcast(F32), ALU.subtract)\
               .then_inc(sems["c_split"], 1)
            dve.memset(eps_x, EPS).then_inc(sems["setup_step"], 1)
            dve.wait_ge(sems["setup_step"], 1)
            dve.wait_ge(sems["cst_in"], 16)
            lam_in = c("lru_lambda")
            dve.tensor_scalar(setup[2], lam_in, -1.0, None, ALU.mult).then_inc(sems["setup_step"], 1)
            dve.wait_ge(sems["setup_step"], 2)
            dve.tensor_tensor(setup[1], setup[2], lam_in, ALU.min).then_inc(sems["setup_step"], 1)
            dve.wait_ge(sems["setup_step"], 3)
            lp = c("lam_p").rearrange("p (a b d) -> p a b d", a=2, b=2)
            dots = sg[0][:, 0:2 * HEAD_DIM].rearrange("p (a d) -> p a d", a=2)
            dve.tensor_tensor(dots, lp[:, :, 0, :], lp[:, :, 1, :], ALU.mult).then_inc(sems["setup_step"], 1)
            dve.wait_ge(sems["setup_step"], 4)
            dve.tensor_reduce(lam4[:, 0:2], dots, AXX, ALU.add).then_inc(sems["setup_step"], 1)
            dve.wait_ge(sems["setup_step"], 5)
            dve.wait_ge(sems["setup_exp"], 2)
            dve.tensor_tensor(lam4[:, 0:1], lam4[:, 3:4], lam4[:, 2:3], ALU.subtract).then_inc(sems["setup_step"], 1)
            dve.wait_ge(sems["setup_step"], 6)
            dve.tensor_scalar(neg_lam, lam4[:, 0:1], -LAM_INIT, None, ALU.add).then_inc(sems["setup_step"], 1)
            dve.wait_ge(sems["setup_step"], 7)
            dve.tensor_scalar(lam4[:, 1:2], neg_lam, -1.0, None, ALU.mult).then_inc(sems["setup_step"], 1)
            dve.wait_ge(sems["setup_step"], 8)
            dve.tensor_tensor(lam4[:, 1:2], lam4[:, 1:2], neg_lam, ALU.max).then_inc(sems["setup_step"], 1)
            dve.wait_ge(sems["setup_step"], 9)
            dve.tensor_scalar(lam4[:, 1:2], lam4[:, 1:2], 1.0, None, ALU.add).then_inc(sems["setup_step"], 1)
            dve.wait_ge(sems["setup_step"], 10)
            dve.reciprocal(map_gain[:, 0:1], lam4[:, 1:2]).then_inc(sems["setup_step"], 1)
            dve.wait_ge(sems["setup_step"], 11)
            dve.tensor_tensor(map_gain[:, 1:2], map_gain[:, 0:1], neg_lam, ALU.mult).then_inc(sems["setup_step"], 1)
            dve.wait_ge(sems["setup_step"], 12)
            dve.tensor_scalar(eps_o, map_gain[:, 0:1], EPS, None, ALU.mult).then_inc(sems["setup_step"], 1)
            dve.wait_ge(sems["setup_step"], 13)
            dve.tensor_tensor(eps_o, eps_o, map_gain[:, 0:1], ALU.mult).then_inc(sems["setup_step"], 1)
            dve.wait_ge(sems["setup_step"], 14)
            dve.tensor_tensor(row_sign, c("map0"), map_gain[:, 0:1], ALU.mult).then_inc(sems["setup_step"], 1)
            dve.wait_ge(sems["setup_step"], 15)
            dve.scalar_tensor_tensor(row_sign, c("map1"), map_gain[:, 1:2], row_sign, ALU.mult, ALU.add)\
               .then_inc(sems["setup_step"], 1)
            dve.wait_ge(sems["setup_step"], 16)
            dve.tensor_scalar(gain_o, c("subln_g"), 1.0 - LAM_INIT, None, ALU.mult).then_inc(sems["setup_step"], 1)
            dve.wait_ge(sems["setup_step"], 17)
            e, z, z2, acc = setup[0], setup[1], setup[3], setup[4]
            dve.tensor_scalar(z, e, 2.0, None, ALU.add).then_inc(sems["setup_step"], 1)
            dve.wait_ge(sems["setup_step"], 18)
            dve.reciprocal(z2, z).then_inc(sems["setup_step"], 1)
            dve.wait_ge(sems["setup_step"], 19)
            dve.tensor_tensor(z, z2, e, ALU.mult).then_inc(sems["setup_step"], 1)
            dve.wait_ge(sems["setup_step"], 20)
            dve.tensor_tensor(z2, z, z, ALU.mult).then_inc(sems["setup_step"], 1)
            dve.wait_ge(sems["setup_step"], 21)
            dve.tensor_scalar(acc, z2, 1.0 / 17, 1.0 / 15, ALU.mult, ALU.add).then_inc(sems["setup_step"], 1)
            dve.wait_ge(sems["setup_step"], 22)
            for i, n in enumerate((13, 11, 9, 7, 5, 3, 1)):
                dve.tensor_tensor(acc, acc, z2, ALU.mult).then_inc(sems["setup_step"], 1)
                dve.wait_ge(sems["setup_step"], 23 + 2 * i)
                dve.tensor_scalar(acc, acc, 1.0 / n, None, ALU.add).then_inc(sems["setup_step"], 1)
                dve.wait_ge(sems["setup_step"], 24 + 2 * i)
            dve.tensor_tensor(acc, acc, z, ALU.mult).then_inc(sems["setup_step"], 1)
            dve.wait_ge(sems["setup_step"], 37)
            dve.tensor_scalar(z, setup[2], 0.0, None, ALU.max).then_inc(sems["setup_step"], 1)
            dve.wait_ge(sems["setup_step"], 38)
            dve.scalar_tensor_tensor(acc, acc, 2.0, z, ALU.mult, ALU.add).then_inc(sems["setup_step"], 1)
            dve.wait_ge(sems["setup_step"], 39)
            dve.tensor_scalar(rg_c4, acc, 4.0, None, ALU.mult).then_inc(sems["setup_step"], 1)
            dve.wait_ge(sems["setup_step"], 40)
            dve.tensor_scalar(rg_nc4, acc, -4.0, None, ALU.mult).then_inc(sems["setup_step"], 1)
            dve.wait_ge(sems["setup_step"], 41)
            dve.tensor_scalar(rg_brh, c("b_rg"), 0.5, None, ALU.mult).then_inc(sems["setup_step"], 1)
            dve.wait_ge(sems["setup_step"], 42)
            dve.tensor_scalar(rg_bih, c("b_ig"), 0.5, None, ALU.mult).then_inc(sems["setup_done"], 1)

            def split_unit(u, j):
                dve.wait_ge(sems["w_hi"], u + 1)
                dve.wait_ge(sems["w_done"], u - 1 + CREDITS["w_done"])
                dve.tensor_tensor(w_lo[j][:, :, :].rearrange("p k n -> p (k n)"), raw[j][:, :],
                                  w_hi[j][:, :, :].rearrange("p k n -> p (k n)").bitcast(F32),
                                  ALU.subtract).then_inc(sems["w_lo"], 1)

            def first_split(a, j):
                dve.wait_ge(sems["ada_hi"], a + 1)
                dve.wait_ge(sems["ada_done"], a - 1 + CREDITS["ada_done"])
                dve.tensor_tensor(ada_lo[j % 2][:, :, :], pro[j][:, :, :], ada_hi[j % 2][:, :, :].bitcast(F32),
                                  ALU.subtract).then_inc(sems["ada_lo"], 1)

            def ada_split(a, j):
                dve.wait_ge(sems["ada_hi"], a + 1)
                dve.tensor_tensor(ada_lo[j][:, :, :], ada[j][:, :, :], ada_hi[j][:, :, :].bitcast(F32),
                                  ALU.subtract).then_inc(sems["ada_lo"], 1)

            def ada_bias(a, j):
                dve.wait_ge(sems["ada_turned"], a + 1)
                dve.tensor_tensor(mods[:, bass.ds(2 * a, 2), :],
                                  ps[:, 4 + j, 256:256 + 2 * NC_].rearrange("p (t n) -> p t n", t=2),
                                  c("ada_b")[:, bass.ds(2 * a, 2)].unsqueeze(2).to_broadcast([P, 2, NC_]),
                                  ALU.add).then_inc(sems["ada_evac"], 1)

            def clear_sums(n0):
                dve.wait_ge(sems["norm_t"], n0)
                dve.memset(rstd[:, :], 0.0).then_inc(sems["sq_sum"], 1)

            def add_square(st, k, j):
                dve.wait_ge(sems["sq_full"], 8 * st + k + 1)
                dve.wait_ge(sems["sq_sum"], 9 * st + k + 1)
                dve.tensor_tensor(rstd[:, :], rstd[:, :], sg[j][:, :], ALU.add).then_inc(sems["sq_sum"], 1)

            dve.memset(rstd[:, :], 0.0).then_inc(sems["sq_sum"], 1)
            first_split(0, 0)
            with dve.Fori(0, ADA_FIRST // 4) as i:
                for j in range(4):
                    first_split(4 * i + j + 1, (j + 1) % 4)
                    ada_bias(4 * i + j, j % 2)
            for a in range(ADA_FIRST // 4 * 4, ADA_FIRST - 1):
                first_split(a + 1, (a + 1) % 4)
                ada_bias(a, a % 2)
            ada_bias(ADA_FIRST - 1, (ADA_FIRST - 1) % 2)
            with dve.Fori(0, KT // 2) as i:
                for j in range(2):
                    add_square(0, 2 * i + j, j)
            split_unit(0, 0)

            def residual(u, k, t, res):
                dve.wait_ge(sems["w_done" if t else "out0_full"], count("w_done" if t else "out0_full", u + 1))
                dve.scalar_tensor_tensor(x[:, k, 0:TH], ps[:, 2 * t, 0:TH], mod_g[:, k, 0:1], x[:, k, 0:TH],
                                         ALU.mult, ALU.add)
                dve.scalar_tensor_tensor(x[:, k, TH:SEQ], ps[:, 2 * t + 1, 0:PB], mod_g[:, k, 0:1], x[:, k, TH:SEQ],
                                         ALU.mult, ALU.add)
                dve.wait_ge(sems["s0_free" if t else "s1_free"], count("s0_free" if t else "s1_free", u + t))
                dve.tensor_tensor(by_seq(r_tmp), by_seq(ps[:, 2 * t + 1, PB:TH]),
                                  mod_g[:, k, 1:NC_].unsqueeze(2).to_broadcast([P, DEC_BATCH, DEC_SEQ]),
                                  ALU.mult).then_inc(sems["res_tmp"], 1)
                dve.wait_ge(sems["res_tmp"], res + 1 + CREDITS["res_tmp"])
                dve.tensor_tensor(x[:, k, SEQ:T], r_tmp, x[:, k, SEQ:T], ALU.add)\
                   .then_inc(sems["s1_free" if t else "s0_free"], 1)

            def rope(u, t, r, scale, j):
                dve.wait_ge(sems["w_done" if t else "out0_full"], count("w_done" if t else "out0_full", u + 1))
                dve.wait_ge(sems["rope_swap"], r + 1)
                dve.scalar_tensor_tensor(halves(rope_a[:, :]), slot(t), scale, halves(c("cos")), ALU.mult, ALU.mult)\
                   .then_inc(sems["s1_free" if t else "s0_free"], 1)
                dve.scalar_tensor_tensor(rope_b[:, :], swapped[:, :], scale, c("sin"), ALU.mult, ALU.mult)\
                   .then_inc(sems["rope_t2"], 1)
                dve.wait_ge(sems["rope_t2"], r + 1)
                dve.tensor_tensor(rk[j][:, :], rope_a[:, :], rope_b[:, :], ALU.add).then_inc(sems["rope_done"], 1)

            for s in plan:
                u0, h0 = s["u"], s["h"]
                n0 = 8 * s["norm"]
                if s["kind"] in ("norm", "final"):
                    if s["kind"] == "norm":
                        dve.wait_ge(sems["ada_evac"], s["ada"] + CREDITS["ada_evac"])
                        dve.wait_ge(sems["norm_p"], n0 + CREDITS["norm_p"])
                        dve.wait_ge(sems["norm_s"], n0 + CREDITS["norm_s"])
                        dve.wait_ge(sems["s1_free"], u0 + CREDITS["s1_free"])
                        sc = mods[:, s["sc"]:s["sc"] + 8, :]
                        gain = dve.scalar_tensor_tensor(
                            mod_a[:, :, :], sc, 1.0,
                            cst[:, s["g"]:s["g"] + 8].unsqueeze(2).to_broadcast([P, 8, NC_]), ALU.add, ALU.mult)
                        if s["ga"] is None:
                            gain.then_inc(sems["mod_ready"], 1)
                        else:
                            dve.tensor_scalar(mod_g[:, :, :], mods[:, s["ga"]:s["ga"] + 8, :], s["half"], None,
                                              ALU.mult).then_inc(sems["mod_ready"], 1)
                        dve.wait_ge(sems["mod_ready"], s["norm"] + 1 + CREDITS["mod_ready"])
                    dve.wait_ge(sems["h_lo"], h0 + CREDITS["h_lo"])
                    dve.wait_ge(sems["rstd_ready"], s["stat"])
                    def scaled(k, j):
                        dve.wait_ge(sems["norm_p"], n0 + k - 1 + CREDITS["norm_p"])
                        if s["kind"] == "norm":
                            dve.wait_ge(sems["norm_s"], n0 + k - 1 + CREDITS["norm_s"])
                        dve.tensor_tensor(nt[j % 2][:, :], x[:, k, :], rstd[:, :], ALU.mult)\
                           .then_inc(sems["norm_t"], 1)

                    def sample_gain(k, j):
                        dve.wait_ge(sems["norm_t"], n0 + k + 1)
                        dve.tensor_tensor(by_seq(m_tmp[j % 2]), by_seq(nt[j % 2][:, SEQ:T]),
                                          mod_a[:, k, 1:NC_].unsqueeze(2).to_broadcast([P, DEC_BATCH, DEC_SEQ]),
                                          ALU.mult).then_inc(sems["norm_tmp"], 1)

                    def sample_shift(k, j):
                        dve.wait_ge(sems["norm_tmp"], n0 + k + 1)
                        dve.wait_ge(sems["norm_lo"], n0 + k - 3 + CREDITS["norm_lo"])
                        dve.tensor_tensor(by_seq(mt[j][:, SEQ:T]), by_seq(m_tmp[j % 2]),
                                          mods[:, s["sh"] + k, 1:NC_].unsqueeze(2).to_broadcast(
                                              [P, DEC_BATCH, DEC_SEQ]),
                                          ALU.add).then_inc(sems["norm_s"], 1)

                    with dve.Fori(0, 2) as i:
                        for q in (0, 2):
                            for part in (scaled, sample_gain, sample_shift) if s["kind"] == "norm" else (scaled,):
                                for j in (q, q + 1):
                                    part(4 * i + j, j)
                if s["kind"] == "up":
                    with dve.Fori(0, s["units"] // 2) as i:
                        for j in range(2):
                            u, h = u0 + 2 * i + j, h0 + 2 * i + j
                            if s["has_ada"]:
                                ada_split(s["ada"] + 2 * i + j, j)
                            split_unit(u + 1, 1 - j)
                            dve.wait_ge(sems["w_done"], u + 1 + CREDITS["w_done"])
                            dve.wait_ge(sems["s0_free"], u + 1 + CREDITS["s0_free"])
                            dve.wait_ge(sems["h_lo"], h - 1 + CREDITS["h_lo"])
                            dve.tensor_tensor(halves(hf[j][:, :]), halves(sg[j][:, :]), slot(1), ALU.mult)\
                               .then_inc(sems["s1_free"], 1)
                            if s["has_ada"]:
                                ada_bias(s["ada"] + 2 * i + j, j)
                if s["kind"] == "down":
                    if s["sums"]:
                        clear_sums(n0)
                    if s["last"]:
                        for n in range(s["units"]):
                            if n < s["units"] - 1:
                                split_unit(u0 + n + 1, 1 - n % 2)
                            for t in range(2):
                                residual(u0 + n, 2 * n + t, t, s["res"] + 2 * n + t)
                                add_square(s["stat"], 2 * n + t, t)
                    else:
                        with dve.Fori(0, s["units"] // 2) as i:
                            for j in range(2):
                                split_unit(u0 + 2 * i + j + 1, 1 - j)
                                for t in range(2):
                                    n = 4 * i + 2 * j + t
                                    residual(u0 + 2 * i + j, n, t, s["res"] + n)
                                    if s["sums"]:
                                        add_square(s["stat"], n, t)
                if s["kind"] == "rglru":
                    dve.wait_ge(sems["norm_lo"], n0 + CREDITS["norm_lo"])
                    dve.memset(xp[:, 0:PADS], 0.0).then_inc(sems["rg_pad"], 1)
                    dve.wait_ge(sems["rg_pad"], 1)
                    def conv(n, j):
                        u, cv = u0 + n, NCV * n + CREDITS["rg_conv"]
                        dve.wait_ge(sems["rg_conv"], cv)
                        dve.tensor_copy(seq_cols(xp, S0, PADS), c("st_conv")[:, bass.ds(24 * n, 24)].rearrange(
                            "p (b s) -> p b s", b=DEC_BATCH)).then_inc(sems["rg_conv"], 1)
                        dve.wait_ge(sems["s0_free"], u + 1 + CREDITS["s0_free"])
                        dve.tensor_copy(conv_sb[:, n, 0, :], xp[:, SEQ:SEQ + PADS])\
                           .then_inc(sems["rg_conv"], 1)
                        dve.tensor_copy(conv_sb[:, n, 1:NC_, :], seq_cols(xp, S0 + DEC_SEQ, PADS))\
                           .then_inc(sems["rg_conv"], 1)
                        dve.wait_ge(sems["gates_done"], n - 1 + CREDITS["gates_done"])
                        dve.wait_ge(sems["rg_scan"], NSC * (n - 1) + CREDITS["rg_scan"])
                        dve.wait_ge(sems["rg_conv"], cv + CV["state_in"])
                        cw = c("conv_w")
                        dve.tensor_scalar(xc[j][:, :], xp[:, 0:TC], cw[:, bass.ds(4 * n, 1)],
                                              c("conv_b")[:, bass.ds(n, 1)], ALU.mult, ALU.add)\
                                                 .then_inc(sems["rg_conv"], 1)
                        for w in range(1, CONV_W):
                            dve.wait_ge(sems["rg_conv"], cv + CV[f"tap{w - 1}"])
                            dve.scalar_tensor_tensor(xc[j][:, :], xp[:, w:w + TC], cw[:, bass.ds(4 * n + w, 1)],
                                                         xc[j][:, :], ALU.mult, ALU.add)\
                                                            .then_inc(sems["rg_conv"], 1)

                    def gelu(n, j):
                        u, cv = u0 + n, NCV * n + CREDITS["rg_conv"]
                        dve.wait_ge(sems["rg_gelu"], NGE * n + GE["y2"])
                        dve.tensor_scalar(gv[:, 0:T], gv[:, 0:T], 0.044715, 1.0, ALU.mult, ALU.add)\
                           .then_inc(sems["rg_conv"], 1)
                        dve.wait_ge(sems["rg_conv"], cv + CV["gelu_poly"])
                        dve.tensor_tensor(halves(gv[:, 0:T]), halves(gv[:, 0:T]), slot(1), ALU.mult)\
                           .then_inc(sems["rg_conv"], 1)
                        dve.wait_ge(sems["rg_gelu"], NGE * n + GE["gelu_tanh"])
                        dve.scalar_tensor_tensor(halves(gy[j][:, 0:T]), halves(gt[:, 0:T]), 1.0, slot(1), ALU.add,
                                                 ALU.mult).then_inc(sems["s1_free"], 1)
                        dve.wait_ge(sems["s1_free"], u + 1 + CREDITS["s1_free"])

                    def back(n, j):
                        sc, ga = NSC * n + CREDITS["rg_scan"], NGA * n + CREDITS["rg_gate"]
                        dve.wait_ge(sems["rg_gate"], ga + GA["tanh_i"])
                        dve.scalar_tensor_tensor(xc[j][:, :], th_i[:, :], 1.0, xc[j][:, :], ALU.add, ALU.mult)\
                           .then_inc(sems["rg_scan"], 1)
                        dve.wait_ge(sems["rg_gate"], ga + GA["a2"])
                        dve.scalar_tensor_tensor(tau[:, :], dec2[:, :], 1.0, tau[:, :], ALU.add, ALU.mult)\
                           .then_inc(sems["rg_scan"], 1)
                        dve.wait_ge(sems["rg_gate"], ga + GA["root"])
                        dve.wait_ge(sems["rg_scan"], sc + SC["gated_x"])
                        dve.scalar_tensor_tensor(xc[j][:, :], dec2[:, :], 0.5, xc[j][:, :], ALU.mult, ALU.mult)\
                           .then_inc(sems["rg_scan"], 1)
                        dve.wait_ge(sems["rg_scan"], sc + SC["u"])
                        dve.memset(seq_cols(dec, S0 - 1, 1), 0.0).then_inc(sems["rg_scan"], 1)
                        dve.tensor_copy(seq_cols(xc[j], S0 - 1, 1),
                                            c("st_h")[:, bass.ds(8 * n, 8)].unsqueeze(2))\
                                               .then_inc(sems["rg_scan"], 1)
                        dve.wait_ge(sems["rg_scan"], sc + SC["reset_u"])
                        dve.tensor_tensor_scan(hs[:, :], dec[:, :], xc[j][:, :], 0.0, ALU.mult, ALU.add)\
                           .then_inc(sems["rg_scan"], 1)
                        dve.wait_ge(sems["rg_scan"], sc + SC["scan"])
                        dve.tensor_copy(h_sb[:, n, 0:1], hs[:, SEQ - 1:SEQ])\
                           .then_inc(sems["rg_scan"], 1)
                        dve.tensor_copy(h_sb[:, n, 1:NC_].unsqueeze(2), seq_cols(hs, S0 + DEC_SEQ - 1, 1))\
                           .then_inc(sems["rg_scan"], 1)
                        dve.wait_ge(sems["h_lo"], h0 + n - 1 + CREDITS["h_lo"])
                        dve.scalar_tensor_tensor(hf[j][:, 0:SEQ], hs[:, 0:SEQ], 0.5, gy[j][:, 0:SEQ], ALU.mult,
                                                     ALU.mult).then_inc(sems["rg_scan"], 1)
                        dve.scalar_tensor_tensor(by_seq(hf[j][:, SEQ:T]), seq_cols(hs, S0, DEC_SEQ), 0.5,
                                                     by_seq(gy[j][:, SEQ:T]), ALU.mult, ALU.mult)\
                                                        .then_inc(sems["rg_scan"], 1)

                    split_unit(u0 + 1, 1)
                    conv(0, 0)
                    gelu(0, 0)
                    with dve.Fori(0, KT // 2 - 1) as i:
                        for j in range(2):
                            split_unit(u0 + 2 * i + j + 2, j)
                            conv(2 * i + j + 1, 1 - j)
                            back(2 * i + j, j)
                            gelu(2 * i + j + 1, 1 - j)
                    split_unit(u0 + KT, 0)
                    conv(KT - 1, 1)
                    back(KT - 2, 0)
                    gelu(KT - 1, 1)
                    back(KT - 1, 1)
                if s["kind"] in ("kv", "q"):
                    kv = s["kind"] == "kv"
                    with dve.Fori(0, s["units"] // 2) as i:
                        for j in range(2):
                            u = u0 + 2 * i + j
                            split_unit(u + 1, 1 - j)
                            for t in range(1 if kv else 2):
                                n = 2 * i + j if kv else 4 * i + 2 * j + t
                                rj = j if kv else t
                                stores = i if kv else 4 + 2 * i + j
                                dve.wait_ge(sems[f"k_out{rj}"], 16 * stores + CREDITS[f"k_out{rj}"])
                                rope(u, t, s["rope"] + n, 1.0 if kv else HEAD_DIM ** -0.5, rj)
                            if kv:
                                dve.wait_ge(sems["v_turned"], 2 * i + j + 1 + CREDITS["v_turned"])
                                dve.wait_ge(sems[f"v_out{j}"], 32 * i + CREDITS[f"v_out{j}"])
                                dve.tensor_copy(vt[j][:, :], ps[:, 4, :])
                                dve.tensor_copy(vts[j][:, :], ps[0:S_TOK, 5, 0:P]).then_inc(sems["v_ready"], 1)
                if s["kind"] == "attention":
                    causal = c("causal").unsqueeze(1).to_broadcast([P, 2, P])

                    def maximum(i, t):
                        n = P * (i + 1)
                        dve.wait_ge(sems["sc_full"], t + 1)
                        dve.tensor_tensor(ps[:, 4:6, P * i:P * i + P], ps[:, 4:6, P * i:P * i + P], causal,
                                          ALU.add).then_inc(sems["masked"], 1)
                        dve.wait_ge(sems["masked"], t + 1)
                        dve.wait_ge(sems["nmx_ready"], t + CREDITS["nmx_ready"])
                        dve.tensor_reduce(mx, ps[:, 4:6, 0:n], AXX, ALU.max).then_inc(sems["max_ready"], 1)
                        dve.wait_ge(sems["max_ready"], t + 1)
                        dve.wait_ge(sems["p_ready"], t + CREDITS["p_ready"])
                        dve.tensor_scalar(nmx, mx, -1.0, None, ALU.mult).then_inc(sems["nmx_ready"], 1)

                    def differ(i, t):
                        n = P * (i + 1)
                        dve.wait_ge(sems["p_ready"], t + 1 + CREDITS["p_ready"])
                        dve.wait_ge(sems["att_ready"], t + CREDITS["att_ready"])
                        dve.reciprocal(rsum, sums[i % 2]).then_inc(sems["coef_ready"], 1)
                        dve.wait_ge(sems["coef_ready"], 2 * t + 1)
                        dve.tensor_tensor(rsum, rsum, map_gain, ALU.mult)\
                           .then_inc(sems["coef_ready"], 1)
                        dve.wait_ge(sems["coef_ready"], 2 * t + 2)
                        dve.wait_ge(sems["tp_done"], t + CREDITS["tp_done"])
                        dve.tensor_scalar(att[:, 0:n], pp[i % 2][:, 0, 0:n], rsum[:, 0:1], None, ALU.mult)\
                           .then_inc(sems["att_part"], 1)
                        dve.wait_ge(sems["att_part"], t + 1)
                        dve.scalar_tensor_tensor(att[:, 0:n], pp[i % 2][:, 1, 0:n], rsum[:, 1:2], att[:, 0:n],
                                                 ALU.mult, ALU.add).then_inc(sems["att_ready"], 1)

                    def head_out(h):
                        dve.wait_ge(sems["pv_done"], 4 * h + 4 + CREDITS["pv_done"])
                        dve.tensor_copy(oT[:, h, 0:SEQ], ps[:, 7, :]).then_inc(sems["o_evac"], 1)

                    def sample_mask(b):
                        dve.wait_ge(sems["ss_full"], b + 1 + CREDITS["ss_full"])
                        dve.wait_ge(sems["sp_ready"], b + CREDITS["sp_ready"])
                        dve.tensor_tensor(new_sc, ps[:, 6, 0:S_TOK], c("smask")[:, bass.ds(S_TOK * b, S_TOK)], ALU.add)\
                           .then_inc(sems["smasked"], 1)

                    def sample_max(b):
                        dve.wait_ge(sems["smasked"], b + 1)
                        dve.tensor_reduce(mxs2[:, 0:1], page_sc, AXX, ALU.max).then_inc(sems["smax"], 1)
                        dve.tensor_reduce(mxs2[:, 1:2], new_sc, AXX, ALU.max).then_inc(sems["smax"], 1)
                        dve.wait_ge(sems["smax"], 3 * b + 2)
                        dve.tensor_tensor(mxs, mxs2[:, 0:1], mxs2[:, 1:2], ALU.max).then_inc(sems["smax"], 1)
                        dve.wait_ge(sems["smax"], 3 * b + 3)
                        dve.tensor_scalar(nmxs, mxs, -1.0, None, ALU.mult).then_inc(sems["snmx"], 1)

                    def sample_coef(b):
                        dve.wait_ge(sems["sp_ready"], b + 1 + CREDITS["sp_ready"])
                        dve.tensor_tensor(sumss, sumss2[:, 0:1], sumss2[:, 1:2], ALU.add).then_inc(sems["srs"], 1)
                        dve.wait_ge(sems["srs"], 3 * b + 1)
                        dve.reciprocal(rss, sumss).then_inc(sems["srs"], 1)
                        dve.wait_ge(sems["srs"], 3 * b + 2)
                        dve.tensor_tensor(coef, rss, row_sign, ALU.mult).then_inc(sems["srs"], 1)
                        dve.wait_ge(sems["srs"], 3 * b + 3)
                        dve.wait_ge(sems["at_done"], b + CREDITS["at_done"])
                        dve.tensor_scalar(cmat, c("comb"), coef, None, ALU.mult).then_inc(sems["c_ready"], 1)

                    def sample_out(b):
                        dve.wait_ge(sems["os_picked"], b + 1 + CREDITS["os_picked"])
                        dve.tensor_copy(oT[:, :, bass.ds(SEQ + DEC_SEQ * b, DEC_SEQ)],
                                        ps[:, 3, 0:S_TOK].rearrange("p (h s) -> p h s", h=N_HEADS))\
                           .then_inc(sems["os_evac"], 1)

                    def round_(n, more):
                        for i in range(4):
                            maximum(i, 4 * n + i)
                            if i == 1 and more:
                                sample_mask(n + 1)
                            differ(i, 4 * n + i)
                            if i == 1 and more:
                                sample_max(n + 1)
                        if more:
                            sample_coef(n + 1)
                        head_out(n)
                        sample_out(n)

                    for j in range(2):
                        dve.wait_ge(sems[f"k_out{j}"], 16 * 8 + CREDITS[f"k_out{j}"])
                    sample_mask(0)
                    sample_max(0)
                    sample_coef(0)
                    with dve.Fori(0, N_HEADS - 1) as n:
                        round_(n, True)
                    round_(N_HEADS - 1, False)
                    dve.wait_ge(sems["o_evac"], N_HEADS + CREDITS["o_evac"])
                    dve.wait_ge(sems["os_evac"], DEC_BATCH + CREDITS["os_evac"])
                    for h in range(N_HEADS):
                        if h >= 4:
                            dve.wait_ge(sems["so_sum"], h - 3)
                        dve.tensor_tensor(sq[h % 4][:, :], oT[:, h, :], oT[:, h, :], ALU.mult)\
                           .then_inc(sems["so_sq"], 1)
                    for h in range(N_HEADS):
                        dve.wait_ge(sems["so_rs"], h + 1)
                        dve.wait_ge(sems["h_lo"], h0 + h - 1 + CREDITS["h_lo"])
                        dve.scalar_tensor_tensor(hf[h % 2][:, :], oT[:, h, :], gain_o, rs[h][:, :], ALU.mult,
                                                 ALU.mult).then_inc(sems["so_n"], 1)

        @block.gpsimd
        def _(pool):
            credit(pool, "norm_lo", "h_lo")

            def lo_part(tile, k, hi, lo, hi_sem, n, lo_sem):
                pool.wait_ge(sems[hi_sem], count(hi_sem, n + 1))
                pool.tensor_tensor(lo[:, k, :], tile[:, :], hi[:, k, :].bitcast(F32), ALU.subtract)\
                    .then_inc(sems[lo_sem], 1)

            for s in plan:
                n0, h0 = 8 * s["norm"], s["h"]
                if s["kind"] == "norm":
                    with pool.Fori(0, 2) as i:
                        for j in range(4):
                            lo_part(mt[j], 4 * i + j, hh_hi, hh_lo, "norm_hi", n0 + 4 * i + j, "norm_lo")
                if s["kind"] in ("up", "rglru"):
                    with pool.Fori(0, s["units"] // 2) as i:
                        for j in range(2):
                            lo_part(hf[j], 2 * i + j, h_hi, h_lo, "h_hi", h0 + 2 * i + j, "h_lo")
                if s["kind"] == "attention":
                    pool.wait_ge(sems["qs_in"], 16)
                    pool.memset(qbd[:, :], 0.0).then_inc(sems["qbd_zero"], 1)
                    pool.wait_ge(sems["qbd_zero"], 1)
                    with pool.Fori(0, DEC_BATCH) as b:
                        pool.wait_ge(sems["ss_full"], b + CREDITS["ss_full"])
                        for m in range(2):
                            base = qbd[64 * m:64 * m + 64, 8 * m:8 * m + 8]
                            out = bass.AP(base.tensor, base.offset, [list(base.ap[0]), [144, N_HEADS], [1, DEC_SEQ]])
                            pool.tensor_copy(out, qs[64 * m:64 * m + 64, :, bass.ds(DEC_SEQ * b, DEC_SEQ)])\
                                .then_inc(sems["qbd_ready"], 1)
                    with pool.Fori(0, 4) as i:
                        for j in range(2):
                            lo_part(hf[j], 2 * i + j, h_hi, h_lo, "h_hi", h0 + 2 * i + j, "h_lo")


def constants():
    out = {"ident": np.eye(P), "ones": np.ones((P, P)),
           "causal": np.where(np.arange(P)[None] <= np.arange(P)[:, None], 0, NEG)}
    half = HEAD_DIM // 2
    inv = (1.0 / (np.float32(ROPE_THETA) ** (np.arange(half, dtype=np.float32) * np.float32(2.0 / HEAD_DIM))))
    pos = np.concatenate([np.arange(SEQ), np.tile(PAST_LEN + np.arange(DEC_SEQ), DEC_BATCH)]).astype(np.float32)
    ang = (inv.astype(np.float32)[:, None] * pos[None]).astype(np.float32)
    out["cos"] = np.tile(np.cos(ang), (4, 1))
    out["sin"] = np.tile(np.concatenate([-np.sin(ang), np.sin(ang)]), (2, 1))
    row = np.arange(P)
    h, m, q = row // 16, row // 8 % 2, row % 8
    key = np.arange(S_TOK)
    seen = (key[None, None] // 8 == np.arange(DEC_BATCH)[None, :, None]) & (key[None, None] % 8 <= q[:, None, None])
    out["smask"] = np.where(seen, 0, NEG).reshape(P, -1)
    out["comb"] = key[None] == (8 * h + q)[:, None]
    out["fold"] = (np.arange(NC_)[None] == row[:, None] % NC_) & (row < 2 * NC_)[:, None]
    out["map0"], out["map1"] = (m == 0)[:, None], (m == 1)[:, None]
    return {k: v.astype(np.float32) for k, v in out.items()}


def kernel(**inputs):
    import concourse.bacc as bacc
    from concourse.bass_utils import run_bass_kernel_spmd

    a = {k: np.asarray(v) for k, v in inputs.items()}

    def rows(v):
        v = v.reshape(-1, KT, P)
        return v.transpose(2, 0, 1).reshape(P, -1)

    def units(w):
        k, n = w.shape
        return np.ascontiguousarray(w.reshape(k // P, P, n // 256, 256).transpose(2, 1, 0, 3)).reshape(n // 256, P, -1)

    def paired(wa, wb):
        k, n = wa.shape
        both = np.stack([w.reshape(k // P, P, n // P, P) for w in (wa, wb)], axis=3)
        return np.ascontiguousarray(both.transpose(2, 1, 0, 3, 4)).reshape(n // P, P, -1)

    k = constants()
    cond = np.concatenate([a["c_prompt"], a["c_sample"]])
    k["cond"] = cond.reshape(NC_, KT, P).transpose(2, 1, 0).reshape(P, -1)
    k["ada_b"] = rows(np.concatenate([a["ada_b"][0], a["kv_ada_b"], a["ada_b"][1]]))
    k["norm_g"], k["kv_g"], k["final_g"] = rows(a["norm_g"]), rows(a["kv_norm_g"]), rows(a["final_g"])
    k["conv_w"] = a["a_conv_w"][0].reshape(CONV_W, KT, P).transpose(2, 1, 0).reshape(P, -1)
    k["conv_b"], k["b_rg"], k["b_ig"] = rows(a["a_conv_b"]), rows(a["a_b_rg"]), rows(a["a_b_ig"])
    k["lru_lambda"] = rows(a["a_lambda"])
    k["subln_g"] = a["b_subln_g"].reshape(P, 1)
    k["lam_p"] = np.broadcast_to(a["b_lambda"].reshape(1, -1), (P, 4 * HEAD_DIM))
    k["st_conv"] = a["state_conv"][0].reshape(DEC_BATCH, PADS, KT, P).transpose(3, 2, 0, 1).reshape(P, -1)
    k["st_h"] = a["state_h"][0].reshape(DEC_BATCH, KT, P).transpose(2, 1, 0).reshape(P, -1)
    consts = np.concatenate([k[name].reshape(P, n) for name, (_, n) in CONST.items()], axis=1)

    tokens = np.concatenate([a["x_prompt"].reshape(SEQ, -1), a["x_sample"].reshape(S_TOK, -1)])
    gu, wd = a["ffn_w_gu"].reshape(4, D_MODEL, 2 * D_FF), a["ffn_w_d"].reshape(4, D_FF, D_MODEL)
    feeds = {
        "consts": consts,
        "xT": tokens.reshape(T, KT, P).transpose(2, 1, 0),
        "page_table": a["page_table"].reshape(1, -1),
        "ada_w": np.concatenate([units(a["ada_w"][0]), units(a["kv_ada_w"]), units(a["ada_w"][1])]),
        "w_gu": np.stack([paired(w[:, :D_FF], w[:, D_FF:]) for w in gu]),
        "w_d8": np.stack([np.stack([units(w[1024 * n:1024 * n + 1024]) for n in range(2)]) for w in wd]),
        "w_d6": np.stack([units(w[2048:]) for w in wd]),
        "w_in": paired(a["a_w_in"][0][:, :D_MODEL], a["a_w_in"][0][:, D_MODEL:]),
        "w_gate": np.concatenate([a["a_w_rg"][0], a["a_w_ig"][0]], axis=2),
        "w_out": units(a["a_w_out"][0]),
        "w_kv": paired(a["w_kv"][:, :D_MODEL], a["w_kv"][:, D_MODEL:]),
        "w_q": units(a["b_w_q"][0]),
        "w_o": units(a["b_w_o"][0]),
        "k_cache": a["cache_k"].transpose(0, 3, 4, 2, 1).reshape(-1, P, N_HEADS * PAGE),
        "v_cache": a["cache_v"].reshape(-1, PAGE, N_HEADS * P),
    }
    outs = {"yT": (KT, P, T), "conv_out": (P, KT, NC_, PADS), "h_out": (P, KT, NC_), "kT_out": (N_HEADS, P, T),
            "v_prompt": (N_HEADS, P, 4, P), "v_sample": (N_HEADS, S_TOK, P)}

    nc = bacc.Bacc("TRN2", target_bir_lowering=False, num_devices=1)
    arrays, args = {}, []
    for name, v in feeds.items():
        v = np.ascontiguousarray(v)
        arrays["in_" + name] = v
        args.append(nc.dram_tensor("in_" + name, v.shape, mybir.dt.from_np(v.dtype), kind="ExternalInput").ap())
    for name, shape in outs.items():
        args.append(nc.dram_tensor("out_" + name, shape, F32, kind="ExternalOutput").ap())
    trunk(nc, *args)
    r = run_bass_kernel_spmd(nc, [arrays], core_ids=[0]).results[0]
    o = {name: r["out_" + name] for name in outs}

    y = o["yT"].reshape(D_MODEL, T).transpose(1, 0)
    conv = o["conv_out"].transpose(2, 3, 1, 0).reshape(NC_, PADS, D_MODEL)
    h = o["h_out"].transpose(2, 1, 0).reshape(NC_, D_MODEL)
    kk = o["kT_out"].transpose(2, 0, 1).reshape(T, N_HEADS, 2, HEAD_DIM)
    vp = o["v_prompt"].transpose(2, 1, 0, 3)
    vs = o["v_sample"].transpose(1, 0, 2)
    got = (y[:SEQ].reshape(1, SEQ, D_MODEL), y[SEQ:].reshape(DEC_BATCH, DEC_SEQ, D_MODEL),
           conv[:1].reshape(1, 1, PADS, D_MODEL), h[:1].reshape(1, 1, D_MODEL),
           kk[:SEQ].reshape(1, SEQ, N_HEADS, 2, HEAD_DIM), vp.reshape(1, SEQ, N_HEADS, P),
           conv[1:].reshape(1, DEC_BATCH, PADS, D_MODEL), h[1:].reshape(1, DEC_BATCH, D_MODEL),
           kk[SEQ:].reshape(DEC_BATCH, DEC_SEQ, N_HEADS, 2, HEAD_DIM), vs.reshape(DEC_BATCH, DEC_SEQ, N_HEADS, P))
    return tuple(np.ascontiguousarray(v) for v in got)
```
